# Optimizing a Trainium2 kernel written in Bass

```python
import math
import jax, jax.numpy as jnp
from jax import lax
import numpy as np

D_MODEL = 1024
BATCH = 1
SEQ = 256
DEPTH = 1

N_ATTN_HEADS = 8
SUB_HEAD_DIM = 64
V_HEAD_DIM = 2 * SUB_HEAD_DIM
ATTN_WIDTH = N_ATTN_HEADS * V_HEAD_DIM
ROPE_THETA = 10000.0
Q_BLOCK = 128
LAMBDA_BASE = 0.8
LAMBDA_AMP = 0.6
LAMBDA_RATE = 0.3

LRU_WIDTH = 1024
LRU_BLOCKS = 8
LRU_BLOCK_DIM = LRU_WIDTH // LRU_BLOCKS
CONV_WIDTH = 4
CONV_PAD_LEFT = (CONV_WIDTH - 1) // 2
CONV_PAD_RIGHT = CONV_WIDTH - 1 - CONV_PAD_LEFT
LRU_C = 8.0
N_DIRECTIONS = 2

N_GATED_BRANCHES = 2
PROJ_WIDTH = 3 * ATTN_WIDTH + 2 * LRU_WIDTH + N_GATED_BRANCHES * D_MODEL
SPLIT_POINTS = (ATTN_WIDTH, 2 * ATTN_WIDTH, 3 * ATTN_WIDTH,
                3 * ATTN_WIDTH + LRU_WIDTH, 3 * ATTN_WIDTH + 2 * LRU_WIDTH)

N_GROUPS = 4
EXPERTS_PER_GROUP = 4
N_EXPERTS = N_GROUPS * EXPERTS_PER_GROUP
TOP_K_IN_GROUP = 2
EXPERT_HIDDEN = 512
TOKEN_BLOCK = 128

RMS_EPS = 1e-6


def rms_norm(x, gain):
    xf = x.astype(jnp.float32)
    y = xf * lax.rsqrt(jnp.mean(xf * xf, axis=-1, keepdims=True) + RMS_EPS)
    return (y * gain.astype(jnp.float32)).astype(x.dtype)

def lambda_init_fn(layer_idx):
    return LAMBDA_BASE - LAMBDA_AMP * math.exp(-LAMBDA_RATE * layer_idx)

def rope_tables(seq, dim):
    pos = jnp.arange(seq, dtype=jnp.float32)
    inv_freq = ROPE_THETA ** (-jnp.arange(0, dim, 2, dtype=jnp.float32) / dim)
    ang = pos[:, None] * inv_freq[None, :]
    return jnp.cos(ang), jnp.sin(ang)

def apply_rope(x, cos, sin):
    xf = x.astype(jnp.float32)
    x1, x2 = jnp.split(xf, 2, axis=-1)
    c = cos[None, :, None, None, :]
    s = sin[None, :, None, None, :]
    return jnp.concatenate([x1 * c - x2 * s, x1 * s + x2 * c], axis=-1).astype(x.dtype)

def diff_attention(q, k, v, lam):
    B, S, H, _, dh = q.shape
    scale = dh ** -0.5
    n_blk = S // Q_BLOCK
    qb = q.reshape(B, n_blk, Q_BLOCK, H, 2, dh).transpose(1, 0, 2, 3, 4, 5)

    def one_block(q_blk):
        s = jnp.einsum('bqhcd,bkhcd->bhcqk', q_blk, k,
                       preferred_element_type=jnp.float32) * scale
        p = jax.nn.softmax(s, axis=-1)
        p_diff = p[:, :, 0] - lam * p[:, :, 1]
        return jnp.einsum('bhqk,bkhd->bqhd', p_diff.astype(v.dtype), v)

    out = lax.map(one_block, qb)
    return out.transpose(1, 0, 2, 3, 4).reshape(B, S, H, v.shape[-1])

def centred_depthwise_conv(x, w, b):
    y = lax.conv_general_dilated(
        x, w[:, None, :], window_strides=(1,),
        padding=[(CONV_PAD_LEFT, CONV_PAD_RIGHT)],
        dimension_numbers=('NWC', 'WIO', 'NWC'),
        feature_group_count=x.shape[-1])
    return y + b

def block_diag_linear(x, w, b):
    B, S, C = x.shape
    xb = x.reshape(B, S, LRU_BLOCKS, LRU_BLOCK_DIM)
    y = jnp.einsum('bsnd,nde->bsne', xb, w)
    return y.reshape(B, S, C) + b

def rg_lru(x, w_a, b_a, w_i, b_i, lam_param, reverse):
    r = jax.nn.sigmoid(block_diag_linear(x, w_a, b_a).astype(jnp.float32))
    i = jax.nn.sigmoid(block_diag_linear(x, w_i, b_i).astype(jnp.float32))
    log_a = -LRU_C * r * jax.nn.softplus(-lam_param.astype(jnp.float32))
    a = jnp.exp(log_a)
    mult = jnp.sqrt(-jnp.expm1(2.0 * log_a))
    u = mult * (i * x.astype(jnp.float32))

    def combine(c1, c2):
        a1, b1 = c1
        a2, b2 = c2
        return a1 * a2, a2 * b1 + b2

    _, h = lax.associative_scan(combine, (a, u), axis=1, reverse=reverse)
    return h.astype(x.dtype)

def hierarchical_moe(h, w_group, b_group, w_er, b_er, w_gate, w_up, w_down):
    B, S, D = h.shape
    N = B * S
    xt = h.reshape(N, D)
    g_logits = (xt @ w_group + b_group).astype(jnp.float32)
    g_prob = jax.nn.softmax(g_logits, axis=-1)
    g_sel = jnp.argmax(g_logits, axis=-1)
    g_w = jnp.take_along_axis(g_prob, g_sel[:, None], axis=-1)
    e_logits = (xt @ w_er + b_er).astype(jnp.float32).reshape(N, N_GROUPS, EXPERTS_PER_GROUP)
    e_sel_logits = jnp.take_along_axis(e_logits, g_sel[:, None, None], axis=1)[:, 0]
    top_val, top_idx = lax.top_k(e_sel_logits, TOP_K_IN_GROUP)
    top_w = jax.nn.softmax(top_val, axis=-1) * g_w
    expert_id = g_sel[:, None] * EXPERTS_PER_GROUP + top_idx
    combine_w = jnp.sum(jax.nn.one_hot(expert_id, N_EXPERTS, dtype=jnp.float32)
                        * top_w[..., None], axis=1)

    n_blk = S // TOKEN_BLOCK
    xb = h.reshape(B, n_blk, TOKEN_BLOCK, D).transpose(1, 0, 2, 3).reshape(n_blk, B * TOKEN_BLOCK, D)
    cb = combine_w.reshape(B, n_blk, TOKEN_BLOCK, N_EXPERTS).transpose(1, 0, 2, 3)
    cb = cb.reshape(n_blk, B * TOKEN_BLOCK, N_EXPERTS).astype(h.dtype)

    def expert_block(args):
        xs, cs = args
        a = jnp.einsum('nd,edf->nef', xs, w_gate)
        u = jnp.einsum('nd,edf->nef', xs, w_up)
        hid = jax.nn.silu(a) * u * cs[:, :, None]
        return jnp.einsum('nef,efd->nd', hid, w_down)

    y = lax.map(expert_block, (xb, cb))
    y = y.reshape(n_blk, B, TOKEN_BLOCK, D).transpose(1, 0, 2, 3)
    return y.reshape(B, S, D)

def first_inputs(seed: int = 0) -> dict:
    key = jax.random.key(seed)
    ks = jax.random.split(key, 32)
    f32 = jnp.float32
    nrm = lambda k, shape, scale: jax.random.normal(k, shape, f32) * scale
    gain = lambda k, shape: jnp.ones(shape, f32) + 0.02 * jax.random.normal(k, shape, f32)

    a_c = jax.random.uniform(ks[16], (DEPTH, N_DIRECTIONS, LRU_WIDTH), f32, 0.9, 0.999)
    a_base = a_c ** (1.0 / LRU_C)
    lru_lambda = jnp.log(a_base) - jnp.log1p(-a_base)

    return {
        "x": jax.random.normal(ks[0], (BATCH, SEQ, D_MODEL), f32),
        "norm1_gain": gain(ks[1], (DEPTH, D_MODEL)),
        "w_in": nrm(ks[2], (DEPTH, D_MODEL, PROJ_WIDTH), D_MODEL ** -0.5),
        "b_gates": nrm(ks[3], (DEPTH, N_GATED_BRANCHES * D_MODEL), 0.02),
        "q_norm_gain": gain(ks[4], (DEPTH, SUB_HEAD_DIM)),
        "k_norm_gain": gain(ks[5], (DEPTH, SUB_HEAD_DIM)),
        "lambda_q1": nrm(ks[6], (DEPTH, SUB_HEAD_DIM), 0.1),
        "lambda_k1": nrm(ks[7], (DEPTH, SUB_HEAD_DIM), 0.1),
        "lambda_q2": nrm(ks[8], (DEPTH, SUB_HEAD_DIM), 0.1),
        "lambda_k2": nrm(ks[9], (DEPTH, SUB_HEAD_DIM), 0.1),
        "attn_subln_gain": gain(ks[10], (DEPTH, V_HEAD_DIM)),
        "w_attn_o": nrm(ks[11], (DEPTH, ATTN_WIDTH, D_MODEL), ATTN_WIDTH ** -0.5),
        "conv_w": nrm(ks[12], (DEPTH, CONV_WIDTH, LRU_WIDTH), CONV_WIDTH ** -0.5),
        "conv_b": nrm(ks[13], (DEPTH, LRU_WIDTH), 0.02),
        "lru_wa": nrm(ks[14], (DEPTH, N_DIRECTIONS, LRU_BLOCKS, LRU_BLOCK_DIM, LRU_BLOCK_DIM), LRU_BLOCK_DIM ** -0.5),
        "lru_ba": nrm(ks[15], (DEPTH, N_DIRECTIONS, LRU_WIDTH), 0.02),
        "lru_wi": nrm(ks[17], (DEPTH, N_DIRECTIONS, LRU_BLOCKS, LRU_BLOCK_DIM, LRU_BLOCK_DIM), LRU_BLOCK_DIM ** -0.5),
        "lru_bi": nrm(ks[18], (DEPTH, N_DIRECTIONS, LRU_WIDTH), 0.02),
        "lru_lambda": lru_lambda,
        "w_lru_o": nrm(ks[19], (DEPTH, LRU_WIDTH, D_MODEL), LRU_WIDTH ** -0.5),
        "w_out": nrm(ks[20], (DEPTH, D_MODEL, D_MODEL), D_MODEL ** -0.5),
        "norm2_gain": gain(ks[21], (DEPTH, D_MODEL)),
        "w_group_router": nrm(ks[22], (DEPTH, D_MODEL, N_GROUPS), D_MODEL ** -0.5),
        "b_group_router": nrm(ks[23], (DEPTH, N_GROUPS), 0.01),
        "w_expert_router": nrm(ks[24], (DEPTH, D_MODEL, N_EXPERTS), D_MODEL ** -0.5),
        "b_expert_router": nrm(ks[25], (DEPTH, N_EXPERTS), 0.01),
        "w_expert_gate": nrm(ks[26], (DEPTH, N_EXPERTS, D_MODEL, EXPERT_HIDDEN), D_MODEL ** -0.5),
        "w_expert_up": nrm(ks[27], (DEPTH, N_EXPERTS, D_MODEL, EXPERT_HIDDEN), D_MODEL ** -0.5),
        "w_expert_down": nrm(ks[28], (DEPTH, N_EXPERTS, EXPERT_HIDDEN, D_MODEL), EXPERT_HIDDEN ** -0.5),
    }

def first_block(x, norm1_gain, w_in, b_gates, q_norm_gain, k_norm_gain,
              lambda_q1, lambda_k1, lambda_q2, lambda_k2, attn_subln_gain, w_attn_o,
              conv_w, conv_b, lru_wa, lru_ba, lru_wi, lru_bi, lru_lambda, w_lru_o,
              w_out, norm2_gain, w_group_router, b_group_router,
              w_expert_router, b_expert_router, w_expert_gate, w_expert_up, w_expert_down):
    B, S, D = x.shape
    cos, sin = rope_tables(S, SUB_HEAD_DIM)
    for l in range(DEPTH):
        lam_init = lambda_init_fn(l)
        h = rms_norm(x, norm1_gain[l])
        proj = jnp.einsum('bsd,dc->bsc', h, w_in[l])
        q, k, v, lru_x, lru_g, gate_pre = jnp.split(proj, SPLIT_POINTS, axis=-1)

        q = q.reshape(B, S, N_ATTN_HEADS, 2, SUB_HEAD_DIM)
        k = k.reshape(B, S, N_ATTN_HEADS, 2, SUB_HEAD_DIM)
        v = v.reshape(B, S, N_ATTN_HEADS, V_HEAD_DIM)
        q = apply_rope(rms_norm(q, q_norm_gain[l]), cos, sin)
        k = apply_rope(rms_norm(k, k_norm_gain[l]), cos, sin)
        lam = (jnp.exp(jnp.sum(lambda_q1[l].astype(jnp.float32) * lambda_k1[l].astype(jnp.float32)))
               - jnp.exp(jnp.sum(lambda_q2[l].astype(jnp.float32) * lambda_k2[l].astype(jnp.float32)))
               + lam_init)
        o = diff_attention(q, k, v, lam)
        o = rms_norm(o, attn_subln_gain[l]) * (1.0 - lam_init)
        attn_d = jnp.einsum('bsc,cd->bsd', o.reshape(B, S, ATTN_WIDTH), w_attn_o[l])

        xr = centred_depthwise_conv(lru_x, conv_w[l], conv_b[l])
        h_fwd = rg_lru(xr, lru_wa[l, 0], lru_ba[l, 0], lru_wi[l, 0], lru_bi[l, 0], lru_lambda[l, 0], False)
        h_bwd = rg_lru(xr, lru_wa[l, 1], lru_ba[l, 1], lru_wi[l, 1], lru_bi[l, 1], lru_lambda[l, 1], True)
        y_lru = (h_fwd + h_bwd) * jax.nn.gelu(lru_g)
        lru_d = jnp.einsum('bsc,cd->bsd', y_lru, w_lru_o[l])

        g_attn, g_lru = jnp.split(jax.nn.sigmoid(gate_pre + b_gates[l]), N_GATED_BRANCHES, axis=-1)
        merged = g_attn * attn_d + g_lru * lru_d
        x = x + jnp.einsum('bsd,de->bse', merged, w_out[l])

        h2 = rms_norm(x, norm2_gain[l])
        x = x + hierarchical_moe(h2, w_group_router[l], b_group_router[l],
                                 w_expert_router[l], b_expert_router[l],
                                 w_expert_gate[l], w_expert_up[l], w_expert_down[l])
    return x


DEPTH_2 = 2

HEAD_DIM = 64
N_HEADS = 4
BRANCH_WIDTH = N_HEADS * HEAD_DIM
N_BRANCHES = 4

DSW_PATTERNS = ((128, 1), (512, 4), (2048, 16))

MLA_Q_RANK = 192
MLA_KV_RANK = 128
MLA_NOPE_DIM = 64
MLA_ROPE_DIM = 32
MLA_V_DIM = 64

NSA_CMP_BLOCK = 32
NSA_CMP_STRIDE = 16
NSA_CMP_HIDDEN = 128
NSA_SEL_BLOCK = 64
NSA_TOP_N = 16
NSA_WINDOW = 512
NSA_KV_DIM = 64
NSA_FORCE_SCORE = 1e9

N_ALIBI_HEADS = 8

IN_SPLITS = (
    ("a_q", BRANCH_WIDTH), ("a_k", BRANCH_WIDTH), ("a_v", BRANCH_WIDTH), ("a_gate", BRANCH_WIDTH),
    ("b_cq", MLA_Q_RANK), ("b_ckv", MLA_KV_RANK), ("b_kpe", MLA_ROPE_DIM), ("b_gate", BRANCH_WIDTH),
    ("c_q", BRANCH_WIDTH), ("c_kc", NSA_KV_DIM), ("c_vc", NSA_KV_DIM), ("c_ks", NSA_KV_DIM),
    ("c_vs", NSA_KV_DIM), ("c_kw", NSA_KV_DIM), ("c_vw", NSA_KV_DIM), ("c_g", 3 * N_HEADS),
    ("c_gate", BRANCH_WIDTH),
    ("d_q", BRANCH_WIDTH), ("d_k", BRANCH_WIDTH), ("d_v", BRANCH_WIDTH), ("d_gate", BRANCH_WIDTH),
)
D_IN = sum(w for _, w in IN_SPLITS)


def rmsnorm(x, g):
    xf = x.astype(jnp.float32)
    y = xf * lax.rsqrt(jnp.mean(xf * xf, axis=-1, keepdims=True) + RMS_EPS)
    return (y * g.astype(jnp.float32)).astype(x.dtype)

def split_columns(p):
    out, off = {}, 0
    for name, w in IN_SPLITS:
        out[name] = p[..., off:off + w]
        off += w
    return out

def alibi_slopes():
    s = 2.0 ** (-8.0 * (np.arange(N_ALIBI_HEADS) + 1) / N_ALIBI_HEADS)
    s = jnp.asarray(s, jnp.float32)
    return s[0::2], s[1::2]

def masked_softmax(s, mask):
    s = jnp.where(mask, s, -jnp.inf)
    m = jnp.max(s, axis=-1, keepdims=True)
    m = jnp.where(jnp.isfinite(m), m, 0.0)
    e = jnp.exp(s - m)
    return e / jnp.maximum(jnp.sum(e, axis=-1, keepdims=True), 1e-30)

def sweep_query_blocks(block_fn, seq):
    out = lax.map(block_fn, jnp.arange(seq // Q_BLOCK))
    nq, b, tq, h, d = out.shape
    return jnp.swapaxes(out, 0, 1).reshape(b, nq * tq, h, d)

def rope(x, pos):
    half = x.shape[-1] // 2
    inv = ROPE_THETA ** (-jnp.arange(half, dtype=jnp.float32) / half)
    ang = pos.astype(jnp.float32)[:, None] * inv[None, :]
    cos, sin = jnp.cos(ang)[:, None, :], jnp.sin(ang)[:, None, :]
    xf = x.astype(jnp.float32)
    x1, x2 = xf[..., :half], xf[..., half:]
    return jnp.concatenate([x1 * cos - x2 * sin, x1 * sin + x2 * cos], axis=-1).astype(x.dtype)

def dilated_window_attention(q, k, v, slopes):
    B, S, H, Dh = q.shape
    scale = Dh ** -0.5

    def block(qb):
        t0 = qb * Q_BLOCK
        t = t0 + jnp.arange(Q_BLOCK)
        qblk = lax.dynamic_slice_in_dim(q, t0, Q_BLOCK, axis=1)
        outs, lses = [], []
        for window, dil in DSW_PATTERNS:
            dist = dil * jnp.arange(window // dil + 1)
            idx = t[:, None] - dist[None, :]
            valid = idx >= 0
            idxc = jnp.maximum(idx, 0)
            kg, vg = k[:, idxc], v[:, idxc]
            s = jnp.einsum('bqhd,bqjhd->bhqj', qblk, kg).astype(jnp.float32) * scale
            s = s - slopes[:, None, None] * dist.astype(jnp.float32)
            s = jnp.where(valid[None, None], s, -jnp.inf)
            lse = jax.nn.logsumexp(s, axis=-1)
            p = jnp.exp(s - lse[..., None])
            outs.append(jnp.einsum('bhqj,bqjhd->bqhd', p.astype(v.dtype), vg))
            lses.append(lse)
        w = jax.nn.softmax(jnp.stack(lses, axis=0), axis=0)
        o = 0.0
        for i in range(len(DSW_PATTERNS)):
            o = o + jnp.transpose(w[i], (0, 2, 1))[..., None].astype(v.dtype) * outs[i]
        return o

    return sweep_query_blocks(block, S)

def blocked_causal_softmax(q, k, v, scale):
    B, S, H, _ = q.shape
    kpos = jnp.arange(S)

    def block(qb):
        t0 = qb * Q_BLOCK
        t = t0 + jnp.arange(Q_BLOCK)
        qblk = lax.dynamic_slice_in_dim(q, t0, Q_BLOCK, axis=1)
        s = jnp.einsum('bqhd,bkhd->bhqk', qblk, k).astype(jnp.float32) * scale
        s = jnp.where(kpos[None, :] <= t[:, None], s, -jnp.inf)
        p = jax.nn.softmax(s, axis=-1)
        return jnp.einsum('bhqk,bkhd->bqhd', p.astype(v.dtype), v)

    return sweep_query_blocks(block, S)

def mla_attention(cq, ckv, kpe, q_norm_g, w_uq, kv_norm_g, w_ukv):
    B, S, _ = cq.shape
    pos = jnp.arange(S)
    q = (rmsnorm(cq, q_norm_g) @ w_uq).reshape(B, S, N_HEADS, MLA_NOPE_DIM + MLA_ROPE_DIM)
    q = jnp.concatenate([q[..., :MLA_NOPE_DIM], rope(q[..., MLA_NOPE_DIM:], pos)], axis=-1)
    kv = (rmsnorm(ckv, kv_norm_g) @ w_ukv).reshape(B, S, N_HEADS, MLA_NOPE_DIM + MLA_V_DIM)
    k_nope, v = kv[..., :MLA_NOPE_DIM], kv[..., MLA_NOPE_DIM:]
    k_pe = rope(kpe[:, :, None, :], pos)
    k = jnp.concatenate([k_nope, jnp.broadcast_to(k_pe, (B, S, N_HEADS, MLA_ROPE_DIM))], axis=-1)
    return blocked_causal_softmax(q, k, v, (MLA_NOPE_DIM + MLA_ROPE_DIM) ** -0.5)

def compress_blocks(tok, pos_emb, w1, b1, w2, b2):
    B, S, Dk = tok.shape
    n_cmp = (S - NSA_CMP_BLOCK) // NSA_CMP_STRIDE + 1
    idx = np.arange(n_cmp)[:, None] * NSA_CMP_STRIDE + np.arange(NSA_CMP_BLOCK)[None, :]
    blocks = tok[:, idx] + pos_emb
    hid = jax.nn.gelu(blocks.reshape(B, n_cmp, NSA_CMP_BLOCK * Dk) @ w1 + b1)
    return hid @ w2 + b2

def nsa_attention(q, kc, vc, ks, vs, kw, vw, gates, pos_emb, w1, b1, w2, b2, slopes):
    B, S, H, Dh = q.shape
    scale = Dh ** -0.5
    k_cmp = compress_blocks(kc, pos_emb[0], w1[0], b1[0], w2[0], b2[0])
    v_cmp = compress_blocks(vc, pos_emb[1], w1[1], b1[1], w2[1], b2[1])
    n_cmp = k_cmp.shape[1]
    cmp_end = jnp.arange(n_cmp) * NSA_CMP_STRIDE + NSA_CMP_BLOCK - 1
    n_sel = S // NSA_SEL_BLOCK
    top_n = min(NSA_TOP_N, n_sel)
    r_sel, r_cmp = NSA_SEL_BLOCK // NSA_CMP_STRIDE, NSA_CMP_BLOCK // NSA_CMP_STRIDE
    src = (jnp.arange(n_sel)[:, None, None] * r_sel - jnp.arange(r_sel)[None, :, None]
           - jnp.arange(r_cmp)[None, None, :]).reshape(n_sel, -1)
    sel_map = jnp.sum(src[..., None] == jnp.arange(n_cmp), axis=1).astype(jnp.float32)
    kw_pad = jnp.pad(kw, ((0, 0), (NSA_WINDOW, 0), (0, 0)))
    vw_pad = jnp.pad(vw, ((0, 0), (NSA_WINDOW, 0), (0, 0)))
    blk = jnp.arange(n_sel)
    sel_off = jnp.arange(NSA_SEL_BLOCK)

    def block(qb):
        t0 = qb * Q_BLOCK
        t = t0 + jnp.arange(Q_BLOCK)
        qblk = lax.dynamic_slice_in_dim(q, t0, Q_BLOCK, axis=1)
        gblk = lax.dynamic_slice_in_dim(gates, t0, Q_BLOCK, axis=1)
        dist_c = (t[:, None] - cmp_end[None, :]).astype(jnp.float32)
        s = jnp.einsum('bqhd,bnd->bhqn', qblk, k_cmp).astype(jnp.float32) * scale
        p_cmp = masked_softmax(s - slopes[:, None, None] * dist_c, dist_c >= 0)
        o_cmp = jnp.einsum('bhqn,bnd->bqhd', p_cmp.astype(v_cmp.dtype), v_cmp)
        p_sel = jnp.einsum('bhqn,jn->bqj', p_cmp, sel_map)
        cur = t // NSA_SEL_BLOCK
        valid = blk[None, :] * NSA_SEL_BLOCK <= t[:, None]
        forced = (blk[None, :] == 0) | (blk[None, :] == cur[:, None]) | (blk[None, :] == cur[:, None] - 1)
        score = jnp.where(valid, jnp.where(forced, NSA_FORCE_SCORE, p_sel), -jnp.inf)
        _, sel = lax.top_k(score, top_n)
        tok = (sel[..., None] * NSA_SEL_BLOCK + sel_off).reshape(B, Q_BLOCK, top_n * NSA_SEL_BLOCK)
        ks_g = jax.vmap(lambda a, i: a[i])(ks, tok)
        vs_g = jax.vmap(lambda a, i: a[i])(vs, tok)
        dist_s = (t[None, :, None] - tok).astype(jnp.float32)
        s = jnp.einsum('bqhd,bqkd->bhqk', qblk, ks_g).astype(jnp.float32) * scale
        s = s - slopes[None, :, None, None] * dist_s[:, None]
        p = masked_softmax(s, (dist_s >= 0)[:, None])
        o_slc = jnp.einsum('bhqk,bqkd->bqhd', p.astype(vs_g.dtype), vs_g)
        kwin = lax.dynamic_slice_in_dim(kw_pad, t0, Q_BLOCK + NSA_WINDOW, axis=1)
        vwin = lax.dynamic_slice_in_dim(vw_pad, t0, Q_BLOCK + NSA_WINDOW, axis=1)
        spos = t0 - NSA_WINDOW + jnp.arange(Q_BLOCK + NSA_WINDOW)
        dist_w = t[:, None] - spos[None, :]
        mask_w = (dist_w >= 0) & (dist_w < NSA_WINDOW) & (spos[None, :] >= 0)
        s = jnp.einsum('bqhd,bkd->bhqk', qblk, kwin).astype(jnp.float32) * scale
        p = masked_softmax(s - slopes[:, None, None] * dist_w.astype(jnp.float32), mask_w)
        o_win = jnp.einsum('bhqk,bkd->bqhd', p.astype(vwin.dtype), vwin)
        return gblk[..., 0:1] * o_cmp + gblk[..., 1:2] * o_slc + gblk[..., 2:3] * o_win

    return sweep_query_blocks(block, S)

def stick_breaking_attention(q, k, v):
    B, S, H, Dh = q.shape
    scale = Dh ** -0.5
    kpos = jnp.arange(S)

    def block(qb):
        t0 = qb * Q_BLOCK
        t = t0 + jnp.arange(Q_BLOCK)
        qblk = lax.dynamic_slice_in_dim(q, t0, Q_BLOCK, axis=1)
        z = jnp.einsum('bqhd,bkhd->bhqk', qblk, k).astype(jnp.float32) * scale
        mask = kpos[None, :] < t[:, None]
        log1m = jnp.where(mask, jax.nn.log_sigmoid(-z), 0.0)
        after = lax.cumsum(log1m, axis=3, reverse=True) - log1m
        a = jnp.where(mask, jnp.exp(jax.nn.log_sigmoid(z) + after), 0.0)
        return jnp.einsum('bhqk,bkhd->bqhd', a.astype(v.dtype), v)

    return sweep_query_blocks(block, S)

def second_inputs(seed: int = 0) -> dict:
    key = jax.random.key(seed)
    ks = jax.random.split(key, 18)
    f32 = jnp.float32

    def nrm(k, shape, fan_in):
        return jax.random.normal(k, shape, f32) * (fan_in ** -0.5)

    def gain(k, shape):
        return 1.0 + 0.05 * jax.random.normal(k, shape, f32)

    return {
        "x": jax.random.normal(ks[0], (BATCH, SEQ, D_MODEL), f32),
        "norm_g": gain(ks[1], (DEPTH_2, D_MODEL)),
        "w_in": nrm(ks[2], (DEPTH_2, D_MODEL, D_IN), D_MODEL),
        "mla_q_norm": gain(ks[3], (DEPTH_2, MLA_Q_RANK)),
        "mla_w_uq": nrm(ks[4], (DEPTH_2, MLA_Q_RANK, N_HEADS * (MLA_NOPE_DIM + MLA_ROPE_DIM)), MLA_Q_RANK),
        "mla_kv_norm": gain(ks[5], (DEPTH_2, MLA_KV_RANK)),
        "mla_w_ukv": nrm(ks[6], (DEPTH_2, MLA_KV_RANK, N_HEADS * (MLA_NOPE_DIM + MLA_V_DIM)), MLA_KV_RANK),
        "nsa_pos": 0.1 * jax.random.normal(ks[7], (DEPTH_2, 2, NSA_CMP_BLOCK, NSA_KV_DIM), f32),
        "nsa_w1": nrm(ks[8], (DEPTH_2, 2, NSA_CMP_BLOCK * NSA_KV_DIM, NSA_CMP_HIDDEN), NSA_CMP_BLOCK * NSA_KV_DIM),
        "nsa_b1": 0.02 * jax.random.normal(ks[9], (DEPTH_2, 2, NSA_CMP_HIDDEN), f32),
        "nsa_w2": nrm(ks[10], (DEPTH_2, 2, NSA_CMP_HIDDEN, NSA_KV_DIM), NSA_CMP_HIDDEN),
        "nsa_b2": 0.02 * jax.random.normal(ks[11], (DEPTH_2, 2, NSA_KV_DIM), f32),
        "w_branch": nrm(ks[12], (DEPTH_2, N_BRANCHES, BRANCH_WIDTH, D_MODEL), BRANCH_WIDTH),
        "w_merge": nrm(ks[13], (DEPTH_2, N_BRANCHES, D_MODEL, D_MODEL), D_MODEL),
        "b_merge": 0.02 * jax.random.normal(ks[14], (DEPTH_2, N_BRANCHES, D_MODEL), f32),
        "w_out": nrm(ks[15], (DEPTH_2, D_MODEL, D_MODEL), D_MODEL),
        "final_norm_g": gain(ks[16], (D_MODEL,)),
    }

def second_block(x, norm_g, w_in, mla_q_norm, mla_w_uq, mla_kv_norm, mla_w_ukv, nsa_pos, nsa_w1,
              nsa_b1, nsa_w2, nsa_b2, w_branch, w_merge, b_merge, w_out, final_norm_g):
    B, S, D = x.shape
    slopes_a, slopes_c = alibi_slopes()
    for l in range(DEPTH_2):
        h = rmsnorm(x, norm_g[l])
        c = split_columns(h @ w_in[l])
        heads = lambda a: a.reshape(B, S, N_HEADS, HEAD_DIM)
        flat = lambda a: a.reshape(B, S, BRANCH_WIDTH)
        y_a = flat(dilated_window_attention(heads(c["a_q"]), heads(c["a_k"]), heads(c["a_v"]), slopes_a))
        y_a = y_a * jax.nn.silu(c["a_gate"])
        y_b = flat(mla_attention(c["b_cq"], c["b_ckv"], c["b_kpe"], mla_q_norm[l], mla_w_uq[l],
                                 mla_kv_norm[l], mla_w_ukv[l]))
        y_b = y_b * jax.nn.silu(c["b_gate"])
        g_c = jax.nn.sigmoid(c["c_g"]).reshape(B, S, N_HEADS, 3)
        y_c = flat(nsa_attention(heads(c["c_q"]), c["c_kc"], c["c_vc"], c["c_ks"], c["c_vs"],
                                 c["c_kw"], c["c_vw"], g_c, nsa_pos[l], nsa_w1[l], nsa_b1[l],
                                 nsa_w2[l], nsa_b2[l], slopes_c))
        y_c = y_c * jax.nn.silu(c["c_gate"])
        y_d = flat(stick_breaking_attention(heads(c["d_q"]), heads(c["d_k"]), heads(c["d_v"])))
        y_d = y_d * jax.nn.silu(c["d_gate"])
        merged = 0.0
        for i, y in enumerate((y_a, y_b, y_c, y_d)):
            gate = jax.nn.sigmoid(h @ w_merge[l, i] + b_merge[l, i])
            merged = merged + gate * (y @ w_branch[l, i])
        x = x + merged @ w_out[l]
    return rmsnorm(x, final_norm_g)


def setup_inputs(seed=0):
    out = dict(first_inputs(seed))
    for name, value in second_inputs(seed + 1).items():
        if name != "x":
            out[name + "_2"] = value
    return out


def reference(
    x, norm1_gain, w_in, b_gates, q_norm_gain, k_norm_gain, lambda_q1, lambda_k1, lambda_q2,
    lambda_k2, attn_subln_gain, w_attn_o, conv_w, conv_b, lru_wa, lru_ba, lru_wi, lru_bi,
    lru_lambda, w_lru_o, w_out, norm2_gain, w_group_router, b_group_router, w_expert_router,
    b_expert_router, w_expert_gate, w_expert_up, w_expert_down, norm_g_2, w_in_2, mla_q_norm_2,
    mla_w_uq_2, mla_kv_norm_2, mla_w_ukv_2, nsa_pos_2, nsa_w1_2, nsa_b1_2, nsa_w2_2, nsa_b2_2,
    w_branch_2, w_merge_2, b_merge_2, w_out_2, final_norm_g_2,
):
    x = first_block(
        x, norm1_gain, w_in, b_gates, q_norm_gain, k_norm_gain, lambda_q1, lambda_k1, lambda_q2,
        lambda_k2, attn_subln_gain, w_attn_o, conv_w, conv_b, lru_wa, lru_ba, lru_wi, lru_bi,
        lru_lambda, w_lru_o, w_out, norm2_gain, w_group_router, b_group_router, w_expert_router,
        b_expert_router, w_expert_gate, w_expert_up, w_expert_down,
    )
    return second_block(
        x, norm_g_2, w_in_2, mla_q_norm_2, mla_w_uq_2, mla_kv_norm_2, mla_w_ukv_2, nsa_pos_2,
        nsa_w1_2, nsa_b1_2, nsa_w2_2, nsa_b2_2, w_branch_2, w_merge_2, b_merge_2, w_out_2,
        final_norm_g_2,
    )


_drawn_inputs = setup_inputs


def setup_inputs(seed=0):
    import zlib

    import numpy as np

    out = dict(_drawn_inputs(seed))
    spreads = {}
    factors = {'q_norm_gain': 4.316,
     'k_norm_gain': 2.798,
     'lambda_k2': 5.161,
     'lru_ba': 8.0,
     'lru_bi': 5.261,
     'b_group_router': 4.428,
     'b_expert_router': 3.267,
     'mla_q_norm_2': 8.0,
     'mla_kv_norm_2': 8.0,
     'nsa_pos_2': 4.771,
     'nsa_b1_2': 8.0,
     'nsa_b2_2': 8.0,
     'b_merge_2': 8.0}
    for name, (base, spread) in spreads.items():
        noise = np.random.default_rng([zlib.crc32(name.encode()), seed]).standard_normal(out[name].shape)
        drawn = base * np.exp(spread * noise) if base else spread * noise
        out[name] = __import__('jax').numpy.asarray(drawn.astype(out[name].dtype))
    for name, factor in factors.items():
        out[name] = (out[name] * factor).astype(out[name].dtype)
    return out
```

```python
import math
from contextlib import ExitStack

import numpy as np

import concourse.bass as bass
from concourse import mybir

P = 128
SEQ = 256
NT = SEQ // P
D = 1024
NC = D // P
PROJ = 7168
HEADS = 8
SUB = 64
VD = 2 * SUB
CONV = 4
EXPERTS = 16
GROUPS = 4
PER_GROUP = EXPERTS // GROUPS
HIDDEN = 512
LAYERS = 2
PROJ2 = 3564
H2 = 4
HD = 64
BW = H2 * HD
MQ, MKV, MN, MR = 192, 128, 64, 32
MQK = MN + MR
CMP_BLOCK, CMP_STRIDE, CMP_HID = 32, 16, 128
N_CMP = (SEQ - CMP_BLOCK) // CMP_STRIDE + 1
NCP = 16
EPS = 1e-6
LAM_INIT = 0.8 - 0.6 * math.exp(-0.3 * 0)
NEG = -1e30
SLOT = 2048
AQ, AK, AV, AG = 0, 256, 512, 768
BCQ, BCKV, BKPE, BG = 1024, 1216, 1344, 1376
CQ, CKC, CKS, CVS, CKW, CVW, CGT, CG = 1632, 1888, 2016, 2080, 2144, 2208, 2272, 2284
DQ, DK, DV, DG = 2540, 2796, 3052, 3308


def param_table():
    widths = [("ident", P), ("g1", NC), ("g2", NC), ("qg", SUB), ("kg", SUB), ("lam", 4 * SUB), ("subln", 1),
              ("conv_w", CONV * NC), ("conv_b", NC), ("ba", 2 * NC), ("bi", 2 * NC), ("lru_lam", 2 * NC),
              ("bg", 2 * NC), ("router_b", 20), ("router_w", NC * 20), ("cos", NT * 32), ("sin", NT * 32),
              ("mcos", NT * 16), ("msin", NT * 16), ("first", GROUPS)]
    return offsets(widths)


def layer_param_table():
    return offsets([("ng", NC), ("mqg", 2), ("mkvg", 1), ("pos", CMP_BLOCK), ("b1", 2), ("w2", 2 * HD), ("b2k", 1),
                    ("b2v", HD), ("bm", 4 * NC)])


def offsets(widths):
    at, table = 0, {}
    for name, n in widths:
        table[name] = (at, n)
        at += n
    return table, at


PARAMS, N_PARAMS = param_table()
LAYER_PARAMS, N_LAYER_PARAMS = layer_param_table()
OWN_DVE, OWN_ACT = 105, 7
MASKS = ["dist", "causal", "count", "strict", "strict_neg"]
SLOPES = [2.0 ** (-8.0 * (i + 1) / 8) for i in range(8)]
SLOPES_A, SLOPES_C = SLOPES[0::2], SLOPES[1::2]


class Own:

    def __init__(self, eng, sem, base=0):
        self.eng, self.sem, self.base, self.n = eng, sem, base, 0

    def done(self, instruction):
        instruction.then_inc(self.sem, 1)
        self.n += 1
        return instruction

    def wait(self):
        if self.n:
            self.eng.wait_ge(self.sem, self.n + self.base)


def two_blocks(nc, w, out, dbg=None):
    f32, f32r = mybir.dt.float32, mybir.dt.float32r
    ALU, ACT, AX = mybir.AluOpType, mybir.ActivationFunctionType, mybir.AxisListType
    ctx = ExitStack()
    with ctx:
        def sb(name, shape, dt=f32):
            return ctx.enter_context(nc.sbuf_tensor(name, shape, dt))

        def sem(name):
            return ctx.enter_context(nc.semaphore(name))

        RAW_SLOTS, SPLIT_SLOTS = 4, 2
        raw = sb("weights_raw", [P, RAW_SLOTS, SLOT])
        whi = sb("weights_high", [P, SPLIT_SLOTS, SLOT], f32r)
        wlo = sb("weights_low", [P, SPLIT_SLOTS, SLOT], f32r)
        act_hi = sb("act_high", [P, NC, SEQ], f32r)
        act_lo = sb("act_low", [P, NC, SEQ], f32r)
        mid_hi = sb("mid_high", [P, NC, SEQ], f32r)
        mid_lo = sb("mid_low", [P, NC, SEQ], f32r)
        x_tm = sb("x_tokens", [P, NT, D])
        arena = sb("arena", [P, 12 * SLOT])
        par = sb("params", [P, N_PARAMS])
        tiny = sb("tiny", [P, 256])
        layer_par = sb("layer_params", [P, N_LAYER_PARAMS])
        extra = sb("extra", [P, 240])
        psum = ctx.enter_context(nc.psum_tensor("psum", [P, 8 * 512], f32))

        def slot(n, k=1):
            return arena[:, n * SLOT:(n + k) * SLOT]

        def fm(n):
            return slot(n).rearrange("p (c t) -> p c t", c=NC)

        def tm(n):
            return slot(n).rearrange("p (t n) -> p t n", t=NT)

        def prm(name, a=0, b=None):
            at, n = PARAMS[name]
            return par[:, at + a:at + (n if b is None else b)]

        def lpar(name, a=0, b=None):
            at, n = LAYER_PARAMS[name]
            return layer_par[:, at + a:at + (n if b is None else b)]

        def bank(b, n=1):
            return psum[:, b * 512:(b + n) * 512]

        ident = prm("ident")
        tiny_at = [0]

        def small(n):
            a = tiny_at[0]
            tiny_at[0] += n
            assert tiny_at[0] <= 256
            return tiny[:, a:a + n]

        raw_ready = [sem(f"raw_ready{s}") for s in range(RAW_SLOTS)]
        hi_ready = sem("hi_ready")
        lo_ready = sem("lo_ready")
        tile_used = sem("tile_used")
        block_done = sem("block_done")
        block_free = [sem(f"block_free{p}") for p in range(2)]
        par_in = sem("params_in")
        x_in = sem("x_in")
        act_own, dve_own = sem("act_own"), sem("dve_own")
        norm_ss = sem("norm_sums")
        norm_ms = sem("norm_means")
        norm_rt = sem("norm_roots")
        norm_rs = sem("norm_scales")
        src_ready = sem("turn_source")
        turned = sem("turned")
        turned_hi = sem("turned_hi")
        turned_lo = sem("turned_lo")
        conv_ready = sem("conv_ready")
        lru_w_in = sem("lru_weights_in")
        lru_mm = sem("lru_products")
        lru_sig = sem("lru_sigmoids")
        lru_y = sem("lru_exponents")
        lru_ta = sem("lru_tanh_and_decay")
        lru_q = sem("lru_quotients")
        lru_mult = sem("lru_multipliers")
        lru_scan = sem("lru_scans")
        lru_sp = sem("lru_softplus")
        y_sum = sem("y_lru_sum")
        mid_hi_ready = sem("mid_high_ready")
        mid_lo_ready = sem("mid_low_ready")
        roped = sem("qk_roped")
        qk_turned = sem("qk_turned")
        qk_copied = sem("qk_copied")
        lam_e = sem("lambda_exps")
        lam_in = sem("lambda_sums")
        a_scores = sem("a_scores")
        a_shift = sem("a_shift")
        a_exp = sem("a_exp")
        a_diff = sem("a_diff")
        a_turned = sem("a_turned")
        a_pt = sem("a_pt")
        a_pv = sem("a_pv")
        a_out = sem("a_out")
        o_sq = sem("o_squares")
        o_ms = sem("o_means")
        o_rt = sem("o_roots")
        merged_ready = sem("merged_ready")
        merged_hi = sem("merged_high")
        merged_lo = sem("merged_low")
        router_split = sem("router_split")
        router_mm = sem("router_products")
        route_exp = sem("route_exchange")
        mask_in, layer_in, gain_in = sem("masks_in"), sem("layer_params_in"), sem("gain_in")
        l_act_own, l_dve_own = sem("layer_act_own"), sem("layer_dve_own")
        prep_pe = sem("prepared_pe")
        prep_act = sem("prepared_act")
        prep_dve = sem("prepared_dve")
        gates_ready = sem("branch_gates")
        l_scores = sem("l_scores")
        l_logs = sem("l_logs")
        l_shift = sem("l_shift")
        l_exp = sem("l_exp")
        l_turned = sem("l_turned")
        l_copied = sem("l_copied")
        l_pv = sem("l_pv")
        l_out = sem("l_out")
        out_ready, stored = sem("out_ready"), sem("stored")
        hid_hi = sem("hidden_high")
        hid_lo = sem("hidden_low")

        tiles, blocks = [], []

        def k_major(m, k0, c0, n=512):
            return m[k0:k0 + 512, c0:c0 + n].rearrange("(k p) n -> p k n", p=P)

        def matrix(m, order, n_last=512):
            for j in order:
                n = n_last if j == order[-1] else 512
                for h in range(2):
                    tiles.append((k_major(m, 512 * h, 512 * j, n), n))

        T_IN = 0
        w_in = w["w_in"][0]
        matrix(w_in, [6, 7, 8, 9, 0, 1, 2, 3, 4, 5, 10, 11, 12, 13])
        T_LRUO = len(tiles)
        matrix(w["w_lru_o"][0], [0, 1])
        T_ATTNO = len(tiles)
        matrix(w["w_attn_o"][0], [0, 1])
        T_OUT = len(tiles)
        matrix(w["w_out"][0], [0, 1])
        T_MOE = len(tiles)

        def gate_tiles(m, e):
            return [(k_major(m[e], 512 * h, 0), 512) for h in range(2)]

        def down_tiles(e):
            return [(k_major(w["w_expert_down"][0][e], 0, 512 * h), 512) for h in range(2)]

        wg, wu = w["w_expert_gate"][0], w["w_expert_up"][0]
        tiles += gate_tiles(wg, 0) + gate_tiles(wu, 0)
        for e in range(1, EXPERTS):
            tiles += gate_tiles(wg, e) + down_tiles(e - 1) + gate_tiles(wu, e)
        tiles += down_tiles(EXPERTS - 1)
        T_LAYERS = len(tiles)
        T_STOP = T_LAYERS
        tiles += [(None, 512)] * 12 + [(None, PROJ2 - 6 * 512)] * 2 + [(None, 512)] * 28

        def raw_tile(i, n=512):
            return raw[:, i % RAW_SLOTS, 0:4 * n]

        def hi_tile(i, n=512):
            return whi[:, i % SPLIT_SLOTS, 0:4 * n]

        def lo_tile(i, n=512):
            return wlo[:, i % SPLIT_SLOTS, 0:4 * n]

        def pair(g):
            return bank(2 * (g % 2), 2)

        block = ctx.enter_context(nc.Block())

        def load_tile(sp, i, r=0, source=None):
            if i >= RAW_SLOTS:
                sp.wait_ge(lo_ready, i - RAW_SLOTS + 1 + r)
            src, n = source or tiles[i]
            sp.dma_start(raw_tile(i, n).rearrange("p (k n) -> p k n", k=src.shape[1]), src)\
                .then_inc(raw_ready[i % RAW_SLOTS], 16)

        def high(act, i, r=0):
            n = tiles[i][1]
            act.wait_ge(raw_ready[i % RAW_SLOTS], 16 * (i // RAW_SLOTS + 1) + r * (16 // RAW_SLOTS))
            if i >= SPLIT_SLOTS:
                act.wait_ge(tile_used, i - SPLIT_SLOTS + 1 + r)
            nc.scalar.activation(hi_tile(i, n), raw_tile(i, n), ACT.Copy).then_inc(hi_ready, 1)

        def low(dve, i, r=0):
            n = tiles[i][1]
            dve.wait_ge(hi_ready, i + 1 + r)
            dve.tensor_tensor(lo_tile(i, n), raw_tile(i, n), hi_tile(i, n).bitcast(f32), ALU.subtract)\
                .then_inc(lo_ready, 1)

        def block_read(eng, g):
            eng.wait_ge(block_free[g % 2], g // 2 + 1)

        n_ss, n_ms, n_rt, n_rs = small(2), small(2), small(2), small(2)
        xn = tm(11)

        def norm_act(act, k, width=D):
            for t in range(NT):
                nc.scalar.activation(tm(5)[:, t, :], x_tm[:, t, :], ACT.Square, accum_out=n_ss[:, t:t + 1])\
                    .then_inc(norm_ss, 1)
            act.wait_ge(norm_ms, k + 1)
            nc.scalar.activation(n_rt, n_ms, ACT.Sqrt).then_inc(norm_rt, 1)
            act.wait_ge(norm_rs, k + 1)
            nc.scalar.activation(xn[:, 0, :], x_tm[:, 0, :], ACT.Copy, scale=n_rs[:, 0:1]).then_inc(src_ready, 1)

        def norm_dve(dve, k):
            dve.wait_ge(norm_ss, (k + 1) * 2)
            dve.tensor_scalar(n_ms, n_ss, 1.0 / D, EPS, ALU.mult, ALU.add).then_inc(norm_ms, 1)
            dve.wait_ge(norm_rt, k + 1)
            dve.reciprocal(n_rs, n_rt).then_inc(norm_rs, 1)
            dve.wait_ge(norm_rs, k + 1)
            dve.tensor_scalar(xn[:, 1, :], x_tm[:, 1, :], n_rs[:, 1:2], None, ALU.mult).then_inc(src_ready, 1)

        def turn_pe(pe, k, src):
            pe.wait_ge(src_ready, (k + 1) * 2)
            if not isinstance(k, int) or k:
                pe.wait_ge(turned_lo, k * 4)
            for b in range(4):
                for cc in range(2):
                    for t in range(NT):
                        c = 2 * b + cc
                        last = pe.transpose(bank(4 + b)[:, cc * SEQ + t * P:cc * SEQ + (t + 1) * P],
                                            src[:, t, c * P:(c + 1) * P], ident)
                last.then_inc(turned, 1)

        def turn_act(act, k, hi, gain):
            for b in range(4):
                act.wait_ge(turned, k * 4 + b + 1)
                for cc in range(2):
                    last = nc.scalar.activation(hi[:, 2 * b + cc, :], bank(4 + b)[:, cc * SEQ:(cc + 1) * SEQ],
                                                ACT.Copy, scale=gain(2 * b + cc))
                last.then_inc(turned_hi, 1)

        def turn_dve(dve, k, hi, lo, gain):
            for b in range(4):
                dve.wait_ge(turned_hi, k * 4 + b + 1)
                for cc in range(2):
                    c = 2 * b + cc
                    last = dve.scalar_tensor_tensor(lo[:, c, :], bank(4 + b)[:, cc * SEQ:(cc + 1) * SEQ], gain(c),
                                                    hi[:, c, :].bitcast(f32), ALU.mult, ALU.subtract)
                last.then_inc(turned_lo, 1)

        def passes(a_hi, a_lo, i, n):
            whole_hi, whole_lo = hi_tile(i, n), lo_tile(i, n)
            return ((a_hi, whole_hi), (a_hi, whole_lo), (a_lo, whole_hi))

        def start_tile(pe, i, g, first, r=0, rb=0):
            pe.wait_ge(lo_ready, i + 1 + r)
            if first and g >= 2:
                pe.wait_ge(block_free[g % 2], g // 2 + rb)

        def token_tile(pe, i, g, h, a_hi, a_lo, r=0, rb=0, halves=2):
            n = tiles[i][1]
            start_tile(pe, i, g, h == 0, r, rb)
            for k in range(4):
                for t in range(NT):
                    for q, (a, b) in enumerate(passes(a_hi, a_lo, i, n)):
                        last = pe.matmul(pair(g)[:, t * 512:t * 512 + n], a[:, 4 * h + k, t * P:(t + 1) * P],
                                         b[:, k * n:(k + 1) * n], start=(h == 0 and k == 0 and q == 0),
                                         stop=(h == halves - 1 and k == 3 and q == 2))
            last.then_inc(tile_used, 1)

        def feature_tile(pe, i, g, h, a_hi, a_lo, r=0, rb=0):
            start_tile(pe, i, g, h == 0, r, rb)
            for s in range(4):
                for k in range(4):
                    for q, (a, b) in enumerate(passes(a_hi, a_lo, i, 512)):
                        last = pe.matmul(pair(g)[:, s * SEQ:(s + 1) * SEQ], b[:, k * 512 + s * P:k * 512 + (s + 1) * P],
                                         a[:, 4 * h + k, :], start=(h == 0 and k == 0 and q == 0 and s % 2 == 0),
                                         stop=(h == 1 and k == 3 and q == 2), skip_group_check=True)
            last.then_inc(tile_used, 1)

        neg_lam, lam_s, lam_x = small(1), small(2), small(2)
        a_sum, a_rs, a_nb, a_c1 = small(8), small(4), small(4), small(2)
        ssq, rsq = small(64), small(64)
        g_o = small(1)
        sp_z, sp_s, sp_s2, sp_p = small(16), small(16), small(16), small(16)
        G1 = lambda c: prm("g1", c, c + 1)
        G2 = lambda c: prm("g2", c, c + 1)
        rope_t = slot(1)[:, 0:512].rearrange("p (z j t n) -> p z j t n", z=2, j=4, t=NT)
        qT, kT = fm(0), fm(1)
        v_tm, o_tm = tm(6), tm(4)
        r_fm, i_fm, y_fm = fm(3), fm(4), fm(7)
        h_fm = [fm(5), fm(0)]
        merged = fm(5)
        lru_w = slot(8, 2).rearrange("p (m g n) -> p m g n", m=2, g=2 * NC)

        def bc(a, shape):
            return a.unsqueeze(2).broadcast_to(shape)

        GA = 8

        def first_pe(pe):
            pe.wait_ge(par_in, 16)
            turn_pe(pe, 0, xn)
            pe.wait_ge(turned_lo, 4)
            for i in range(0, 8):
                feature_tile(pe, i, i // 2, i % 2, act_hi, act_lo)
            for d in range(2):
                for i in range(8 + 0 if d == 0 else 16 - 4, 12 if d == 0 else 20):
                    token_tile(pe, i, i // 2, i % 2, act_hi, act_lo)
                if d == 0:
                    pe.wait_ge(conv_ready, 1)
                    pe.wait_ge(lru_w_in, 32)
                for c in range(NC):
                    n = d * NC + c
                    if n >= 4:
                        pe.wait_ge(lru_sig, 2 * (n - 3))
                    for m in range(2):
                        last = pe.matmul(bank(4 + c % 4)[:, m * SEQ:(m + 1) * SEQ], lru_w[:, m, d * NC + c, :],
                                         fm(2)[:, c, :], start=True, stop=True)
                    last.then_inc(lru_mm, 1)
            for i in range(20, 28):
                feature_tile(pe, i, i // 2, i % 2, act_hi, act_lo)
            pe.wait_ge(mid_lo_ready, 1)
            for i in range(28, 32):
                feature_tile(pe, i, i // 2, i % 2, mid_hi, mid_lo)
            pe.wait_ge(lru_sig, 32)
            for z in range(2):
                pe.wait_ge(roped, z + 1)
                for b in range(4):
                    if z:
                        pe.wait_ge(qk_copied, b + 1)
                    for hh in range(2):
                        for t in range(NT):
                            last = pe.transpose(bank(4 + b)[:, hh * SEQ + t * P:hh * SEQ + (t + 1) * P],
                                                tm(2 + z)[:, t, (2 * b + hh) * P:(2 * b + hh + 1) * P], ident)
                    last.then_inc(qk_turned, 1)

            def scores(g):
                hp, t = g // 2, g % 2
                if g:
                    pe.wait_ge(a_exp, 4 * g)
                else:
                    pe.wait_ge(qk_copied, 8)
                for hh in range(2):
                    for c in range(2):
                        rows = slice(c * SUB, (c + 1) * SUB)
                        last = pe.matmul(bank(4 + c)[:, hh * SEQ:(hh + 1) * SEQ],
                                         qT[rows, 2 * hp + hh, t * P:(t + 1) * P], kT[rows, 2 * hp + hh, :],
                                         start=True, stop=True)
                last.then_inc(a_scores, 1)

            scores(0)
            for g in range(GA):
                hp = g // 2
                p = slot(7)[:, (g % 2) * 1024:(g % 2 + 1) * 1024].rearrange("p (s k) -> p s k", s=4)
                pt = slot(3)[:, (g % 2) * 512:(g % 2 + 1) * 512].rearrange("p (s k) -> p s k", s=4)
                if g + 1 < GA:
                    scores(g + 1)
                pe.wait_ge(a_diff, g + 1)
                if g:
                    pe.wait_ge(a_pt, g)
                for hh in range(2):
                    for kt in range(NT):
                        last = pe.transpose(bank(6)[:, (2 * hh + kt) * P:(2 * hh + kt + 1) * P],
                                            p[:, hh, kt * P:(kt + 1) * P], ident)
                last.then_inc(a_turned, 1)
                pe.wait_ge(a_pt, g + 1)
                if g:
                    pe.wait_ge(a_out, g)
                for hh in range(2):
                    for kt in range(NT):
                        last = pe.matmul(bank(7)[:, hh * VD:(hh + 1) * VD], pt[:, 2 * hh + kt, :],
                                         v_tm[:, kt, (2 * hp + hh) * VD:(2 * hp + hh + 1) * VD],
                                         start=(kt == 0), stop=(kt == 1))
                last.then_inc(a_pv, 1)
            pe.wait_ge(a_out, GA)
            turn_pe(pe, 1, tm(7))
            pe.wait_ge(turned_lo, 8)
            for i in range(32, 36):
                feature_tile(pe, i, i // 2, i % 2, act_hi, act_lo)
            pe.wait_ge(mid_lo_ready, 2)
            for i in range(36, 40):
                token_tile(pe, i, i // 2, i % 2, mid_hi, mid_lo)

        def first_act(act):
            own = Own(act, act_own)
            act.wait_ge(x_in, 16)
            norm_act(act, 0)
            act.wait_ge(par_in, 16)
            turn_act(act, 0, act_hi, G1)
            high(act, 0)
            high(act, 1)

            def read_block(g):
                act.wait_ge(tile_used, 2 * g + 2)
                src = pair(g)
                if g < 2:
                    nc.scalar.activation(slot(0)[:, g * 1024:(g + 1) * 1024], src, ACT.Copy)\
                        .then_inc(block_free[g % 2], 1)
                elif g < 4:
                    nc.scalar.activation(slot(1)[:, (g - 2) * 1024:(g - 1) * 1024], src, ACT.Gelu_apprx_tanh)\
                        .then_inc(block_free[g % 2], 1)
                elif g < 10:
                    dst = [tm(10), tm(11), tm(6)][(g - 4) // 2]
                    n = (g % 2) * 512
                    nc.scalar.activation(dst[:, :, n:n + 512], src.rearrange("p (t n) -> p t n", t=NT), ACT.Copy)\
                        .then_inc(block_free[g % 2], 1)
                else:
                    if g == 10:
                        act.wait_ge(lru_mm, 16)
                    for s in range(4):
                        c = 4 * (g - 10) + s
                        last = nc.scalar.activation(slot(8, 2)[:, c * SEQ:(c + 1) * SEQ], src[:, s * SEQ:(s + 1) * SEQ],
                                                    ACT.Sigmoid, bias=prm("bg", c, c + 1))
                    last.then_inc(block_free[g % 2], 1)

            def sigmoids(d):
                if d:
                    act.wait_ge(lru_scan, 1)
                for c in range(NC):
                    act.wait_ge(lru_mm, d * NC + c + 1)
                    for m, (dst, b) in enumerate(((r_fm, "ba"), (i_fm, "bi"))):
                        nc.scalar.activation(dst[:, c, :], bank(4 + c % 4)[:, m * SEQ:(m + 1) * SEQ], ACT.Sigmoid,
                                             bias=prm(b, d * NC + c, d * NC + c + 1)).then_inc(lru_sig, 1)

            def decay(d):
                act.wait_ge(lru_y, d + 1)
                own.done(nc.scalar.activation(r_fm, y_fm, ACT.Exp, scale=-1.0))
                own.wait()
                nc.scalar.activation(y_fm, y_fm, ACT.Tanh).then_inc(lru_ta, 1)

            def roots(d):
                act.wait_ge(lru_q, d + 1)
                nc.scalar.activation(h_fm[d], h_fm[d], ACT.Sqrt, scale=2.0).then_inc(lru_mult, 1)

            for i in range(28):
                high(act, i + 2)
                if i % 2:
                    read_block(i // 2)
                if i == 11:
                    sigmoids(0)
                if i == 19:
                    sigmoids(1)
                if i == 4:
                    act.wait_ge(lru_sp, 1)
                    nc.scalar.activation(sp_z, sp_z, ACT.Exp, scale=-1.0).then_inc(lru_sp, 1)
                if i == 13:
                    decay(0)
                if i == 15:
                    roots(0)
                if i == 21:
                    decay(1)
                if i == 23:
                    roots(1)
            act.wait_ge(y_sum, 1)
            nc.scalar.activation(mid_hi[:, :, :], fm(5), ACT.Copy).then_inc(mid_hi_ready, 1)
            act.wait_ge(lam_in, 1)
            nc.scalar.activation(lam_x, lam_s, ACT.Exp).then_inc(lam_e, 1)
            act.wait_ge(o_ms, 1)
            nc.scalar.activation(ssq, ssq, ACT.Sqrt).then_inc(o_rt, 1)
            for i in range(30, 34):
                high(act, i)
            for n in range(8):
                act.wait_ge(qk_turned, n + 1)
                dst = (qT if n < 4 else kT)[:, 2 * (n % 4):2 * (n % 4) + 2, :]
                nc.scalar.activation(dst, bank(4 + n % 4).rearrange("p (h t) -> p h t", h=2), ACT.Copy,
                                     scale=(SUB ** -0.5 if n < 4 else 1.0)).then_inc(qk_copied, 1)

            for g in range(GA):
                p = slot(7)[:, (g % 2) * 1024:(g % 2 + 1) * 1024].rearrange("p (s k) -> p s k", s=4)
                act.wait_ge(a_shift, g + 1)
                if g >= 2:
                    act.wait_ge(a_turned, g - 1)
                for s in range(4):
                    nc.scalar.activation(p[:, s, :], bank(4, 2)[:, s * SEQ:(s + 1) * SEQ], ACT.Exp,
                                         bias=a_nb[:, s:s + 1], accum_out=a_sum[:, 4 * (g % 2) + s:4 * (g % 2) + s + 1])\
                        .then_inc(a_exp, 1)
                act.wait_ge(a_turned, g + 1)
                if g >= 2:
                    act.wait_ge(a_pv, g - 1)
                nc.scalar.activation(slot(3)[:, (g % 2) * 512:(g % 2 + 1) * 512], bank(6), ACT.Copy)\
                    .then_inc(a_pt, 1)
            act.wait_ge(o_ms, 2)
            nc.scalar.activation(ssq[:, 0:16], ssq[:, 0:16], ACT.Sqrt).then_inc(o_rt, 1)
            turn_act(act, 1, act_hi, lambda c: g_o)
            for i in range(32, 36):
                if i >= 34 - 2:
                    high(act, i + 2)
            act.wait_ge(merged_ready, 1)
            nc.scalar.activation(mid_hi[:, :, :], merged, ACT.Copy).then_inc(mid_hi_ready, 1)
            for i in range(36, 40):
                high(act, i + 2)

        def first_dve(dve):
            own = Own(dve, dve_own)
            norm_dve(dve, 0)
            turn_dve(dve, 0, act_hi, act_lo, G1)
            feed = [0]

            def lows(n):
                for _ in range(n):
                    low(dve, feed[0])
                    feed[0] += 1

            lows(2)
            dve.wait_ge(par_in, 16)
            lam = prm("lru_lam")
            dve.scalar_tensor_tensor(sp_z, lam, -1.0, lam, ALU.mult, ALU.max).then_inc(lru_sp, 1)
            lows(4)
            dve.wait_ge(lru_sp, 2)
            own.done(dve.tensor_scalar(sp_s, sp_z, 2.0, None, ALU.add))
            own.wait()
            own.done(dve.reciprocal(sp_s, sp_s))
            own.wait()
            own.done(dve.tensor_tensor(sp_s, sp_s, sp_z, ALU.mult))
            own.wait()
            own.done(dve.tensor_tensor(sp_s2, sp_s, sp_s, ALU.mult))
            own.wait()
            own.done(dve.tensor_scalar(sp_p, sp_s2, 1.0 / 15, None, ALU.mult))
            for k in (13, 11, 9, 7, 5, 3):
                own.wait()
                own.done(dve.scalar_tensor_tensor(sp_p, sp_p, 1.0 / k, sp_s2, ALU.add, ALU.mult))
            own.wait()
            own.done(dve.scalar_tensor_tensor(sp_p, sp_p, 1.0, sp_s, ALU.add, ALU.mult))
            own.done(dve.tensor_scalar(sp_z, lam, -8.0, 0.0, ALU.mult, ALU.max))
            own.wait()
            own.done(dve.scalar_tensor_tensor(sp_z, sp_p, 16.0, sp_z, ALU.mult, ALU.add))

            for g in range(2):
                block_read(dve, g)
            lx, xr = fm(0), fm(2)
            for c in range(NC):
                cw = lambda j: prm("conv_w", j * NC + c, j * NC + c + 1)
                own.done(dve.tensor_scalar(xr[:, c, :], lx[:, c, :], cw(1), prm("conv_b", c, c + 1),
                                           ALU.mult, ALU.add))
            for n, (j, a, b) in enumerate(((0, 1, 0), (2, 0, 1), (3, 0, 2))):
                lows(1)
                own.wait()
                m = SEQ - max(a, b)
                for c in range(NC):
                    cw = prm("conv_w", j * NC + c, j * NC + c + 1)
                    last = own.done(dve.scalar_tensor_tensor(xr[:, c, a:a + m], lx[:, c, b:b + m], cw,
                                                             xr[:, c, a:a + m], ALU.mult, ALU.add))
            own.wait()
            dve.nop().then_inc(conv_ready, 1)
            lows(14 - feed[0])

            def lru(d, middle, late):
                dve.wait_ge(lru_sig, 16 * (d + 1))
                dve.tensor_tensor(y_fm, r_fm, bc(sp_z[:, d * NC:(d + 1) * NC], [P, NC, SEQ]), ALU.mult)\
                    .then_inc(lru_y, 1)
                own.done(dve.tensor_tensor(i_fm, i_fm, xr, ALU.mult))
                lows(middle)
                dve.wait_ge(lru_ta, d + 1)
                own.done(dve.tensor_scalar(h_fm[d], y_fm, 1.0, None, ALU.add))
                own.wait()
                own.done(dve.reciprocal(h_fm[d], h_fm[d]))
                own.wait()
                dve.tensor_tensor(h_fm[d], h_fm[d], y_fm, ALU.mult).then_inc(lru_q, 1)
                lows(2)
                dve.wait_ge(lru_mult, d + 1)
                own.done(dve.tensor_tensor(i_fm, i_fm, h_fm[d], ALU.mult))
                own.wait()
                step = 1 if d == 0 else -1
                for c in range(NC):
                    if c == 4:
                        lows(late)
                    last = dve.tensor_tensor_scan(h_fm[d][:, c, ::step], r_fm[:, c, ::step], i_fm[:, c, ::step], 0.0,
                                                  ALU.mult, ALU.add)
                last.then_inc(lru_scan, 1)

            lru(0, 2, 2)
            lows(23 - feed[0])
            lru(1, 1, 1)
            dve.wait_ge(lru_scan, 2)
            for g in (2, 3):
                block_read(dve, g)
            own.done(dve.tensor_tensor(fm(5), fm(5), fm(0), ALU.add))
            lows(28 - feed[0])
            own.wait()
            dve.tensor_tensor(fm(5), fm(5), fm(1), ALU.mult).then_inc(y_sum, 1)
            dve.wait_ge(y_sum, 1)
            lows(30 - feed[0])

            for g in range(4, 8):
                block_read(dve, g)
            for z in range(2):
                sq = slot(7)
                own.wait()
                own.done(dve.tensor_tensor(sq, slot(10 + z), slot(10 + z), ALU.mult))
                own.wait()
                own.done(dve.tensor_reduce(ssq[:, 32 * z:32 * z + 32], sq.rearrange("p (m n) -> p m n", n=SUB),
                                           AX.X, ALU.add))
            dve.wait_ge(mid_hi_ready, 1)
            dve.tensor_tensor(mid_lo[:, :, :], fm(5), mid_hi[:, :, :].bitcast(f32), ALU.subtract)\
                .then_inc(mid_lo_ready, 1)
            for m in range(2):
                a, b = prm("lam", 2 * m * SUB, (2 * m + 1) * SUB), prm("lam", (2 * m + 1) * SUB, (2 * m + 2) * SUB)
                own.done(dve.tensor_tensor_reduce(out=slot(2)[:, m * SUB:(m + 1) * SUB], in0=a, in1=b, scale=1.0,
                                                  scalar=0.0, op0=ALU.mult, op1=ALU.add,
                                                  accum_out=lam_s[:, m:m + 1]))
            own.wait()
            dve.nop().then_inc(lam_in, 1)
            own.wait()
            dve.tensor_scalar(ssq, ssq, 1.0 / SUB, EPS, ALU.mult, ALU.add).then_inc(o_ms, 1)
            own.done(dve.tensor_scalar(g_o, prm("subln"), 1.0 - LAM_INIT, None, ALU.mult))
            for z, gain in enumerate(("qg", "kg")):
                g = prm(gain)
                for j, (tab, half) in enumerate((("cos", 0), ("sin", 1), ("sin", 0), ("cos", 1))):
                    own.done(dve.tensor_tensor(
                        rope_t[:, z, j, :, :], prm(tab).rearrange("p (t n) -> p t n", t=NT),
                        g[:, 32 * half:32 * half + 32].unsqueeze(1).broadcast_to([P, NT, 32]), ALU.mult))
            dve.wait_ge(lam_e, 1)
            own.done(dve.scalar_tensor_tensor(neg_lam, lam_x[:, 1:2], -LAM_INIT, lam_x[:, 0:1], ALU.add,
                                              ALU.subtract))
            dve.wait_ge(o_rt, 1)
            own.done(dve.reciprocal(rsq, ssq))
            for z in range(2):
                own.wait()
                xs = slot(4).rearrange("p (t h n) -> p t h n", t=NT, h=16)
                own.done(dve.tensor_tensor(slot(4).rearrange("p (m n) -> p m n", n=SUB),
                                           slot(10 + z).rearrange("p (m n) -> p m n", n=SUB),
                                           bc(rsq[:, 32 * z:32 * z + 32], [P, 32, SUB]), ALU.mult))
                own.wait()
                x1, x2 = xs[:, :, :, 0:32], xs[:, :, :, 32:64]
                t1 = slot(7)[:, 0:1024].rearrange("p (t h n) -> p t h n", t=NT, h=16)
                t2 = slot(7)[:, 1024:2048].rearrange("p (t h n) -> p t h n", t=NT, h=16)
                dst = slot(2 + z).rearrange("p (t h n) -> p t h n", t=NT, h=16)

                def table(j):
                    return rope_t[:, z, j, :, :].unsqueeze(2).broadcast_to([P, NT, 16, 32])

                for half, op in ((0, ALU.subtract), (1, ALU.add)):
                    if half or z:
                        own.wait()
                    own.done(dve.tensor_tensor(t1, x1, table(2 * half), ALU.mult))
                    own.done(dve.tensor_tensor(t2, x2, table(2 * half + 1), ALU.mult))
                    own.wait()
                    last = own.done(dve.tensor_tensor(dst[:, :, :, 32 * half:32 * half + 32], t1, t2, op))
                own.wait()
                dve.nop().then_inc(roped, 1)
                lows(1)
                if z == 1:
                    lows(34 - feed[0])
                for g in ((14,) if z == 0 else (15,)):
                    gate_product(dve, g)

            def shift(g):
                dve.wait_ge(a_scores, g + 1)
                if g:
                    dve.wait_ge(a_exp, 4 * g)
                dve.tensor_reduce(a_nb, bank(4, 2).rearrange("p (s k) -> p s k", s=4), AX.X, ALU.max, negate=True)\
                    .then_inc(a_shift, 1)

            def output(g):
                hp, t = g // 2, g % 2
                dve.wait_ge(a_pv, g + 1)
                dve.tensor_tensor(o_tm[:, t, 2 * hp * VD:(2 * hp + 2) * VD].rearrange("p (h n) -> p h n", h=2),
                                  bank(7)[:, 0:2 * VD].rearrange("p (h n) -> p h n", h=2),
                                  bc(a_rs[:, 0:2], [P, 2, VD]), ALU.mult).then_inc(a_out, 1)

            for g in range(GA):
                p = slot(7)[:, (g % 2) * 1024:(g % 2 + 1) * 1024].rearrange("p (s k) -> p s k", s=4)
                shift(g)
                if g:
                    output(g - 1)
                    dve.wait_ge(a_out, g)
                dve.wait_ge(a_exp, 4 * (g + 1))
                s = a_sum[:, 4 * (g % 2):4 * (g % 2) + 4]
                own.done(dve.reciprocal(a_rs, s))
                own.wait()
                own.done(dve.scalar_tensor_tensor(a_c1, s[:, 0:2], neg_lam, a_rs[:, 2:4], ALU.mult, ALU.mult))
                own.wait()
                for hh in range(2):
                    last = dve.scalar_tensor_tensor(p[:, hh, :], p[:, 2 + hh, :], a_c1[:, hh:hh + 1],
                                                    p[:, hh, :], ALU.mult, ALU.add)
                last.then_inc(a_diff, 1)
            output(GA - 1)
            dve.wait_ge(a_out, GA)
            own.done(dve.tensor_tensor(slot(7), slot(4), slot(4), ALU.mult))
            own.wait()
            own.done(dve.tensor_reduce(ssq[:, 0:16], slot(7).rearrange("p (m n) -> p m n", n=VD), AX.X, ALU.add))
            own.wait()
            dve.tensor_scalar(ssq[:, 0:16], ssq[:, 0:16], 1.0 / VD, EPS, ALU.mult, ALU.add).then_inc(o_ms, 1)
            dve.wait_ge(o_rt, 2)
            own.done(dve.reciprocal(rsq[:, 0:16], ssq[:, 0:16]))
            own.wait()
            dve.tensor_tensor(slot(7).rearrange("p (m n) -> p m n", n=VD), slot(4).rearrange("p (m n) -> p m n", n=VD),
                              bc(rsq[:, 0:16], [P, 16, VD]), ALU.mult).then_inc(src_ready, 2)
            turn_dve(dve, 1, act_hi, act_lo, lambda c: g_o)
            lows(2)
            gate_product(dve, 16)
            lows(2)
            gate_product(dve, 17)
            dve.wait_ge(mid_hi_ready, 2)
            dve.tensor_tensor(mid_lo[:, :, :], merged, mid_hi[:, :, :].bitcast(f32), ALU.subtract)\
                .then_inc(mid_lo_ready, 1)
            for g in (18, 19):
                lows(2)
                add_block(dve, g, 2 * g + 2, g - 18)

            return own

        def gate_product(dve, g):
            dve.wait_ge(tile_used, 2 * g + 2)
            n = (g % 2) * 1024
            m = slot(5)[:, n:n + 1024]
            if g < 16:
                block_read(dve, 12 + g % 2)
                dve.tensor_tensor(m, pair(g), slot(9)[:, n:n + 1024], ALU.mult).then_inc(block_free[g % 2], 1)
            else:
                t = slot(7)[:, n:n + 1024]
                dve.tensor_tensor(t, pair(g), slot(8)[:, n:n + 1024], ALU.mult).then_inc(block_free[g % 2], 1)
                block_read(dve, g)
                dve.tensor_tensor(m, m, t, ALU.add).then_inc(merged_lo, 1)
                if g == 17:
                    dve.wait_ge(merged_lo, 2)
                    dve.nop().then_inc(merged_ready, 1)

        def add_block(dve, g, used, half):
            dve.wait_ge(tile_used, used)
            xs = x_tm[:, :, 512 * half:512 * half + 512]
            dve.tensor_tensor(xs, xs, pair(g).rearrange("p (t n) -> p t n", t=NT), ALU.add)\
                .then_inc(block_free[g % 2], 1)

        PAIRS = (EXPERTS - 2) // 2
        M0, B0 = T_MOE, T_MOE // 2
        PER_PAIR, BLOCKS_PAIR = 12, 8
        logits = slot(0)[:, 0:40].rearrange("p (t n) -> p t n", t=NT)
        cs = slot(1)[:, 0:NT * EXPERTS]
        silu_g, hid = slot(2)[:, 0:1024], slot(2)[:, 1024:2048]
        router_wh, router_wl = mid_hi[:, 7, 0:NC * 20], mid_lo[:, 7, 0:NC * 20]
        scratch_at = [64]

        def scratch(*dims):
            n = int(np.prod(dims))
            a = slot(0)[:, scratch_at[0]:scratch_at[0] + n]
            scratch_at[0] += n
            if len(dims) == 1:
                return a
            names = "abcd"[:len(dims)]
            return a.rearrange(f"p ({' '.join(names)}) -> p {' '.join(names)}", **dict(zip(names, dims)))

        g_dif, g_exp = scratch(2, 4), scratch(2, 4)
        e_dif, e_exp = scratch(2), scratch(2)

        def tiles_of(e):
            return M0 + 4 + 6 * (e - 1), B0 + 2 + 4 * (e - 1)

        def down_tile(pe, i, g, e, r=0, rb=0):
            start_tile(pe, i, g, True, r, rb)
            half = 4 * (e % 2)
            for k in range(4):
                for t in range(NT):
                    for q, (a, b) in enumerate(passes(mid_hi, mid_lo, i, 512)):
                        last = pe.matmul(pair(g)[:, t * 512:(t + 1) * 512], a[:, half + k, t * P:(t + 1) * P],
                                         b[:, k * 512:(k + 1) * 512], start=(k == 0 and q == 0),
                                         stop=(k == 3 and q == 2))
            last.then_inc(tile_used, 1)

        def expert_pe(pe, e, r=0, rb=0, re=0):
            i, g = tiles_of(e)
            for h in range(2):
                feature_tile(pe, i + h, g, h, act_hi, act_lo, r, rb)
            pe.wait_ge(hid_lo, e + re)
            for n in range(2):
                down_tile(pe, i + 2 + n, g + 1 + n, e - 1, r, rb)
            for h in range(2):
                feature_tile(pe, i + 4 + h, g + 3, h, act_hi, act_lo, r, rb)

        def moe_pe(pe):
            turn_pe(pe, 2, xn)
            pe.wait_ge(turned_lo, 12)
            pe.wait_ge(router_split, 2)
            for t in range(NT):
                for k in range(NC):
                    for q, (a, b) in enumerate(((act_hi, router_wh), (act_hi, router_wl), (act_lo, router_wh))):
                        last = pe.matmul(bank(4)[:, t * 20:t * 20 + 20], a[:, k, t * P:(t + 1) * P],
                                         b[:, k * 20:(k + 1) * 20], start=(k == 0 and q == 0),
                                         stop=(k == NC - 1 and q == 2))
            last.then_inc(router_mm, 1)
            for i in range(4):
                feature_tile(pe, M0 + i, B0 + i // 2, i % 2, act_hi, act_lo)
            with pe.Fori(0, PAIRS) as j:
                for e in (1, 2):
                    expert_pe(pe, e, j * PER_PAIR, j * (BLOCKS_PAIR // 2), j * 2)
            expert_pe(pe, EXPERTS - 1)
            pe.wait_ge(hid_lo, EXPERTS)
            i, g = tiles_of(EXPERTS)
            for n in range(2):
                down_tile(pe, i + n, g + n, EXPERTS - 1)

        def expert_high(act, e, g, used, r=0, rb=0):
            act.wait_ge(block_free[g % 2], g // 2 + 1 + rb)
            nc.scalar.activation(mid_hi[:, 4 * (e % 2):4 * (e % 2) + 4, :], hid.rearrange("p (k t) -> p k t", k=4),
                                 ACT.Copy).then_inc(hid_hi, 1)

        def expert_silu(act, i, g, r=0, rb=0, re=0, e=0):
            act.wait_ge(tile_used, i + 2 + r)
            if e:
                act.wait_ge(hid_lo, e + re)
            nc.scalar.activation(silu_g, pair(g), ACT.Silu).then_inc(block_free[g % 2], 1)

        def expert_act(act, e, r=0, rb=0, re=0):
            i, g = tiles_of(e)
            for n in range(6):
                if i + n + 2 < T_STOP:
                    high(act, i + n + 2, r)
                if n == 1:
                    expert_silu(act, i, g, r, rb, re, e)
                if n == 5:
                    expert_high(act, e, g + 3, i + 6, r, rb)

        def moe_act(act):
            for g in (18, 19):
                block_read(act, g)
            norm_act(act, 1)
            nc.scalar.activation(router_wh, prm("router_w"), ACT.Copy).then_inc(router_split, 1)
            turn_act(act, 2, act_hi, G2)
            for n in range(4):
                high(act, M0 + n + 2)
                if n == 0:
                    act.wait_ge(route_exp, 1)
                    nc.scalar.activation(g_exp, g_dif, ACT.Exp).then_inc(route_exp, 1)
                if n == 1:
                    expert_silu(act, M0, B0)
                if n == 2:
                    act.wait_ge(route_exp, 3)
                    nc.scalar.activation(e_exp, e_dif, ACT.Exp).then_inc(route_exp, 1)
                if n == 3:
                    expert_high(act, 0, B0 + 1, M0 + 4)
            with act.Fori(0, PAIRS) as j:
                for e in (1, 2):
                    expert_act(act, e, j * PER_PAIR, j * (BLOCKS_PAIR // 2), j * 2)
            expert_act(act, EXPERTS - 1)
            for n in range(2):
                i = tiles_of(EXPERTS)[0] + n
                if i + 2 < T_STOP:
                    high(act, i + 2)

        def expert_hidden(dve, e, i, g, g_gate, r=0, rb=0, re=0):
            dve.wait_ge(tile_used, i + r)
            dve.wait_ge(block_free[g_gate % 2], g_gate // 2 + 1 + rb)
            dve.tensor_tensor(hid, pair(g), silu_g, ALU.mult).then_inc(block_free[g % 2], 1)
            dve.wait_ge(hid_hi, e + 1 + re)
            h = 4 * (e % 2)
            dve.tensor_tensor(mid_lo[:, h:h + 4, :], hid.rearrange("p (k t) -> p k t", k=4),
                              mid_hi[:, h:h + 4, :].bitcast(f32), ALU.subtract).then_inc(hid_lo, 1)

        def expert_add(dve, e, n, i, g, before, r=0, rb=0, re=0):
            dve.wait_ge(tile_used, i + 1 + r)
            dve.wait_ge(block_free[before % 2], before // 2 + 1 + rb)
            for t in range(NT):
                xs = x_tm[:, t, 512 * n:512 * n + 512]
                c = cs[:, t * EXPERTS + e:t * EXPERTS + e + 1] if isinstance(re, int) else \
                    cs[:, bass.ds(re + (t * EXPERTS + e), 1)]
                last = dve.scalar_tensor_tensor(xs, pair(g)[:, t * 512:(t + 1) * 512], c, xs, ALU.mult, ALU.add)
            last.then_inc(block_free[g % 2], 1)

        def expert_dve(dve, e, r=0, rb=0, re=0):
            i, g = tiles_of(e)
            for n in range(6):
                if i + n + 2 < T_STOP:
                    low(dve, i + n + 2, r)
                if n in (2, 3):
                    expert_add(dve, e - 1, n - 2, i + n, g + n - 1, g + n - 5, r, rb, re)
                if n == 5:
                    expert_hidden(dve, e, i + 6, g + 3, g, r, rb, re)

        def first_match(dve, own, values, best, out4):
            tie, top = scratch(2, 4), scratch(2)
            own.done(dve.tensor_tensor(tie, values, bc(best, [P, NT, 4]), ALU.is_equal))
            own.wait()
            own.done(dve.tensor_tensor(tie, tie, prm("first").unsqueeze(1).broadcast_to([P, NT, 4]), ALU.mult))
            own.wait()
            own.done(dve.tensor_reduce(top, tie, AX.X, ALU.max))
            own.wait()
            own.done(dve.tensor_tensor(out4, tie, bc(top, [P, NT, 4]), ALU.is_equal))
            own.wait()

        def route(dve, own, between):
            g_max, g_one, g_sum = scratch(2), scratch(2, 4), scratch(2)
            dve.wait_ge(router_mm, 1)
            own.done(dve.tensor_tensor(logits, bank(4)[:, 0:40].rearrange("p (t n) -> p t n", t=NT),
                                       prm("router_b").unsqueeze(1).broadcast_to([P, NT, 20]), ALU.add))
            own.wait()
            gl = logits[:, :, 0:4]
            own.done(dve.tensor_reduce(g_max, gl, AX.X, ALU.max))
            own.wait()
            dve.tensor_tensor(g_dif, gl, bc(g_max, [P, NT, 4]), ALU.subtract).then_inc(route_exp, 1)
            first_match(dve, own, gl, g_max, g_one)
            between(1)
            mix, es = scratch(2, 4, 4), scratch(2, 4)
            own.done(dve.tensor_tensor(mix, logits[:, :, 4:20].rearrange("p t (g e) -> p t e g", g=4),
                                       g_one.unsqueeze(2).broadcast_to([P, NT, 4, 4]), ALU.mult))
            own.wait()
            own.done(dve.tensor_reduce(es, mix, AX.X, ALU.add))
            own.wait()
            m1, m2, one1, one2, es2 = scratch(2), scratch(2), scratch(2, 4), scratch(2, 4), scratch(2, 4)
            own.done(dve.tensor_reduce(m1, es, AX.X, ALU.max))
            own.wait()
            first_match(dve, own, es, m1, one1)
            own.done(dve.scalar_tensor_tensor(es2, one1, NEG, es, ALU.mult, ALU.add))
            own.wait()
            own.done(dve.tensor_reduce(m2, es2, AX.X, ALU.max))
            own.wait()
            dve.wait_ge(route_exp, 2)
            dve.tensor_tensor(e_dif, m2, m1, ALU.subtract).then_inc(route_exp, 1)
            first_match(dve, own, es2, m2, one2)
            own.done(dve.tensor_reduce(g_sum, g_exp, AX.X, ALU.add))
            between(2)
            w1, w2, cw, cw2 = scratch(2), scratch(2), scratch(2, 4), scratch(2, 4)
            own.wait()
            dve.wait_ge(route_exp, 4)
            own.done(dve.scalar_tensor_tensor(w1, e_exp, 1.0, g_sum, ALU.add, ALU.mult))
            own.wait()
            own.done(dve.reciprocal(w1, w1))
            own.wait()
            own.done(dve.tensor_tensor(w2, w1, e_exp, ALU.mult))
            own.done(dve.tensor_tensor(cw, one1, bc(w1, [P, NT, 4]), ALU.mult))
            own.wait()
            own.done(dve.tensor_tensor(cw2, one2, bc(w2, [P, NT, 4]), ALU.mult))
            own.wait()
            own.done(dve.tensor_tensor(cw, cw, cw2, ALU.add))
            own.wait()
            own.done(dve.tensor_tensor(cs.rearrange("p (t g e) -> p t g e", t=NT, g=4), bc3(g_one),
                                       cw.unsqueeze(2).broadcast_to([P, NT, 4, 4]), ALU.mult))
            own.wait()

        def bc3(a):
            return a.unsqueeze(3).broadcast_to([P, NT, 4, 4])

        def moe_dve(dve, own):
            norm_dve(dve, 1)
            dve.wait_ge(router_split, 1)
            dve.tensor_tensor(router_wl, prm("router_w"), router_wh.bitcast(f32), ALU.subtract)\
                .then_inc(router_split, 1)
            turn_dve(dve, 2, act_hi, act_lo, G2)
            at = [M0 + 2]

            def between(n):
                for _ in range(n):
                    low(dve, at[0])
                    at[0] += 1

            between(1)
            route(dve, own, between)
            assert at[0] == M0 + 6
            expert_hidden(dve, 0, M0 + 4, B0 + 1, B0)
            with dve.Fori(0, PAIRS) as j:
                for e in (1, 2):
                    expert_dve(dve, e, j * PER_PAIR, j * (BLOCKS_PAIR // 2), j * 2)
            expert_dve(dve, EXPERTS - 1)
            i, g = tiles_of(EXPERTS)
            for n in range(2):
                if i + n + 2 < T_STOP:
                    low(dve, i + n + 2)
                expert_add(dve, EXPERTS - 1, n, i + n, g + n, g + n - 3)

        def moe_sp(sp):
            for i in range(M0, M0 + 4):
                load_tile(sp, i)
            with sp.Fori(0, PAIRS) as j:
                for e in (1, 2):
                    i = tiles_of(e)[0]
                    for n in range(6):
                        m = (w["w_expert_gate"], w["w_expert_down"], w["w_expert_up"])[n // 2][0]
                        one = m[bass.ds(j * 2 + (e - 1 if n in (2, 3) else e), 1)]
                        if n in (2, 3):
                            src = one[:, :, 512 * (n - 2):512 * (n - 2) + 512]
                        else:
                            src = one[:, 512 * (n % 2):512 * (n % 2) + 512, :]
                        load_tile(sp, i + n, j * PER_PAIR, (src.rearrange("o (k p) n -> p (o k) n", p=P), 512))
            for i in range(tiles_of(EXPERTS - 1)[0], T_LAYERS):
                load_tile(sp, i)

        L_TILES, L_BLOCKS = 40, 26
        W_GATE, W_CMP, W_BRANCH, W_OUT = 14, 22, 32, 36
        B_GATE, B_BRANCH, B_LOUT = 8, 16, 24
        TB, BB = T_LAYERS, 84

        def gate_tile(n):
            return W_GATE + n if n < 8 else W_CMP + 2 + n - 8

        KINDS = ["A", "D", "B", "cmp", "slc", "win"]
        GROUPS_L = [(kind, t) for kind in KINDS for t in range(NT)]
        NG = len(GROUPS_L)
        ROUNDS = [t + 1 if kind != "cmp" else 1 for kind, t in GROUPS_L]
        FIRST_ROUND = [sum(ROUNDS[:g]) for g in range(NG + 1)]
        NR = FIRST_ROUND[NG]
        FILLER = [0, 1, 2, 3, 6, 7, 8, 9, 10, 11, 12, 13]

        proj = arena[:, 0:NT * PROJ2].rearrange("p (t n) -> p t n", t=NT)
        kTs = arena[:, 7168:8192].rearrange("p (h t) -> p h t", h=4)
        gates = slot(4, 4)
        y_tm = tm(8)
        mask_at = 9 * SLOT
        mask_all = arena[:, mask_at:mask_at + 5 * 512]
        mask = {m: arena[:, mask_at + 512 * n:mask_at + 512 * n + 512].rearrange("p (t k) -> p t k", t=NT)
                for n, m in enumerate(MASKS)}
        pTs = arena[:, mask_at + 2560:mask_at + 3072]
        qTs = arena[:, mask_at + 3072:mask_at + 4096].rearrange("p (h t) -> p h t", h=4)
        uq = slot(7)[:, 0:768].rearrange("p (k n) -> p k n", k=2)
        ukv = slot(7)[:, 768:1280]
        probs = [slot(11)[:, 1024 * b:1024 * b + 1024].rearrange("p (h k) -> p h k", h=4) for b in range(2)]
        c_mask = extra[:, 0:128].rearrange("p (t h n) -> p t h n", t=NT, h=4)
        blk_hi, blk_lo = (m[:, 0:2, :].rearrange("p c t -> p (c t)") for m in (mid_hi, mid_lo))
        hidT = extra[:, 128:160].rearrange("p (v n) -> p v n", v=2)
        kcT = extra[0:HD, 160:176]
        vcmp = extra[0:NCP, 176:240]
        l_nb, l_sum, l_rs, l_co = small(4), small(4), small(4), small(4)
        m_ss, m_ms, m_rt, m_rs = small(4), small(4), small(4), small(4)
        NGAIN = lambda c: lpar("ng", c, c + 1)
        UNIT = lambda c: 1.0

        def rows_of(kind):
            return MQK if kind == "B" else HD

        def keys_of(kind, t, h):
            n = (t + 1) * P
            if kind == "cmp":
                return kcT
            if kind in ("slc", "win"):
                return kTs[0:HD, 0 if kind == "slc" else 1, 0:n]
            return kTs[0:rows_of(kind), h, 0:n]

        def values_of(kind, kt, h):
            if kind == "cmp":
                return vcmp
            if kind == "B":
                return y_tm[:, kt, 512 + HD * h:512 + HD * h + HD]
            at = {"A": AV + HD * h, "D": DV + HD * h, "slc": CVS, "win": CVW}[kind]
            return proj[:, kt, at:at + HD]

        def layer_pe(pe, l):
            r, rb = l * L_TILES, l * (L_BLOCKS // 2)
            k = l * 2 + 3
            turn_pe(pe, k, xn)
            pe.wait_ge(turned_lo, k * 4 + 4)
            for i in range(W_GATE):
                token_tile(pe, TB + i, BB + i // 2, i % 2, act_hi, act_lo, r, rb)

            def filler(n):
                feature_tile(pe, TB + gate_tile(n), BB + B_GATE + n // 2, n % 2, act_hi, act_lo, r, rb)

            def turn_heads(b, srcs, width):
                for h, src in enumerate(srcs):
                    for t in range(NT):
                        last = pe.transpose(bank(b)[0:width, h * SEQ + t * P:h * SEQ + (t + 1) * P], src(t), ident)
                return last

            def heads(at, width=HD, n=4):
                return [lambda t, h=h: proj[:, t, at + width * h:at + width * (h + 1)] for h in range(n)]

            def prepare(kind):
                if kind in ("A", "D"):
                    q, kk, n = (AQ, AK, 0) if kind == "A" else (DQ, DK, 1)
                    if kind == "A":
                        for g in (6, 7):
                            pe.wait_ge(block_free[(BB + g) % 2], (BB + g) // 2 + 1 + rb)
                    else:
                        pe.wait_ge(l_out, 2 + l * NG)
                    pe.transpose(bank(4)[:, 0:P], ident, ident)
                    for b, srcs in enumerate((heads(q)[0:2], heads(q)[2:4], heads(kk)[0:2], heads(kk)[2:4])):
                        last = turn_heads(4 + b, srcs, HD)
                    last.then_inc(prep_pe, 1)
                    pe.wait_ge(prep_act, n + 1 + l * 11)
                    pe.wait_ge(prep_dve, n + 1 + l * 9)
                elif kind == "B":
                    pe.wait_ge(l_out, 4 + l * NG)
                    pe.wait_ge(prep_dve, 4 + l * 9)
                    stage = slot(11)[:, 0:640].rearrange("p (t n) -> p t n", t=NT)
                    for t in range(NT):
                        cols = slice(t * P, (t + 1) * P)
                        pe.transpose(bank(4)[:, cols], stage[:, t, 0:P], ident)
                        pe.transpose(bank(4)[0:MQ - P, SEQ + t * P:SEQ + (t + 1) * P], stage[:, t, P:MQ], ident)
                        last = pe.transpose(bank(5)[:, cols], stage[:, t, MQ:MQ + MKV], ident)
                    last.then_inc(prep_pe, 1)
                    filler(4)
                    pe.wait_ge(prep_act, 5 + l * 11)
                    pe.wait_ge(layer_in, 64 + l * 64)
                    cT = slot(11)[:, 1024:1792].rearrange("p (k t) -> p k t", k=3)
                    for t in range(NT):
                        cols = slice(t * P, (t + 1) * P)
                        pe.matmul(bank(6 + t)[:, 0:384], cT[:, 0, cols], uq[:, 0, :], start=True, stop=False)
                        pe.matmul(bank(6 + t)[:, 0:384], cT[0:MQ - P, 1, cols], uq[0:MQ - P, 1, :],
                                  start=False, stop=True)
                        last = pe.matmul(bank(4 + t), cT[:, 2, cols], ukv, start=True, stop=True)
                    last.then_inc(prep_pe, 1)
                    filler(5)
                    pe.wait_ge(prep_act, 6 + l * 11)
                    pe.wait_ge(prep_dve, 5 + l * 9)
                    q, kk = heads(0, MQK), heads(384, MQK)
                    for b, srcs in enumerate((q[0:2], q[2:4], kk[0:2], kk[2:4])):
                        last = turn_heads(4 + b, srcs, MQK)
                    last.then_inc(prep_pe, 1)
                    pe.wait_ge(prep_act, 7 + l * 11)
                    pe.wait_ge(prep_dve, 6 + l * 9)
                elif kind == "cmp":
                    pe.wait_ge(l_out, 6 + l * NG)
                    for t in range(NT):
                        pe.transpose(bank(4)[:, t * P:(t + 1) * P], proj[:, t, CKC:CKC + P], ident)
                    turn_heads(5, heads(CQ)[0:2], HD)
                    turn_heads(6, heads(CQ)[2:4], HD)
                    turn_heads(7, [lambda t: proj[:, t, CKS:CKS + HD], lambda t: proj[:, t, CKW:CKW + HD]], HD)\
                        .then_inc(prep_pe, 1)
                    pe.wait_ge(prep_act, 9 + l * 11)
                    pe.wait_ge(prep_dve, 8 + l * 9)
                    for half in range(2):
                        i = TB + W_CMP + half
                        pe.wait_ge(lo_ready, i + 1 + r)
                        for v in range(2):
                            rows = slice(HD * v, HD * v + HD)
                            for n in range(16):
                                pos = 16 * half + n
                                cols = slice(NCP * pos, NCP * pos + NCP)
                                for q, (a, b) in enumerate(passes(blk_hi, blk_lo, i, 512)):
                                    last = pe.matmul(bank(4 + v)[:, 0:NCP], b[rows, n * P:(n + 1) * P], a[rows, cols],
                                                     start=(pos == 0 and q == 0), stop=(pos == 31 and q == 2))
                        last.then_inc(tile_used, 1)
                    pe.wait_ge(prep_act, 10 + l * 11)
                    pe.matmul(bank(6)[0:HD, 0:NCP], lpar("w2", 0, HD), hidT[:, 0, :], start=True, stop=True)
                    pe.matmul(bank(7)[0:NCP, 0:HD], hidT[:, 1, :], lpar("w2", HD, 2 * HD), start=True, stop=True)\
                        .then_inc(prep_pe, 1)
                    pe.wait_ge(prep_act, 11 + l * 11)
                    pe.wait_ge(prep_dve, 9 + l * 9)

            for g, (kind, t) in enumerate(GROUPS_L):
                if t == 0:
                    prepare(kind)
                n = NCP if kind == "cmp" else (t + 1) * P
                for h in range(H2):
                    last = pe.matmul(bank(4 + h // 2)[:, (h % 2) * SEQ:(h % 2) * SEQ + n],
                                     qTs[0:rows_of(kind), h, t * P:(t + 1) * P], keys_of(kind, t, h),
                                     start=True, stop=True)
                last.then_inc(l_scores, 1)
                filler(FILLER[g])
                pe.wait_ge(l_exp, g + 1 + l * NG)
                per = H2 // ROUNDS[g]
                kts = 1 if kind == "cmp" else t + 1
                for rd in range(ROUNDS[g]):
                    m = FIRST_ROUND[g] + rd
                    keys = NCP if kind == "cmp" else P
                    if m:
                        pe.wait_ge(l_copied, m + l * NR)
                    for hh in range(per):
                        for kt in range(kts):
                            last = pe.transpose(bank(6)[0:keys, (hh * kts + kt) * P:(hh * kts + kt + 1) * P],
                                                probs[g % 2][:, rd * per + hh, kt * P:kt * P + keys], ident)
                    last.then_inc(l_turned, 1)
                    pe.wait_ge(l_copied, m + 1 + l * NR)
                    if rd == 0 and g:
                        pe.wait_ge(l_out, g + l * NG)
                    for hh in range(per):
                        h = rd * per + hh
                        for kt in range(kts):
                            last = pe.matmul(bank(7)[:, HD * h:HD * h + HD],
                                             pTs[0:keys, (hh * kts + kt) * P:(hh * kts + kt + 1) * P],
                                             values_of(kind, kt, h), start=(kt == 0), stop=(kt == kts - 1))
                    last.then_inc(l_pv, 1)
            filler(14)
            filler(15)
            turn_pe(pe, k + 1, y_tm)
            pe.wait_ge(turned_lo, k * 4 + 8)
            for br in range(4):
                i = TB + W_BRANCH + br
                for half in range(2):
                    g = BB + B_BRANCH + 2 * br + half
                    start_tile(pe, i, g, True, r, rb)
                    for s in range(4):
                        at = half * 512 + s * P
                        for kc in range(2):
                            for q, (a, b) in enumerate(passes(mid_hi, mid_lo, i, 512)):
                                last = pe.matmul(pair(g)[:, s * SEQ:(s + 1) * SEQ], b[:, kc * D + at:kc * D + at + P],
                                                 a[:, 2 * br + kc, :], start=(kc == 0 and q == 0 and s % 2 == 0),
                                                 stop=(kc == 1 and q == 2), skip_group_check=True)
                last.then_inc(tile_used, 1)
            pe.wait_ge(mid_lo_ready, l + 3)
            for n in range(4):
                token_tile(pe, TB + W_OUT + n, BB + B_LOUT + n // 2, n % 2, act_hi, act_lo, r, rb)

        def layer_act(act, l):
            own = Own(act, l_act_own, l * OWN_ACT)
            r, rb = l * L_TILES, l * (L_BLOCKS // 2)
            k = l * 2 + 3

            def feed(n):
                high(act, TB + n + 2, r)

            def feed_gate(n):
                feed(gate_tile(n))
                if n % 2:
                    g = BB + B_GATE + n // 2
                    act.wait_ge(tile_used, TB + gate_tile(n) + 1 + r)
                    for s in range(4):
                        c = 4 * (n // 2) + s
                        last = nc.scalar.activation(gates[:, c * SEQ:(c + 1) * SEQ], pair(g)[:, s * SEQ:(s + 1) * SEQ],
                                                    ACT.Sigmoid, bias=lpar("bm", c, c + 1))
                    last.then_inc(block_free[g % 2], 1)

            high(act, TB, r)
            high(act, TB + 1, r)
            for g in (BB - 2, BB - 1):
                act.wait_ge(block_free[g % 2], g // 2 + 1 + rb)
            norm_act(act, l + 2)
            act.wait_ge(layer_in, 64 + l * 64)
            turn_act(act, k, act_hi, NGAIN)
            for i in range(W_GATE):
                feed(i)
                if i % 2:
                    g = i // 2
                    n = min(512, PROJ2 - 512 * g)
                    act.wait_ge(tile_used, TB + i + 1 + r)
                    src = pair(BB + g).rearrange("p (t n) -> p t n", t=NT)[:, :, 0:n]
                    nc.scalar.activation(proj[:, :, 512 * g:512 * g + n], src, ACT.Copy)\
                        .then_inc(block_free[(BB + g) % 2], 1)
            act.nop().then_inc(block_free[(BB + 7) % 2], 1)
            rows = {"A": HD, "D": HD, "B": MQK}

            def take_queries(kind, n, b=4):
                act.wait_ge(prep_pe, n + l * 7)
                w_ = rows_of(kind)
                return nc.scalar.activation(qTs[0:w_, :, :], bank(b, 2)[0:w_, :].rearrange("p (h t) -> p h t", h=4),
                                            ACT.Copy, scale=float(w_) ** -0.5)

            def prepare(kind):
                if kind == "A":
                    take_queries(kind, 1).then_inc(prep_act, 1)
                    for g in (5, 6):
                        act.wait_ge(block_free[(BB + g) % 2], (BB + g) // 2 + 1 + rb)
                    for at in (AG, BG, CG, DG):
                        nc.scalar.activation(proj[:, :, at:at + BW], proj[:, :, at:at + BW], ACT.Silu)
                    nc.scalar.activation(proj[:, :, CGT:CGT + 12], proj[:, :, CGT:CGT + 12], ACT.Sigmoid)\
                        .then_inc(gates_ready, 1)
                elif kind == "D":
                    take_queries(kind, 2).then_inc(prep_act, 1)
                elif kind == "B":
                    act.wait_ge(l_turned, FIRST_ROUND[3] + l * NR)
                    for n, (at, w_) in enumerate(((BCQ, MQ), (BCKV, MKV))):
                        for t in range(NT):
                            last = nc.scalar.activation(slot(11)[:, 0:w_], proj[:, t, at:at + w_], ACT.Square,
                                                        accum_out=m_ss[:, 2 * n + t:2 * n + t + 1])
                            if (n, t) != (1, 1):
                                own.done(last)
                                own.wait()
                    last.then_inc(prep_act, 1)
                    act.wait_ge(prep_dve, 3 + l * 9)
                    nc.scalar.activation(m_rt, m_ms, ACT.Sqrt).then_inc(prep_act, 1)
                    act.wait_ge(prep_pe, 3 + l * 7)
                    cT = slot(11)[:, 1024:1792].rearrange("p (k t) -> p k t", k=3)
                    nc.scalar.activation(cT[:, 0, :], bank(4)[:, 0:SEQ], ACT.Copy, scale=lpar("mqg", 0, 1))
                    nc.scalar.activation(cT[0:MQ - P, 1, :], bank(4)[0:MQ - P, SEQ:2 * SEQ], ACT.Copy,
                                         scale=lpar("mqg", 1, 2)[0:MQ - P])
                    nc.scalar.activation(cT[:, 2, :], bank(5)[:, 0:SEQ], ACT.Copy, scale=lpar("mkvg", 0, 1))\
                        .then_inc(prep_act, 1)
                    feed_gate(4)
                    act.wait_ge(prep_pe, 4 + l * 7)
                    nc.scalar.activation(proj[:, :, 0:384], bank(6, 2).rearrange("p (t n) -> p t n", t=NT)[:, :, 0:384],
                                         ACT.Copy)
                    kv = bank(4, 2).rearrange("p (t h n) -> p t h n", t=NT, h=4)
                    nc.scalar.activation(proj[:, :, 384:768].rearrange("p t (h n) -> p t h n", h=4)[:, :, :, 0:MN],
                                         kv[:, :, :, 0:MN], ACT.Copy)
                    nc.scalar.activation(y_tm[:, :, 512:768].rearrange("p t (h n) -> p t h n", h=4),
                                         kv[:, :, :, MN:MN + HD], ACT.Copy).then_inc(prep_act, 1)
                    feed_gate(5)
                    take_queries(kind, 5).then_inc(prep_act, 1)
                elif kind == "cmp":
                    take_queries(kind, 6, 5)
                    nc.scalar.activation(kTs[0:HD, 0:2, :], bank(7)[0:HD, :].rearrange("p (h t) -> p h t", h=2),
                                         ACT.Copy).then_inc(prep_act, 1)
                    act.wait_ge(prep_dve, 7 + l * 9)
                    nc.scalar.activation(blk_hi, slot(11)[:, 256:768], ACT.Copy).then_inc(prep_act, 1)
                    act.wait_ge(tile_used, TB + W_CMP + 2 + r)
                    for v in range(2):
                        last = nc.scalar.activation(hidT[:, v, :], bank(4 + v)[:, 0:NCP], ACT.Gelu_apprx_tanh,
                                                    bias=lpar("b1", v, v + 1))
                    last.then_inc(prep_act, 1)
                    feed(W_CMP)
                    act.wait_ge(prep_pe, 7 + l * 7)
                    nc.scalar.activation(kcT, bank(6)[0:HD, 0:NCP], ACT.Identity, bias=lpar("b2k", 0, 1)[0:HD])\
                        .then_inc(prep_act, 1)
                    feed(W_CMP + 1)

            for g, (kind, t) in enumerate(GROUPS_L):
                if t == 0:
                    prepare(kind)
                n = NCP if kind == "cmp" else (t + 1) * P
                p = probs[g % 2][:, :, 0:n]
                s = bank(4, 2).rearrange("p (h k) -> p h k", h=4)[:, :, 0:n]
                if kind == "D":
                    act.wait_ge(l_scores, g + 1 + l * NG)
                    own.done(nc.scalar.activation(p, s, ACT.Abs))
                    own.wait()
                    own.done(nc.scalar.activation(p, p, ACT.Exp, scale=-1.0))
                    own.wait()
                    nc.scalar.activation(p, p, ACT.Ln, bias=1.0).then_inc(l_logs, 1)
                    act.wait_ge(l_shift, g + 1 + l * NG)
                    nc.scalar.activation(p, p, ACT.Exp).then_inc(l_exp, 1)
                else:
                    act.wait_ge(l_shift, g + 1 + l * NG)
                    for h in range(H2):
                        last = nc.scalar.activation(p[:, h, :], p[:, h, :], ACT.Exp, bias=l_nb[:, h:h + 1],
                                                    accum_out=l_sum[:, h:h + 1])
                    last.then_inc(l_exp, 1)
                for rd in range(ROUNDS[g]):
                    m = FIRST_ROUND[g] + rd
                    act.wait_ge(l_turned, m + 1 + l * NR)
                    act.wait_ge(l_pv, m + l * NR) if m else None
                    keys = NCP if kind == "cmp" else P
                    nc.scalar.activation(pTs[0:keys, :], bank(6)[0:keys, :], ACT.Copy).then_inc(l_copied, 1)
                feed_gate(FILLER[g])
            feed_gate(14)
            feed_gate(15)
            turn_act(act, k + 1, mid_hi, UNIT)
            for br in range(4):
                feed(W_BRANCH + br)
            act.wait_ge(merged_ready, l + 2)
            nc.scalar.activation(act_hi[:, :, :], fm(0), ACT.Copy).then_inc(mid_hi_ready, 1)
            for n in range(4):
                if n < 2:
                    feed(W_OUT + n)
            return own

        def layer_dve(dve, l):
            own = Own(dve, l_dve_own, l * OWN_DVE)
            r, rb = l * L_TILES, l * (L_BLOCKS // 2)
            k = l * 2 + 3

            def feed(n):
                low(dve, TB + n + 2, r)

            low(dve, TB, r)
            low(dve, TB + 1, r)
            norm_dve(dve, l + 2)
            turn_dve(dve, k, act_hi, act_lo, NGAIN)
            for i in range(W_GATE):
                feed(i)

            def take_keys(kind, n):
                dve.wait_ge(prep_pe, n + l * 7)
                w_ = rows_of(kind)
                dve.tensor_copy(kTs[0:w_, :, :], bank(6, 2)[0:w_, :].rearrange("p (h t) -> p h t", h=4))\
                    .then_inc(prep_dve, 1)

            def rotate(x1, x2, o1, o2, n, at):
                temps = [slot(11)[:, at + 128 * j:at + 128 * j + 32 * n].rearrange("p (t h n) -> p t h n", t=NT, h=n)
                         for j in range(4)]
                cos, sin = (prm(m).rearrange("p (t n) -> p t n", t=NT).unsqueeze(2).broadcast_to([P, NT, n, 16])
                            for m in ("mcos", "msin"))
                for o, a, b in zip(temps, (x1, x2, x1, x2), (cos, sin, sin, cos)):
                    own.done(dve.tensor_tensor(o, a, b, ALU.mult))
                own.wait()
                own.done(dve.tensor_tensor(o1, temps[0], temps[1], ALU.subtract))
                return own.done(dve.tensor_tensor(o2, temps[2], temps[3], ALU.add))

            def prepare(kind):
                if kind == "A":
                    take_keys(kind, 1)
                elif kind == "D":
                    take_keys(kind, 2)
                elif kind == "B":
                    dve.wait_ge(prep_act, 3 + l * 11)
                    own.done(dve.tensor_scalar(m_ms[:, 0:2], m_ss[:, 0:2], 1.0 / MQ, EPS, ALU.mult, ALU.add))
                    own.done(dve.tensor_scalar(m_ms[:, 2:4], m_ss[:, 2:4], 1.0 / MKV, EPS, ALU.mult, ALU.add))
                    own.wait()
                    dve.nop().then_inc(prep_dve, 1)
                    dve.wait_ge(prep_act, 4 + l * 11)
                    own.done(dve.reciprocal(m_rs, m_rt))
                    own.wait()
                    stage = slot(11)[:, 0:640].rearrange("p (t n) -> p t n", t=NT)
                    for n, (at, w_, o) in enumerate(((BCQ, MQ, 0), (BCKV, MKV, MQ))):
                        for t in range(NT):
                            own.done(dve.tensor_scalar(stage[:, t, o:o + w_], proj[:, t, at:at + w_],
                                                       m_rs[:, 2 * n + t:2 * n + t + 1], None, ALU.mult))
                    own.wait()
                    dve.nop().then_inc(prep_dve, 1)
                    feed(gate_tile(4))
                    dve.wait_ge(prep_act, 6 + l * 11)
                    q = proj[:, :, 0:384].rearrange("p t (h n) -> p t h n", h=4)
                    kk = proj[:, :, 384:768].rearrange("p t (h n) -> p t h n", h=4)
                    x1, x2 = q[:, :, :, MN:MN + 16], q[:, :, :, MN + 16:MN + 32]
                    rotate(x1, x2, x1, x2, 4, 0)
                    kp = proj[:, :, BKPE:BKPE + MR].unsqueeze(2)
                    kr = slot(11)[:, 512 + 512:512 + 576].rearrange("p (t h n) -> p t h n", t=NT, h=1)
                    rotate(kp[:, :, :, 0:16], kp[:, :, :, 16:32], kr[:, :, :, 0:16], kr[:, :, :, 16:32], 1, 512)
                    own.wait()
                    for t in range(NT):
                        own.done(dve.tensor_copy(kk[:, t, :, MN:MQK], kr[:, t, :, :].broadcast_to([P, 4, MR])))
                    own.wait()
                    dve.nop().then_inc(prep_dve, 1)
                    feed(gate_tile(5))
                    take_keys(kind, 5)
                elif kind == "cmp":
                    dve.wait_ge(prep_pe, 6 + l * 7)
                    kv = slot(11)[:, 0:SEQ]
                    own.done(dve.tensor_copy(kv, bank(4)[:, 0:SEQ]))
                    blocks_f = slot(11)[:, 256:768].rearrange("p (s n) -> p s n", s=CMP_BLOCK)
                    own.done(dve.memset(blocks_f[:, 16:32, 15:16], 0.0))
                    own.wait()
                    kv = kv.rearrange("p (n s) -> p s n", s=16)
                    for a in range(2):
                        m = NCP - a
                        own.done(dve.tensor_tensor(blocks_f[:, 16 * a:16 * a + 16, 0:m], kv[:, :, a:a + m],
                                                   bc(lpar("pos", 16 * a, 16 * a + 16), [P, 16, m]), ALU.add))
                    own.wait()
                    dve.nop().then_inc(prep_dve, 1)
                    dve.wait_ge(prep_act, 9 + l * 11)
                    dve.tensor_tensor(blk_lo, slot(11)[:, 256:768], blk_hi.bitcast(f32), ALU.subtract)\
                        .then_inc(prep_dve, 1)
                    feed(W_CMP)
                    dve.wait_ge(prep_pe, 7 + l * 7)
                    dve.tensor_tensor(vcmp, bank(7)[0:NCP, 0:HD], lpar("b2v", 0, HD)[0:NCP], ALU.add)\
                        .then_inc(prep_dve, 1)
                    feed(W_CMP + 1)

            def arguments(g, kind, t):
                n = NCP if kind == "cmp" else (t + 1) * P
                p = probs[g % 2][:, :, 0:n]
                s = bank(4, 2).rearrange("p (h k) -> p h k", h=4)[:, :, 0:n]

                def rows_mask(m):
                    return mask[m][:, t, 0:n].unsqueeze(1).broadcast_to([P, 4, n])

                dve.wait_ge(l_scores, g + 1 + l * NG)
                if kind == "D":
                    dve.wait_ge(l_logs, t + 1 + l * 2)
                    own.done(dve.scalar_tensor_tensor(p, s, 0.0, p, ALU.max, ALU.add))
                    own.wait()
                    own.done(dve.tensor_tensor(p, p, rows_mask("strict"), ALU.mult))
                    own.wait()
                    for h in range(H2):
                        own.done(dve.tensor_tensor_scan(p[:, h, ::-1], mask["strict"][:, t, 0:n][:, ::-1], p[:, h, ::-1],
                                                        0.0, ALU.mult, ALU.add))
                    own.wait()
                    own.done(dve.tensor_tensor(p, s, p, ALU.subtract))
                    own.wait()
                    dve.tensor_tensor(p, p, rows_mask("strict_neg"), ALU.add).then_inc(l_shift, 1)
                    return
                if kind in ("A", "slc", "win"):
                    for h in range(H2):
                        own.done(dve.scalar_tensor_tensor(p[:, h, :], mask["dist"][:, t, 0:n],
                                                          (SLOPES_A if kind == "A" else SLOPES_C)[h], s[:, h, :],
                                                          ALU.mult, ALU.add))
                    if kind == "A":
                        own.wait()
                        own.done(dve.tensor_tensor(p, p, rows_mask("count"), ALU.add))
                elif kind == "B":
                    own.done(dve.tensor_tensor(p, s, rows_mask("causal"), ALU.add))
                else:
                    own.done(dve.tensor_tensor(p, s, c_mask[:, t, :, :], ALU.add))
                own.wait()
                if kind != "cmp":
                    dve.tensor_reduce(l_nb, p, AX.X, ALU.max, negate=True).then_inc(l_shift, 1)
                else:
                    own.done(dve.tensor_reduce(l_nb, p, AX.X, ALU.max, negate=True))
                    own.wait()
                    dve.tensor_scalar(l_nb, l_nb, 1e20, None, ALU.min).then_inc(l_shift, 1)

            def factors(g, kind, t):
                if kind == "D":
                    return None
                dve.wait_ge(l_exp, g + 1 + l * NG)
                if kind == "cmp":
                    own.done(dve.tensor_scalar(l_sum, l_sum, 1e-30, None, ALU.max))
                    own.wait()
                own.done(dve.reciprocal(l_rs, l_sum))
                own.wait()
                if kind in ("A", "B"):
                    return l_rs
                j = ("cmp", "slc", "win").index(kind)
                own.done(dve.tensor_tensor(l_co, l_rs, proj[:, t, CGT + j:CGT + 12:3], ALU.mult))
                own.wait()
                return l_co

            def output(g, kind, t, factor):
                br = {"A": 0, "B": 1, "cmp": 2, "slc": 2, "win": 2, "D": 3}[kind]
                y = y_tm[:, t, BW * br:BW * br + BW]
                y4 = y.rearrange("p (h n) -> p h n", h=4)
                gate = proj[:, t, (AG, BG, CG, DG)[br]:(AG, BG, CG, DG)[br] + BW]
                o = bank(7)[:, 0:BW]
                o4 = o.rearrange("p (h n) -> p h n", h=4)
                dve.wait_ge(l_pv, FIRST_ROUND[g + 1] + l * NR)
                if kind == "D":
                    dve.tensor_tensor(y, o, gate, ALU.mult).then_inc(l_out, 1)
                elif kind in ("A", "B"):
                    own.done(dve.tensor_tensor(y4, o4, bc(factor, [P, 4, HD]), ALU.mult))
                    own.wait()
                    dve.tensor_tensor(y, y, gate, ALU.mult).then_inc(l_out, 1)
                elif kind == "cmp":
                    dve.tensor_tensor(y4, o4, bc(factor, [P, 4, HD]), ALU.mult).then_inc(l_out, 1)
                else:
                    part = probs[g % 2][:, 0, :]
                    own.done(dve.tensor_tensor(part.rearrange("p (h n) -> p h n", h=4), o4,
                                               bc(factor, [P, 4, HD]), ALU.mult))
                    own.wait()
                    if kind == "slc":
                        dve.tensor_tensor(y, y, part, ALU.add).then_inc(l_out, 1)
                    else:
                        own.done(dve.tensor_tensor(y, y, part, ALU.add))
                        own.wait()
                        dve.tensor_tensor(y, y, gate, ALU.mult).then_inc(l_out, 1)

            for g, (kind, t) in enumerate(GROUPS_L):
                if t == 0:
                    prepare(kind)
                if g >= 2:
                    dve.wait_ge(l_turned, FIRST_ROUND[g - 1] + l * NR)
                arguments(g, kind, t)
                factor = factors(g, kind, t)
                if g == 0:
                    dve.wait_ge(gates_ready, 1 + l)
                if g >= 2:
                    dve.wait_ge(l_out, g - 1 + l * NG)
                output(g, kind, t, factor)
                feed(gate_tile(FILLER[g]))
            dve.wait_ge(l_out, NG + l * NG)
            dve.nop().then_inc(src_ready, 2)
            feed(gate_tile(14))
            feed(gate_tile(15))
            turn_dve(dve, k + 1, mid_hi, mid_lo, UNIT)
            for br in range(4):
                feed(W_BRANCH + br)
                for half in range(2):
                    g = BB + B_BRANCH + 2 * br + half
                    gate = gates[:, 2048 * br + 1024 * half:2048 * br + 1024 * half + 1024]
                    m, t_ = slot(0)[:, 1024 * half:1024 * half + 1024], slot(1)[:, 1024 * half:1024 * half + 1024]
                    dve.wait_ge(tile_used, TB + W_BRANCH + br + 1 + r)
                    dve.wait_ge(block_free[(BB + 15 - half) % 2], (BB + 15 - half) // 2 + 1 + rb)
                    own.wait()
                    dve.tensor_tensor(m if br == 0 else t_, pair(g), gate, ALU.mult).then_inc(block_free[g % 2], 1)
                    dve.wait_ge(block_free[g % 2], g // 2 + 1 + rb)
                    if br:
                        own.done(dve.tensor_tensor(m, m, t_, ALU.add))
            own.wait()
            dve.nop().then_inc(merged_ready, 1)
            dve.wait_ge(mid_hi_ready, l + 3)
            dve.tensor_tensor(act_lo[:, :, :], fm(0), act_hi[:, :, :].bitcast(f32), ALU.subtract)\
                .then_inc(mid_lo_ready, 1)
            for n in range(2):
                feed(W_OUT + n)
            for half in range(2):
                g = BB + B_LOUT + half
                dve.wait_ge(tile_used, TB + W_OUT + 2 * half + 2 + r)
                xs = x_tm[:, :, 512 * half:512 * half + 512]
                dve.tensor_tensor(xs, xs, pair(g).rearrange("p (t n) -> p t n", t=NT), ALU.add)\
                    .then_inc(block_free[g % 2], 1)
            return own

        def layer_sp(sp, l):
            r = l * L_TILES

            def one(name):
                return w[name][bass.ds(l, 1)]

            def rows4(m, k0, c0, n=512):
                return m[:, k0:k0 + 512, c0:c0 + n].rearrange("o (k p) n -> p (o k) n", p=P), n

            for i in range(W_GATE):
                j = i // 2
                load_tile(sp, TB + i, r, rows4(one("w_in_2"), 512 * (i % 2), 512 * j, min(512, PROJ2 - 512 * j)))

            def merge(n):
                m = one("w_merge_2")[:, n // 4]
                load_tile(sp, TB + gate_tile(n), r, rows4(m, 512 * (n % 2), 512 * (n // 2 % 2)))

            for n in range(8):
                merge(n)
            for half in range(2):
                src = one("nsa_w1")[:, :, SLOT * half:SLOT * half + SLOT].rearrange("o p (k n) -> p (o k) n", k=4)
                load_tile(sp, TB + W_CMP + half, r, (src, 512))
            for n in range(8, 16):
                merge(n)
            for br in range(4):
                load_tile(sp, TB + W_BRANCH + br, r,
                          (one("w_branch_2")[:, br].rearrange("o (k p) n -> p (o k) n", p=P), 512))
            for n in range(4):
                load_tile(sp, TB + W_OUT + n, r, rows4(one("w_out_2"), 512 * (n % 2), 512 * (n // 2)))

        gain_row = slot(4)[:, 0:D]

        def last_act(act):
            g0 = BB + (LAYERS - 1) * L_BLOCKS
            for g in (B_LOUT, B_LOUT + 1):
                block_read(act, g0 + g)
            for t in range(NT):
                nc.scalar.activation(tm(5)[:, t, :], x_tm[:, t, :], ACT.Square, accum_out=n_ss[:, t:t + 1])\
                    .then_inc(norm_ss, 1)
            act.wait_ge(norm_ms, LAYERS + 3)
            nc.scalar.activation(n_rt, n_ms, ACT.Sqrt).then_inc(norm_rt, 1)

        def last_dve(dve):
            k = LAYERS + 2
            dve.wait_ge(norm_ss, 2 * (k + 1))
            dve.tensor_scalar(n_ms, n_ss, 1.0 / D, EPS, ALU.mult, ALU.add).then_inc(norm_ms, 1)
            dve.wait_ge(norm_rt, k + 1)
            dve.reciprocal(n_rs, n_rt).then_inc(norm_rs, 1)
            dve.wait_ge(norm_rs, k + 1)
            dve.wait_ge(gain_in, 16)
            for t in range(NT):
                dve.scalar_tensor_tensor(xn[:, t, :], x_tm[:, t, :], n_rs[:, t:t + 1], gain_row, ALU.mult, ALU.mult)\
                    .then_inc(out_ready, 1)

        def last_sp(sp):
            for t in range(NT):
                sp.wait_ge(out_ready, t + 1)
                sp.dma_start(out[0][t * P:(t + 1) * P, :], xn[:, t, :]).then_inc(stored, 16)
            sp.wait_ge(stored, 16 * NT)

        @block.sync
        def _(sp):
            sp.dma_start(x_tm[:, :, :], w["x"][0].rearrange("(t p) d -> p t d", p=P)).then_inc(x_in, 16)
            for i in range(T_MOE):
                load_tile(sp, i)
            moe_sp(sp)
            with sp.Fori(0, LAYERS) as l:
                layer_sp(sp, l)
            last_sp(sp)

        @block.gpsimd
        def _(pool):
            pool.dma_start(extra[:, 0:128], w["cmp_masks"].rearrange("p t h n -> p (t h n)")).then_inc(mask_in, 16)
            pool.wait_ge(merged_ready, 1)
            pool.dma_start(mask_all, w["masks"].rearrange("p m t k -> p (m t k)")).then_inc(mask_in, 16)
            with pool.Fori(0, LAYERS) as l:
                for g in (BB - 2, BB - 1):
                    pool.wait_ge(block_free[g % 2], g // 2 + 1 + l * (L_BLOCKS // 2))
                flat = "o k n -> (o k) n"
                pool.dma_start(layer_par[:, :], w["layer_params"][bass.ds(l, 1)].rearrange(flat)).then_inc(layer_in, 16)
                up = w["mla_w_uq_2"][bass.ds(l, 1)]
                pool.dma_start(uq[:, 0, :], up[:, 0:P].rearrange(flat)).then_inc(layer_in, 16)
                pool.dma_start(uq[0:MQ - P, 1, :], up[:, P:MQ].rearrange(flat)).then_inc(layer_in, 16)
                pool.dma_start(ukv, w["mla_w_ukv_2"][bass.ds(l, 1)].rearrange(flat)).then_inc(layer_in, 16)
            for g in (B_LOUT, B_LOUT + 1):
                block_read(pool, BB + (LAYERS - 1) * L_BLOCKS + g)
            pool.dma_start(gain_row, w["final_gain"]).then_inc(gain_in, 16)

        @block.tensor
        def _(pe):
            first_pe(pe)
            moe_pe(pe)
            with pe.Fori(0, LAYERS) as l:
                layer_pe(pe, l)

        @block.vector
        def _(dve):
            own = first_dve(dve)
            moe_dve(dve, own)
            dve.wait_ge(mask_in, 32)
            with dve.Fori(0, LAYERS) as l:
                own = layer_dve(dve, l)
                assert own.n == OWN_DVE, own.n
            last_dve(dve)

        @block.scalar
        def _(act):
            act.dma_start(par[:, :], w["params"]).then_inc(par_in, 16)
            for m, name in enumerate(("lru_wa", "lru_wi")):
                act.dma_start(lru_w[:, m, :, :], w[name][0].rearrange("d c i o -> i (d c) o")).then_inc(lru_w_in, 16)
            first_act(act)
            moe_act(act)
            with act.Fori(0, LAYERS) as l:
                own = layer_act(act, l)
                assert own.n == OWN_ACT, own.n
            last_act(act)


DEVICE = ["x", "w_in", "lru_wa", "lru_wi", "w_lru_o", "w_attn_o", "w_out", "w_expert_gate", "w_expert_up",
          "w_expert_down", "w_in_2", "mla_w_uq_2", "mla_w_ukv_2", "w_branch_2", "w_merge_2", "w_out_2"]


def rotary(dim):
    pos = np.arange(SEQ, dtype=np.float32)
    inv = np.float32(10000.0) ** (-np.arange(0, dim, 2, dtype=np.float32) / np.float32(dim))
    ang = (pos[:, None] * inv[None, :]).astype(np.float32)
    lay = lambda a: a.reshape(NT, P, dim // 2).transpose(1, 0, 2).reshape(P, -1).astype(np.float32)
    return lay(np.cos(ang)), lay(np.sin(ang))


def masks():
    t, k = np.arange(SEQ)[:, None], np.arange(SEQ)[None, :]
    d = t - k
    count = (d <= 128).astype(int) + ((d % 4 == 0) & (d <= 512)) + ((d % 16 == 0) & (d <= 2048))
    seen = (d >= 0) & (count > 0)
    all_masks = [
        np.where(d >= 0, -d, NEG), np.where(d >= 0, 0.0, NEG),
        np.where(seen, np.log(np.maximum(count, 1)), NEG),
        (d > 0).astype(float), np.where(d > 0, 0.0, NEG),
    ]
    m = np.stack(all_masks).astype(np.float32)
    return np.ascontiguousarray(m.reshape(5, NT, P, SEQ).transpose(2, 0, 1, 3))


def cmp_masks():
    t = np.arange(SEQ)[:, None]
    end = (np.arange(NCP) * CMP_STRIDE + CMP_BLOCK - 1)[None, :]
    d = t - end
    ok = (d >= 0) & (np.arange(NCP)[None, :] < N_CMP)
    m = np.stack([np.where(ok, -s * d, NEG) for s in SLOPES_C]).astype(np.float32)
    return np.ascontiguousarray(m.reshape(H2, NT, P, NCP).transpose(2, 1, 0, 3))


def pack(inputs):
    cols = lambda a: np.ascontiguousarray(np.asarray(a).reshape(-1, P).T)
    rows = lambda a: np.tile(np.asarray(a).reshape(1, -1), (P, 1))
    cos, sin = rotary(SUB)
    mcos, msin = rotary(MR)
    i = inputs
    parts = {
        "ident": np.eye(P, dtype=np.float32), "g1": cols(i["norm1_gain"]), "g2": cols(i["norm2_gain"]),
        "qg": rows(i["q_norm_gain"]), "kg": rows(i["k_norm_gain"]),
        "lam": rows(np.concatenate([np.asarray(i[n]).ravel() for n in ("lambda_q1", "lambda_k1", "lambda_q2",
                                                                       "lambda_k2")])),
        "subln": cols(i["attn_subln_gain"]), "conv_w": cols(i["conv_w"]), "conv_b": cols(i["conv_b"]),
        "ba": cols(i["lru_ba"]), "bi": cols(i["lru_bi"]), "lru_lam": cols(i["lru_lambda"]),
        "bg": cols(i["b_gates"]),
        "router_b": rows(np.concatenate([np.asarray(i["b_group_router"]).ravel(),
                                         np.asarray(i["b_expert_router"]).ravel()])),
        "router_w": np.concatenate([np.asarray(i["w_group_router"])[0], np.asarray(i["w_expert_router"])[0]], axis=1)
                      .reshape(NC, P, 20).transpose(1, 0, 2).reshape(P, -1),
        "cos": cos, "sin": sin, "mcos": mcos, "msin": msin,
        "first": rows(np.arange(GROUPS, 0, -1).astype(np.float32)),
    }
    return beside([parts[n] for n in PARAMS])


def beside(parts):
    return np.ascontiguousarray(np.concatenate(parts, axis=1), dtype=np.float32)


def pack_layer(i, l):
    cols = lambda a: np.ascontiguousarray(np.asarray(a).reshape(-1, P).T)
    rows = lambda a: np.tile(np.asarray(a).reshape(1, -1), (P, 1))
    mq = np.zeros((P, 2), np.float32)
    g = np.asarray(i["mla_q_norm_2"])[l]
    mq[:, 0], mq[:MQ - P, 1] = g[:P], g[P:]
    b2k = np.zeros((P, 1), np.float32)
    b2k[:HD, 0] = np.asarray(i["nsa_b2_2"])[l, 0]
    parts = {
        "ng": cols(np.asarray(i["norm_g_2"])[l]), "mqg": mq, "mkvg": cols(np.asarray(i["mla_kv_norm_2"])[l]),
        "pos": np.asarray(i["nsa_pos_2"])[l].transpose(0, 2, 1).reshape(P, CMP_BLOCK),
        "b1": cols(np.asarray(i["nsa_b1_2"])[l]),
        "w2": np.asarray(i["nsa_w2_2"])[l].transpose(1, 0, 2).reshape(P, -1), "b2k": b2k,
        "b2v": rows(np.asarray(i["nsa_b2_2"])[l, 1]), "bm": cols(np.asarray(i["b_merge_2"])[l]),
    }
    return beside([parts[n] for n in LAYER_PARAMS])


def kernel(**inputs):
    import concourse.bacc as bacc
    from concourse.bass_utils import run_bass_kernel_spmd

    nc = bacc.Bacc("TRN2", target_bir_lowering=False, num_devices=1)
    arrays = {n: np.ascontiguousarray(inputs[n]) for n in DEVICE}
    w1 = np.asarray(inputs["nsa_w1_2"]).reshape(LAYERS, 2, CMP_BLOCK, HD, CMP_HID).transpose(0, 1, 3, 2, 4)
    arrays["nsa_w1"] = np.ascontiguousarray(w1.reshape(LAYERS, P, CMP_BLOCK * CMP_HID))
    arrays["layer_params"] = np.stack([pack_layer(inputs, l) for l in range(LAYERS)])
    arrays.update(params=pack(inputs), masks=masks(), cmp_masks=cmp_masks(),
                  final_gain=np.tile(np.asarray(inputs["final_norm_g_2"]).reshape(1, -1), (P, 1)))
    w = {n: nc.dram_tensor(f"in_{n}", a.shape, mybir.dt.from_np(a.dtype), kind="ExternalInput").ap()
         for n, a in arrays.items()}
    out = nc.dram_tensor("out", (1, SEQ, D), mybir.dt.float32, kind="ExternalOutput").ap()
    two_blocks(nc, w, out)
    r = run_bass_kernel_spmd(nc, [{f"in_{n}": a for n, a in arrays.items()}], core_ids=[0])
    return r.results[0]["out"]
```

```python
import math
from contextlib import ExitStack

import numpy as np

import concourse.bass as bass
from concourse import mybir

P = 128
SEQ = 256
NT = SEQ // P
D = 1024
NC = D // P
PROJ = 7168
HEADS = 8
SUB = 64
VD = 2 * SUB
CONV = 4
EXPERTS = 16
GROUPS = 4
PER_GROUP = EXPERTS // GROUPS
HIDDEN = 512
LAYERS = 2
PROJ2 = 3564
H2 = 4
HD = 64
BW = H2 * HD
MQ, MKV, MN, MR = 192, 128, 64, 32
MQK = MN + MR
CMP_BLOCK, CMP_STRIDE, CMP_HID = 32, 16, 128
N_CMP = (SEQ - CMP_BLOCK) // CMP_STRIDE + 1
NCP = 16
EPS = 1e-6
LAM_INIT = 0.8 - 0.6 * math.exp(-0.3 * 0)
NEG = -1e30
SLOT = 2048
AQ, AK, AV, AG = 0, 256, 512, 768
BCQ, BCKV, BKPE, BG = 1024, 1216, 1344, 1376
CQ, CKC, CKS, CVS, CKW, CVW, CGT, CG = 1632, 1888, 2016, 2080, 2144, 2208, 2272, 2284
DQ, DK, DV, DG = 2540, 2796, 3052, 3308


def param_table():
    widths = [("ident", P), ("g1", NC), ("g2", NC), ("qg", SUB), ("kg", SUB), ("lam", 4 * SUB), ("subln", 1),
              ("conv_w", CONV * NC), ("conv_b", NC), ("ba", 2 * NC), ("bi", 2 * NC), ("lru_lam", 2 * NC),
              ("bg", 2 * NC), ("router_b", 20), ("router_w", NC * 20), ("cos", NT * 32), ("sin", NT * 32),
              ("mcos", NT * 16), ("msin", NT * 16), ("first", GROUPS)]
    return offsets(widths)


def layer_param_table():
    return offsets([("ng", NC), ("mqg", 2), ("mkvg", 1), ("pos", CMP_BLOCK), ("b1", 2), ("w2", 2 * HD), ("b2k", 1),
                    ("b2v", HD), ("bm", 4 * NC)])


def offsets(widths):
    at, table = 0, {}
    for name, n in widths:
        table[name] = (at, n)
        at += n
    return table, at


PARAMS, N_PARAMS = param_table()
LAYER_PARAMS, N_LAYER_PARAMS = layer_param_table()
OWN_DVE, OWN_ACT = 102, 7
MASKS = ["dist", "causal", "count", "strict", "strict_neg"]
SLOPES = [2.0 ** (-8.0 * (i + 1) / 8) for i in range(8)]
SLOPES_A, SLOPES_C = SLOPES[0::2], SLOPES[1::2]


class Own:

    def __init__(self, eng, sem, base=0):
        self.eng, self.sem, self.base, self.n = eng, sem, base, 0

    def done(self, instruction):
        instruction.then_inc(self.sem, 1)
        self.n += 1
        return instruction

    def wait(self):
        if self.n:
            self.eng.wait_ge(self.sem, self.n + self.base)


def two_blocks(nc, w, out, dbg=None):
    f32, f32r = mybir.dt.float32, mybir.dt.float32r
    ALU, ACT, AX = mybir.AluOpType, mybir.ActivationFunctionType, mybir.AxisListType
    ctx = ExitStack()
    with ctx:
        def sb(name, shape, dt=f32):
            return ctx.enter_context(nc.sbuf_tensor(name, shape, dt))

        def sem(name):
            return ctx.enter_context(nc.semaphore(name))

        RAW_SLOTS, SPLIT_SLOTS = 4, 2
        raw = sb("weights_raw", [P, RAW_SLOTS, SLOT])
        whi = sb("weights_high", [P, SPLIT_SLOTS, SLOT], f32r)
        wlo = sb("weights_low", [P, SPLIT_SLOTS, SLOT], f32r)
        act_hi = sb("act_high", [P, NC, SEQ], f32r)
        act_lo = sb("act_low", [P, NC, SEQ], f32r)
        mid_hi = sb("mid_high", [P, NC, SEQ], f32r)
        mid_lo = sb("mid_low", [P, NC, SEQ], f32r)
        x_tm = sb("x_tokens", [P, NT, D])
        arena = sb("arena", [P, 12 * SLOT])
        par = sb("params", [P, N_PARAMS])
        tiny = sb("tiny", [P, 264])
        layer_par = sb("layer_params", [P, N_LAYER_PARAMS])
        extra = sb("extra", [P, 240])
        psum = ctx.enter_context(nc.psum_tensor("psum", [P, 8 * 512], f32))

        def slot(n, k=1):
            return arena[:, n * SLOT:(n + k) * SLOT]

        def fm(n):
            return slot(n).rearrange("p (c t) -> p c t", c=NC)

        def tm(n):
            return slot(n).rearrange("p (t n) -> p t n", t=NT)

        def prm(name, a=0, b=None):
            at, n = PARAMS[name]
            return par[:, at + a:at + (n if b is None else b)]

        def lpar(name, a=0, b=None):
            at, n = LAYER_PARAMS[name]
            return layer_par[:, at + a:at + (n if b is None else b)]

        def bank(b, n=1):
            return psum[:, b * 512:(b + n) * 512]

        ident = prm("ident")
        tiny_at = [0]

        def small(n):
            a = tiny_at[0]
            tiny_at[0] += n
            assert tiny_at[0] <= 264
            return tiny[:, a:a + n]

        raw_ready = [sem(f"raw_ready{s}") for s in range(RAW_SLOTS)]
        hi_ready = sem("hi_ready")
        lo_ready = sem("lo_ready")
        tile_used = sem("tile_used")
        branch_half = sem("branch_half")
        branch_added = sem("branch_added")
        block_free = [sem(f"block_free{p}") for p in range(2)]
        par_in = sem("params_in")
        x_in = sem("x_in")
        act_own, dve_own = sem("act_own"), sem("dve_own")
        norm_ss = sem("norm_sums")
        norm_ms = sem("norm_means")
        norm_rt = sem("norm_roots")
        norm_rs = sem("norm_scales")
        src_ready = sem("turn_source")
        turned = sem("turned")
        turned_hi = sem("turned_hi")
        turned_lo = sem("turned_lo")
        conv_ready = sem("conv_ready")
        lru_w_in = sem("lru_weights_in")
        lru_mm = sem("lru_products")
        lru_sig = sem("lru_sigmoids")
        lru_y = sem("lru_exponents")
        lru_ta = sem("lru_decay_and_root")
        lru_ix = sem("lru_gated_input")
        lru_scan = sem("lru_scans")
        lru_sp = sem("lru_softplus")
        y_sum = sem("y_lru_sum")
        mid_hi_ready = sem("mid_high_ready")
        mid_lo_ready = sem("mid_low_ready")
        roped = sem("qk_roped")
        qk_turned = sem("qk_turned")
        qk_copied = sem("qk_copied")
        lam_e = sem("lambda_exps")
        lam_in = sem("lambda_sums")
        a_scores = sem("a_scores")
        a_shift = sem("a_shift")
        a_exp = sem("a_exp")
        a_diff = sem("a_diff")
        a_turned = sem("a_turned")
        a_pt = sem("a_pt")
        a_pv = sem("a_pv")
        a_out = sem("a_out")
        o_sq = sem("o_squares")
        o_ms = sem("o_means")
        o_rt = sem("o_roots")
        merged_ready = sem("merged_ready")
        router_split = sem("router_split")
        router_mm = sem("router_products")
        route_exp = sem("route_exchange")
        mask_in, layer_in, gain_in = sem("masks_in"), sem("layer_params_in"), sem("gain_in")
        l_act_own, l_dve_own = sem("layer_act_own"), sem("layer_dve_own")
        prep_pe = sem("prepared_pe")
        prep_act = sem("prepared_act")
        prep_dve = sem("prepared_dve")
        gates_ready = sem("branch_gates")
        l_scores = sem("l_scores")
        l_logs = sem("l_logs")
        l_shift = sem("l_shift")
        l_exp = sem("l_exp")
        l_turned = sem("l_turned")
        l_copied = sem("l_copied")
        l_pv = sem("l_pv")
        l_out = sem("l_out")
        out_ready, stored = sem("out_ready"), sem("stored")
        hid_hi = sem("hidden_high")
        hid_lo = sem("hidden_low")

        tiles, blocks = [], []

        def k_major(m, k0, c0, n=512):
            return m[k0:k0 + 512, c0:c0 + n].rearrange("(k p) n -> p k n", p=P)

        def matrix(m, order, n_last=512):
            for j in order:
                n = n_last if j == order[-1] else 512
                for h in range(2):
                    tiles.append((k_major(m, 512 * h, 512 * j, n), n))

        T_IN = 0
        w_in = w["w_in"][0]
        matrix(w_in, [6, 7, 8, 9, 0, 1, 2, 3, 4, 5, 10, 11, 12, 13])
        T_LRUO = len(tiles)
        matrix(w["w_lru_o"][0], [0, 1])
        T_ATTNO = len(tiles)
        matrix(w["w_attn_o"][0], [0, 1])
        T_OUT = len(tiles)
        OUT_ORDER = [(0, 0), (1, 0), (0, 1), (1, 1)]
        tiles += [(k_major(w["w_out"][0], 512 * h, 512 * j), 512) for j, h in OUT_ORDER]
        T_MOE = len(tiles)

        def gate_tiles(m, e):
            return [(k_major(m[e], 512 * h, 0), 512) for h in range(2)]

        def down_tiles(e):
            return [(k_major(w["w_expert_down"][0][e], 0, 512 * h), 512) for h in range(2)]

        wg, wu = w["w_expert_gate"][0], w["w_expert_up"][0]
        tiles += gate_tiles(wg, 0) + gate_tiles(wu, 0)
        for e in range(1, EXPERTS):
            tiles += gate_tiles(wg, e) + down_tiles(e - 1) + gate_tiles(wu, e)
        tiles += down_tiles(EXPERTS - 1)
        T_LAYERS = len(tiles)
        T_STOP = T_LAYERS
        tiles += [(None, 512)] * 12 + [(None, PROJ2 - 6 * 512)] * 2 + [(None, 512)] * 28

        def raw_tile(i, n=512):
            return raw[:, i % RAW_SLOTS, 0:4 * n]

        def hi_tile(i, n=512):
            return whi[:, i % SPLIT_SLOTS, 0:4 * n]

        def lo_tile(i, n=512):
            return wlo[:, i % SPLIT_SLOTS, 0:4 * n]

        def pair(g):
            return bank(2 * (g % 2), 2)

        block = ctx.enter_context(nc.Block())

        def load_tile(sp, i, r=0, source=None):
            if i >= RAW_SLOTS:
                sp.wait_ge(lo_ready, i - RAW_SLOTS + 1 + r)
            src, n = source or tiles[i]
            sp.dma_start(raw_tile(i, n).rearrange("p (k n) -> p k n", k=src.shape[1]), src)\
                .then_inc(raw_ready[i % RAW_SLOTS], 16)

        def high(act, i, r=0):
            n = tiles[i][1]
            act.wait_ge(raw_ready[i % RAW_SLOTS], 16 * (i // RAW_SLOTS + 1) + r * (16 // RAW_SLOTS))
            if i >= SPLIT_SLOTS:
                act.wait_ge(tile_used, i - SPLIT_SLOTS + 1 + r)
            nc.scalar.activation(hi_tile(i, n), raw_tile(i, n), ACT.Copy).then_inc(hi_ready, 1)

        def low(dve, i, r=0):
            n = tiles[i][1]
            dve.wait_ge(hi_ready, i + 1 + r)
            dve.tensor_tensor(lo_tile(i, n), raw_tile(i, n), hi_tile(i, n).bitcast(f32), ALU.subtract)\
                .then_inc(lo_ready, 1)

        def block_read(eng, g):
            eng.wait_ge(block_free[g % 2], g // 2 + 1)

        n_ss, n_ms, n_rt, n_rs = small(4), small(2), small(2), small(2)
        xn = tm(11)

        def squares_act(act, half_ready):
            for half in range(2):
                half_ready(half)
                for t in range(NT):
                    cols = slice(512 * half, 512 * half + 512)
                    at = 2 * half + t
                    nc.scalar.activation(tm(5)[:, t, cols], x_tm[:, t, cols], ACT.Square, accum_out=n_ss[:, at:at + 1])\
                        .then_inc(norm_ss, 1)

        def root_act(act, k):
            act.wait_ge(norm_ms, k + 1)
            nc.scalar.activation(n_rt, n_ms, ACT.Sqrt, scale=1.0 / D).then_inc(norm_rt, 1)

        def norm_act(act, k, half_ready):
            squares_act(act, half_ready)
            root_act(act, k)
            act.wait_ge(norm_rs, k + 1)
            nc.scalar.activation(xn[:, 0, :], x_tm[:, 0, :], ACT.Copy, scale=n_rs[:, 0:1]).then_inc(src_ready, 1)

        def scales_dve(dve, k):
            dve.wait_ge(norm_ss, (k + 1) * 4)
            dve.scalar_tensor_tensor(n_ms, n_ss[:, 0:2], EPS * D, n_ss[:, 2:4], ALU.add, ALU.add).then_inc(norm_ms, 1)
            dve.wait_ge(norm_rt, k + 1)
            dve.reciprocal(n_rs, n_rt).then_inc(norm_rs, 1)
            dve.wait_ge(norm_rs, k + 1)

        def norm_dve(dve, k):
            scales_dve(dve, k)
            dve.tensor_scalar(xn[:, 1, :], x_tm[:, 1, :], n_rs[:, 1:2], None, ALU.mult).then_inc(src_ready, 1)

        def turn_pe(pe, k, src):
            pe.wait_ge(src_ready, (k + 1) * 2)
            if not isinstance(k, int) or k:
                pe.wait_ge(turned_lo, k * 4)
            for b in range(4):
                for cc in range(2):
                    for t in range(NT):
                        c = 2 * b + cc
                        last = pe.transpose(bank(4 + b)[:, cc * SEQ + t * P:cc * SEQ + (t + 1) * P],
                                            src[:, t, c * P:(c + 1) * P], ident)
                last.then_inc(turned, 1)

        def turn_act(act, k, hi, gain):
            for b in range(4):
                act.wait_ge(turned, k * 4 + b + 1)
                for cc in range(2):
                    last = nc.scalar.activation(hi[:, 2 * b + cc, :], bank(4 + b)[:, cc * SEQ:(cc + 1) * SEQ],
                                                ACT.Copy, scale=gain(2 * b + cc))
                last.then_inc(turned_hi, 1)

        def turn_dve(dve, k, hi, lo, gain, halfway=None):
            for b in range(4):
                if b == 2 and halfway:
                    halfway()
                dve.wait_ge(turned_hi, k * 4 + b + 1)
                for cc in range(2):
                    c = 2 * b + cc
                    last = dve.scalar_tensor_tensor(lo[:, c, :], bank(4 + b)[:, cc * SEQ:(cc + 1) * SEQ], gain(c),
                                                    hi[:, c, :].bitcast(f32), ALU.mult, ALU.subtract)
                last.then_inc(turned_lo, 1)

        def passes(a_hi, a_lo, i, n):
            whole_hi, whole_lo = hi_tile(i, n), lo_tile(i, n)
            return ((a_hi, whole_hi), (a_hi, whole_lo), (a_lo, whole_hi))

        def start_tile(pe, i, g, first, r=0, rb=0):
            pe.wait_ge(lo_ready, i + 1 + r)
            if first and g >= 2:
                pe.wait_ge(block_free[g % 2], g // 2 + rb)

        def token_tile(pe, i, g, h, a_hi, a_lo, r=0, rb=0, halves=2):
            n = tiles[i][1]
            start_tile(pe, i, g, h == 0, r, rb)
            for k in range(4):
                for t in range(NT):
                    for q, (a, b) in enumerate(passes(a_hi, a_lo, i, n)):
                        last = pe.matmul(pair(g)[:, t * 512:t * 512 + n], a[:, 4 * h + k, t * P:(t + 1) * P],
                                         b[:, k * n:(k + 1) * n], start=(h == 0 and k == 0 and q == 0),
                                         stop=(h == halves - 1 and k == 3 and q == 2))
            last.then_inc(tile_used, 1)

        def feature_tile(pe, i, g, h, a_hi, a_lo, r=0, rb=0, s0=0, s1=4):
            if s0 == 0:
                start_tile(pe, i, g, h == 0, r, rb)
            for s in range(s0, s1):
                for k in range(4):
                    for q, (a, b) in enumerate(passes(a_hi, a_lo, i, 512)):
                        last = pe.matmul(pair(g)[:, s * SEQ:(s + 1) * SEQ], b[:, k * 512 + s * P:k * 512 + (s + 1) * P],
                                         a[:, 4 * h + k, :], start=(h == 0 and k == 0 and q == 0 and s % 2 == 0),
                                         stop=(h == 1 and k == 3 and q == 2), skip_group_check=True)
            if s1 == 4:
                last.then_inc(tile_used, 1)

        neg_lam, lam_s, lam_x = small(1), small(2), small(2)
        a_sum, a_rs, a_nb, a_c1 = small(8), small(4), small(4), small(2)
        ssq, rsq = small(64), small(64)
        g_o = small(1)
        sp_z, sp_s, sp_s2, sp_p = small(16), small(16), small(16), small(16)
        G1 = lambda c: prm("g1", c, c + 1)
        G2 = lambda c: prm("g2", c, c + 1)
        rope_t = slot(1)[:, 0:512].rearrange("p (z j t n) -> p z j t n", z=2, j=4, t=NT)
        qT, kT = fm(0), fm(1)
        v_tm, o_tm = tm(6), tm(4)
        r_fm, i_fm, y_fm = fm(3), fm(4), fm(7)
        h_fm = [fm(5), fm(0)]
        merged = fm(5)
        lru_w = slot(8, 2).rearrange("p (m g n) -> p m g n", m=2, g=2 * NC)

        def bc(a, shape):
            return a.unsqueeze(2).broadcast_to(shape)

        GA = 8

        def first_pe(pe):
            pe.wait_ge(par_in, 16)
            turn_pe(pe, 0, xn)
            for i in range(0, 8):
                if i < 2:
                    pe.wait_ge(turned_lo, 2 * i + 2)
                feature_tile(pe, i, i // 2, i % 2, act_hi, act_lo)
            for d in range(2):
                for i in range(8 + 0 if d == 0 else 16 - 4, 12 if d == 0 else 20):
                    token_tile(pe, i, i // 2, i % 2, act_hi, act_lo)
                if d == 0:
                    pe.wait_ge(conv_ready, 1)
                    pe.wait_ge(lru_w_in, 32)
                for c in range(NC):
                    n = d * NC + c
                    if n >= 4:
                        pe.wait_ge(lru_sig, 2 * (n - 3))
                    for m in range(2):
                        last = pe.matmul(bank(4 + c % 4)[:, m * SEQ:(m + 1) * SEQ], lru_w[:, m, d * NC + c, :],
                                         fm(2)[:, c, :], start=True, stop=True)
                    last.then_inc(lru_mm, 1)
            for i in range(20, 28):
                feature_tile(pe, i, i // 2, i % 2, act_hi, act_lo)
            pe.wait_ge(mid_lo_ready, 1)
            for i in range(28, 32):
                feature_tile(pe, i, i // 2, i % 2, mid_hi, mid_lo)
            pe.wait_ge(lru_sig, 32)
            for z in range(2):
                pe.wait_ge(roped, z + 1)
                for b in range(4):
                    if z:
                        pe.wait_ge(qk_copied, b + 1)
                    for hh in range(2):
                        for t in range(NT):
                            last = pe.transpose(bank(4 + b)[:, hh * SEQ + t * P:hh * SEQ + (t + 1) * P],
                                                tm(2 + z)[:, t, (2 * b + hh) * P:(2 * b + hh + 1) * P], ident)
                    last.then_inc(qk_turned, 1)

            def scores(g):
                hp, t = g // 2, g % 2
                if g:
                    pe.wait_ge(a_exp, 4 * g)
                else:
                    pe.wait_ge(qk_copied, 8)
                for hh in range(2):
                    for c in range(2):
                        rows = slice(c * SUB, (c + 1) * SUB)
                        last = pe.matmul(bank(4 + c)[:, hh * SEQ:(hh + 1) * SEQ],
                                         qT[rows, 2 * hp + hh, t * P:(t + 1) * P], kT[rows, 2 * hp + hh, :],
                                         start=True, stop=True)
                last.then_inc(a_scores, 1)

            scores(0)
            for g in range(GA):
                hp = g // 2
                p = slot(7)[:, (g % 2) * 1024:(g % 2 + 1) * 1024].rearrange("p (s k) -> p s k", s=4)
                pt = slot(3)[:, (g % 2) * 512:(g % 2 + 1) * 512].rearrange("p (s k) -> p s k", s=4)
                if g + 1 < GA:
                    scores(g + 1)
                pe.wait_ge(a_diff, g + 1)
                if g:
                    pe.wait_ge(a_pt, g)
                for hh in range(2):
                    for kt in range(NT):
                        last = pe.transpose(bank(6)[:, (2 * hh + kt) * P:(2 * hh + kt + 1) * P],
                                            p[:, hh, kt * P:(kt + 1) * P], ident)
                last.then_inc(a_turned, 1)
                pe.wait_ge(a_pt, g + 1)
                if g:
                    pe.wait_ge(a_out, g)
                for hh in range(2):
                    for kt in range(NT):
                        last = pe.matmul(bank(7)[:, hh * VD:(hh + 1) * VD], pt[:, 2 * hh + kt, :],
                                         v_tm[:, kt, (2 * hp + hh) * VD:(2 * hp + hh + 1) * VD],
                                         start=(kt == 0), stop=(kt == 1))
                last.then_inc(a_pv, 1)
            pe.wait_ge(a_out, GA)
            turn_pe(pe, 1, tm(7))
            for i in range(32, 36):
                if i < 34:
                    pe.wait_ge(turned_lo, 4 + 2 * (i - 32) + 2)
                feature_tile(pe, i, i // 2, i % 2, act_hi, act_lo)
            for n, (j, h) in enumerate(OUT_ORDER):
                if j == 0:
                    pe.wait_ge(mid_lo_ready, 2 + h)
                token_tile(pe, T_OUT + n, T_OUT // 2 + j, h, mid_hi, mid_lo)

        def first_act(act):
            own = Own(act, act_own)
            act.wait_ge(x_in, 16)
            norm_act(act, 0, lambda half: None)
            high(act, 0)
            act.wait_ge(par_in, 16)
            turn_act(act, 0, act_hi, G1)
            high(act, 1)

            def read_block(g):
                act.wait_ge(tile_used, 2 * g + 2)
                src = pair(g)
                if g < 2:
                    nc.scalar.activation(slot(0)[:, g * 1024:(g + 1) * 1024], src, ACT.Copy)\
                        .then_inc(block_free[g % 2], 1)
                elif g < 4:
                    nc.scalar.activation(slot(1)[:, (g - 2) * 1024:(g - 1) * 1024], src, ACT.Gelu_apprx_tanh)\
                        .then_inc(block_free[g % 2], 1)
                elif g < 10:
                    dst = [tm(10), tm(11), tm(6)][(g - 4) // 2]
                    n = (g % 2) * 512
                    nc.scalar.activation(dst[:, :, n:n + 512], src.rearrange("p (t n) -> p t n", t=NT), ACT.Copy)\
                        .then_inc(block_free[g % 2], 1)
                else:
                    if g == 10:
                        act.wait_ge(lru_mm, 16)
                    for s in range(4):
                        c = 4 * (g - 10) + s
                        last = nc.scalar.activation(slot(8, 2)[:, c * SEQ:(c + 1) * SEQ], src[:, s * SEQ:(s + 1) * SEQ],
                                                    ACT.Sigmoid, bias=prm("bg", c, c + 1))
                    last.then_inc(block_free[g % 2], 1)

            def sigmoids(d):
                if d:
                    act.wait_ge(lru_scan, 1)
                for c in range(NC):
                    act.wait_ge(lru_mm, d * NC + c + 1)
                    for m, (dst, b) in enumerate(((r_fm, "ba"), (i_fm, "bi"))):
                        nc.scalar.activation(dst[:, c, :], bank(4 + c % 4)[:, m * SEQ:(m + 1) * SEQ], ACT.Sigmoid,
                                             bias=prm(b, d * NC + c, d * NC + c + 1)).then_inc(lru_sig, 1)

            def decay(d):
                act.wait_ge(lru_y, d + 1)
                own.done(nc.scalar.activation(r_fm, y_fm, ACT.Exp, scale=-1.0))
                own.wait()
                own.done(nc.scalar.activation(y_fm, y_fm, ACT.Tanh, scale=0.5))
                own.wait()
                nc.scalar.activation(y_fm, y_fm, ACT.Sqrt).then_inc(lru_ta, 1)

            for i in range(28):
                high(act, i + 2)
                if i % 2:
                    read_block(i // 2)
                if i == 11:
                    sigmoids(0)
                if i == 19:
                    sigmoids(1)
                if i == 0:
                    act.wait_ge(lru_sp, 1)
                    nc.scalar.activation(sp_z, sp_z, ACT.Exp, scale=-1.0).then_inc(lru_sp, 1)
                if i == 13:
                    decay(0)
                if i == 21:
                    decay(1)
            act.wait_ge(y_sum, 1)
            nc.scalar.activation(mid_hi[:, :, :], fm(5), ACT.Copy).then_inc(mid_hi_ready, 1)
            act.wait_ge(lam_in, 1)
            nc.scalar.activation(lam_x, lam_s, ACT.Exp).then_inc(lam_e, 1)
            act.wait_ge(o_ms, 1)
            nc.scalar.activation(ssq, ssq, ACT.Sqrt).then_inc(o_rt, 1)
            for i in range(30, 34):
                high(act, i)
            for n in range(8):
                act.wait_ge(qk_turned, n + 1)
                dst = (qT if n < 4 else kT)[:, 2 * (n % 4):2 * (n % 4) + 2, :]
                nc.scalar.activation(dst, bank(4 + n % 4).rearrange("p (h t) -> p h t", h=2), ACT.Copy,
                                     scale=(SUB ** -0.5 if n < 4 else 1.0)).then_inc(qk_copied, 1)

            for g in range(GA):
                p = slot(7)[:, (g % 2) * 1024:(g % 2 + 1) * 1024].rearrange("p (s k) -> p s k", s=4)
                act.wait_ge(a_shift, g + 1)
                if g >= 2:
                    act.wait_ge(a_turned, g - 1)
                for s in range(4):
                    nc.scalar.activation(p[:, s, :], bank(4, 2)[:, s * SEQ:(s + 1) * SEQ], ACT.Exp,
                                         bias=a_nb[:, s:s + 1], accum_out=a_sum[:, 4 * (g % 2) + s:4 * (g % 2) + s + 1])\
                        .then_inc(a_exp, 1)
                act.wait_ge(a_turned, g + 1)
                if g >= 2:
                    act.wait_ge(a_pv, g - 1)
                nc.scalar.activation(slot(3)[:, (g % 2) * 512:(g % 2 + 1) * 512], bank(6), ACT.Copy)\
                    .then_inc(a_pt, 1)
            act.wait_ge(o_ms, 2)
            nc.scalar.activation(ssq[:, 0:16], ssq[:, 0:16], ACT.Sqrt).then_inc(o_rt, 1)
            turn_act(act, 1, act_hi, lambda c: g_o)
            for i in range(32, 36):
                if i >= 34 - 2:
                    high(act, i + 2)
            for half in range(2):
                act.wait_ge(merged_ready, half + 1)
                cs4 = slice(4 * half, 4 * half + 4)
                nc.scalar.activation(mid_hi[:, cs4, :], merged[:, cs4, :], ACT.Copy).then_inc(mid_hi_ready, 1)
            for i in range(38, 41):
                high(act, i)

        def first_dve(dve):
            own = Own(dve, dve_own)
            norm_dve(dve, 0)
            feed = [0]

            def lows(n):
                for _ in range(n):
                    low(dve, feed[0])
                    feed[0] += 1

            lows(1)
            dve.wait_ge(par_in, 16)
            turn_dve(dve, 0, act_hi, act_lo, G1)
            lows(1)
            lam = prm("lru_lam")
            dve.scalar_tensor_tensor(sp_z, lam, -1.0, lam, ALU.mult, ALU.max).then_inc(lru_sp, 1)
            lows(2)
            dve.wait_ge(lru_sp, 2)
            own.done(dve.tensor_scalar(sp_s, sp_z, 2.0, None, ALU.add))
            own.wait()
            own.done(dve.reciprocal(sp_s, sp_s))
            own.wait()
            own.done(dve.tensor_tensor(sp_s, sp_s, sp_z, ALU.mult))
            own.wait()
            own.done(dve.tensor_tensor(sp_s2, sp_s, sp_s, ALU.mult))
            own.wait()
            own.done(dve.tensor_scalar(sp_p, sp_s2, 1.0 / 15, None, ALU.mult))
            for k in (13, 11, 9, 7, 5, 3):
                own.wait()
                own.done(dve.scalar_tensor_tensor(sp_p, sp_p, 1.0 / k, sp_s2, ALU.add, ALU.mult))
            own.wait()
            own.done(dve.scalar_tensor_tensor(sp_p, sp_p, 1.0, sp_s, ALU.add, ALU.mult))
            own.done(dve.tensor_scalar(sp_z, lam, -8.0, 0.0, ALU.mult, ALU.max))
            own.wait()
            own.done(dve.scalar_tensor_tensor(sp_z, sp_p, 16.0, sp_z, ALU.mult, ALU.add))

            lows(2)
            for g in range(2):
                block_read(dve, g)
            lx, xr = fm(0), fm(2)
            for c in range(NC):
                cw = lambda j: prm("conv_w", j * NC + c, j * NC + c + 1)
                own.done(dve.tensor_scalar(xr[:, c, :], lx[:, c, :], cw(1), prm("conv_b", c, c + 1),
                                           ALU.mult, ALU.add))
            for n, (j, a, b) in enumerate(((0, 1, 0), (2, 0, 1), (3, 0, 2))):
                lows(1)
                own.wait()
                m = SEQ - max(a, b)
                for c in range(NC):
                    cw = prm("conv_w", j * NC + c, j * NC + c + 1)
                    last = own.done(dve.scalar_tensor_tensor(xr[:, c, a:a + m], lx[:, c, b:b + m], cw,
                                                             xr[:, c, a:a + m], ALU.mult, ALU.add))
            own.wait()
            dve.nop().then_inc(conv_ready, 1)
            lows(14 - feed[0])

            def lru(d, middle, late):
                dve.wait_ge(lru_sig, 16 * (d + 1))
                dve.tensor_tensor(y_fm, r_fm, bc(sp_z[:, d * NC:(d + 1) * NC], [P, NC, SEQ]), ALU.mult)\
                    .then_inc(lru_y, 1)
                lows(middle)
                dve.wait_ge(lru_ta, d + 1)
                own.done(dve.scalar_tensor_tensor(h_fm[d], r_fm, 1.0, y_fm, ALU.add, ALU.mult))
                lows(1)
                own.wait()
                dve.wait_ge(lru_ix, d + 1)
                own.done(dve.tensor_tensor(i_fm, i_fm, h_fm[d], ALU.mult))
                own.wait()
                step = 1 if d == 0 else -1
                for c in range(NC):
                    if c == 4:
                        lows(late)
                    last = dve.tensor_tensor_scan(h_fm[d][:, c, ::step], r_fm[:, c, ::step], i_fm[:, c, ::step], 0.0,
                                                  ALU.mult, ALU.add)
                last.then_inc(lru_scan, 1)

            lru(0, 2, 2)
            lows(23 - feed[0])
            lru(1, 1, 1)
            dve.wait_ge(lru_scan, 2)
            for g in (2, 3):
                block_read(dve, g)
            own.done(dve.tensor_tensor(fm(5), fm(5), fm(0), ALU.add))
            lows(28 - feed[0])
            own.wait()
            dve.tensor_tensor(fm(5), fm(5), fm(1), ALU.mult).then_inc(y_sum, 1)
            dve.wait_ge(y_sum, 1)
            lows(30 - feed[0])

            for g in range(4, 8):
                block_read(dve, g)
            for z in range(2):
                sq = slot(7)
                own.wait()
                own.done(dve.tensor_tensor(sq, slot(10 + z), slot(10 + z), ALU.mult))
                own.wait()
                own.done(dve.tensor_reduce(ssq[:, 32 * z:32 * z + 32], sq.rearrange("p (m n) -> p m n", n=SUB),
                                           AX.X, ALU.add))
            dve.wait_ge(mid_hi_ready, 1)
            dve.tensor_tensor(mid_lo[:, :, :], fm(5), mid_hi[:, :, :].bitcast(f32), ALU.subtract)\
                .then_inc(mid_lo_ready, 1)
            for m in range(2):
                a, b = prm("lam", 2 * m * SUB, (2 * m + 1) * SUB), prm("lam", (2 * m + 1) * SUB, (2 * m + 2) * SUB)
                own.done(dve.tensor_tensor_reduce(out=slot(2)[:, m * SUB:(m + 1) * SUB], in0=a, in1=b, scale=1.0,
                                                  scalar=0.0, op0=ALU.mult, op1=ALU.add,
                                                  accum_out=lam_s[:, m:m + 1]))
            own.wait()
            dve.nop().then_inc(lam_in, 1)
            own.wait()
            dve.tensor_scalar(ssq, ssq, 1.0 / SUB, EPS, ALU.mult, ALU.add).then_inc(o_ms, 1)
            own.done(dve.tensor_scalar(g_o, prm("subln"), 1.0 - LAM_INIT, None, ALU.mult))
            for z, gain in enumerate(("qg", "kg")):
                g = prm(gain)
                for j, (tab, half) in enumerate((("cos", 0), ("sin", 1), ("sin", 0), ("cos", 1))):
                    own.done(dve.tensor_tensor(
                        rope_t[:, z, j, :, :], prm(tab).rearrange("p (t n) -> p t n", t=NT),
                        g[:, 32 * half:32 * half + 32].unsqueeze(1).broadcast_to([P, NT, 32]), ALU.mult))
            dve.wait_ge(lam_e, 1)
            own.done(dve.scalar_tensor_tensor(neg_lam, lam_x[:, 1:2], -LAM_INIT, lam_x[:, 0:1], ALU.add,
                                              ALU.subtract))
            dve.wait_ge(o_rt, 1)
            own.done(dve.reciprocal(rsq, ssq))
            for z in range(2):
                own.wait()
                xs = slot(4).rearrange("p (t h n) -> p t h n", t=NT, h=16)
                own.done(dve.tensor_tensor(slot(4).rearrange("p (m n) -> p m n", n=SUB),
                                           slot(10 + z).rearrange("p (m n) -> p m n", n=SUB),
                                           bc(rsq[:, 32 * z:32 * z + 32], [P, 32, SUB]), ALU.mult))
                own.wait()
                x1, x2 = xs[:, :, :, 0:32], xs[:, :, :, 32:64]
                t1 = slot(7)[:, 0:1024].rearrange("p (t h n) -> p t h n", t=NT, h=16)
                t2 = slot(7)[:, 1024:2048].rearrange("p (t h n) -> p t h n", t=NT, h=16)
                dst = slot(2 + z).rearrange("p (t h n) -> p t h n", t=NT, h=16)

                def table(j):
                    return rope_t[:, z, j, :, :].unsqueeze(2).broadcast_to([P, NT, 16, 32])

                for half, op in ((0, ALU.subtract), (1, ALU.add)):
                    if half or z:
                        own.wait()
                    own.done(dve.tensor_tensor(t1, x1, table(2 * half), ALU.mult))
                    own.done(dve.tensor_tensor(t2, x2, table(2 * half + 1), ALU.mult))
                    own.wait()
                    last = own.done(dve.tensor_tensor(dst[:, :, :, 32 * half:32 * half + 32], t1, t2, op))
                own.wait()
                dve.nop().then_inc(roped, 1)
                lows(1)
                if z == 1:
                    lows(34 - feed[0])
                for g in ((14,) if z == 0 else (15,)):
                    gate_product(dve, g)

            def shift(g):
                dve.wait_ge(a_scores, g + 1)
                if g:
                    dve.wait_ge(a_exp, 4 * g)
                dve.tensor_reduce(a_nb, bank(4, 2).rearrange("p (s k) -> p s k", s=4), AX.X, ALU.max, negate=True)\
                    .then_inc(a_shift, 1)

            def output(g):
                hp, t = g // 2, g % 2
                dve.wait_ge(a_pv, g + 1)
                dve.tensor_tensor(o_tm[:, t, 2 * hp * VD:(2 * hp + 2) * VD].rearrange("p (h n) -> p h n", h=2),
                                  bank(7)[:, 0:2 * VD].rearrange("p (h n) -> p h n", h=2),
                                  bc(a_rs[:, 0:2], [P, 2, VD]), ALU.mult).then_inc(a_out, 1)

            for g in range(GA):
                p = slot(7)[:, (g % 2) * 1024:(g % 2 + 1) * 1024].rearrange("p (s k) -> p s k", s=4)
                shift(g)
                if g:
                    output(g - 1)
                    dve.wait_ge(a_out, g)
                dve.wait_ge(a_exp, 4 * (g + 1))
                s = a_sum[:, 4 * (g % 2):4 * (g % 2) + 4]
                own.done(dve.reciprocal(a_rs, s))
                own.wait()
                own.done(dve.scalar_tensor_tensor(a_c1, s[:, 0:2], neg_lam, a_rs[:, 2:4], ALU.mult, ALU.mult))
                own.wait()
                for hh in range(2):
                    last = dve.scalar_tensor_tensor(p[:, hh, :], p[:, 2 + hh, :], a_c1[:, hh:hh + 1],
                                                    p[:, hh, :], ALU.mult, ALU.add)
                last.then_inc(a_diff, 1)
            output(GA - 1)
            dve.wait_ge(a_out, GA)
            own.done(dve.tensor_tensor(slot(7), slot(4), slot(4), ALU.mult))
            own.wait()
            own.done(dve.tensor_reduce(ssq[:, 0:16], slot(7).rearrange("p (m n) -> p m n", n=VD), AX.X, ALU.add))
            own.wait()
            dve.tensor_scalar(ssq[:, 0:16], ssq[:, 0:16], 1.0 / VD, EPS, ALU.mult, ALU.add).then_inc(o_ms, 1)
            dve.wait_ge(o_rt, 2)
            own.done(dve.reciprocal(rsq[:, 0:16], ssq[:, 0:16]))
            own.wait()
            dve.tensor_tensor(slot(7).rearrange("p (m n) -> p m n", n=VD), slot(4).rearrange("p (m n) -> p m n", n=VD),
                              bc(rsq[:, 0:16], [P, 16, VD]), ALU.mult).then_inc(src_ready, 2)
            turn_dve(dve, 1, act_hi, act_lo, lambda c: g_o)
            lows(2)
            gate_product(dve, 16)
            lows(2)
            gate_product(dve, 17)
            for half in range(2):
                dve.wait_ge(mid_hi_ready, 2 + half)
                cs4 = slice(4 * half, 4 * half + 4)
                dve.tensor_tensor(mid_lo[:, cs4, :], merged[:, cs4, :], mid_hi[:, cs4, :].bitcast(f32), ALU.subtract)\
                    .then_inc(mid_lo_ready, 1)
            lows(2)
            add_block(dve, 18, T_OUT + 3, 0)
            lows(1)
            add_block(dve, 19, T_OUT + 4, 1)

            return own

        def gate_product(dve, g):
            dve.wait_ge(tile_used, 2 * g + 2)
            n = (g % 2) * 1024
            m = slot(5)[:, n:n + 1024]
            if g < 16:
                block_read(dve, 12 + g % 2)
                dve.tensor_tensor(m, pair(g), slot(9)[:, n:n + 1024], ALU.mult).then_inc(block_free[g % 2], 1)
            else:
                t = slot(7)[:, n:n + 1024]
                dve.tensor_tensor(t, pair(g), slot(8)[:, n:n + 1024], ALU.mult).then_inc(block_free[g % 2], 1)
                block_read(dve, g)
                dve.tensor_tensor(m, m, t, ALU.add).then_inc(merged_ready, 1)

        def add_block(dve, g, used, half):
            dve.wait_ge(tile_used, used)
            xs = x_tm[:, :, 512 * half:512 * half + 512]
            dve.tensor_tensor(xs, xs, pair(g).rearrange("p (t n) -> p t n", t=NT), ALU.add)\
                .then_inc(block_free[g % 2], 1)

        PAIRS = (EXPERTS - 2) // 2
        M0, B0 = T_MOE, T_MOE // 2
        PER_PAIR, BLOCKS_PAIR = 12, 8
        logits = slot(0)[:, 0:40].rearrange("p (t n) -> p t n", t=NT)
        cs = slot(1)[:, 0:NT * EXPERTS]
        silu_g, hid = slot(2)[:, 0:1024], slot(2)[:, 1024:2048]
        router_wh, router_wl = mid_hi[:, 7, 0:NC * 20], mid_lo[:, 7, 0:NC * 20]
        scratch_at = [64]

        def scratch(*dims):
            n = int(np.prod(dims))
            a = slot(0)[:, scratch_at[0]:scratch_at[0] + n]
            scratch_at[0] += n
            if len(dims) == 1:
                return a
            names = "abcd"[:len(dims)]
            return a.rearrange(f"p ({' '.join(names)}) -> p {' '.join(names)}", **dict(zip(names, dims)))

        g_dif, g_exp = scratch(2, 4), scratch(2, 4)
        e_dif, e_exp = scratch(2), scratch(2)

        def tiles_of(e):
            return M0 + 4 + 6 * (e - 1), B0 + 2 + 4 * (e - 1)

        def down_tile(pe, i, g, e, r=0, rb=0):
            start_tile(pe, i, g, True, r, rb)
            half = 4 * (e % 2)
            for k in range(4):
                for t in range(NT):
                    for q, (a, b) in enumerate(passes(mid_hi, mid_lo, i, 512)):
                        last = pe.matmul(pair(g)[:, t * 512:(t + 1) * 512], a[:, half + k, t * P:(t + 1) * P],
                                         b[:, k * 512:(k + 1) * 512], start=(k == 0 and q == 0),
                                         stop=(k == 3 and q == 2))
            last.then_inc(tile_used, 1)

        def expert_pe(pe, e, r=0, rb=0, re=0):
            i, g = tiles_of(e)
            for h in range(2):
                feature_tile(pe, i + h, g, h, act_hi, act_lo, r, rb)
            pe.wait_ge(hid_lo, e + re)
            for n in range(2):
                down_tile(pe, i + 2 + n, g + 1 + n, e - 1, r, rb)
            for h in range(2):
                feature_tile(pe, i + 4 + h, g + 3, h, act_hi, act_lo, r, rb)

        def moe_pe(pe):
            turn_pe(pe, 2, xn)
            pe.wait_ge(turned_lo, 10)
            feature_tile(pe, M0, B0, 0, act_hi, act_lo)
            pe.wait_ge(turned_lo, 12)
            pe.wait_ge(router_split, 2)
            for t in range(NT):
                for k in range(NC):
                    for q, (a, b) in enumerate(((act_hi, router_wh), (act_hi, router_wl), (act_lo, router_wh))):
                        last = pe.matmul(bank(4)[:, t * 20:t * 20 + 20], a[:, k, t * P:(t + 1) * P],
                                         b[:, k * 20:(k + 1) * 20], start=(k == 0 and q == 0),
                                         stop=(k == NC - 1 and q == 2))
            last.then_inc(router_mm, 1)
            for i in range(1, 4):
                feature_tile(pe, M0 + i, B0 + i // 2, i % 2, act_hi, act_lo)
            with pe.Fori(0, PAIRS) as j:
                for e in (1, 2):
                    expert_pe(pe, e, j * PER_PAIR, j * (BLOCKS_PAIR // 2), j * 2)
            expert_pe(pe, EXPERTS - 1)
            pe.wait_ge(hid_lo, EXPERTS)
            i, g = tiles_of(EXPERTS)
            for n in range(2):
                down_tile(pe, i + n, g + n, EXPERTS - 1)

        def expert_high(act, e, g, used, r=0, rb=0):
            act.wait_ge(block_free[g % 2], g // 2 + 1 + rb)
            nc.scalar.activation(mid_hi[:, 4 * (e % 2):4 * (e % 2) + 4, :], hid.rearrange("p (k t) -> p k t", k=4),
                                 ACT.Copy).then_inc(hid_hi, 1)

        def expert_silu(act, i, g, r=0, rb=0, re=0, e=0):
            act.wait_ge(tile_used, i + 2 + r)
            if e:
                act.wait_ge(hid_lo, e + re)
            nc.scalar.activation(silu_g, pair(g), ACT.Silu).then_inc(block_free[g % 2], 1)

        def expert_act(act, e, r=0, rb=0, re=0):
            i, g = tiles_of(e)
            for n in range(6):
                if i + n + 2 < T_STOP:
                    high(act, i + n + 2, r)
                if n == 1:
                    expert_silu(act, i, g, r, rb, re, e)
                if n == 5:
                    expert_high(act, e, g + 3, i + 6, r, rb)

        def moe_act(act):
            def half_of_x(half):
                if half:
                    high(act, M0 + 1)
                block_read(act, 18 + half)

            norm_act(act, 1, half_of_x)
            nc.scalar.activation(router_wh, prm("router_w"), ACT.Copy).then_inc(router_split, 1)
            turn_act(act, 2, act_hi, G2)
            for n in range(4):
                high(act, M0 + n + 2)
                if n == 0:
                    act.wait_ge(route_exp, 1)
                    nc.scalar.activation(g_exp, g_dif, ACT.Exp).then_inc(route_exp, 1)
                if n == 1:
                    expert_silu(act, M0, B0)
                if n == 2:
                    act.wait_ge(route_exp, 3)
                    nc.scalar.activation(e_exp, e_dif, ACT.Exp).then_inc(route_exp, 1)
                if n == 3:
                    expert_high(act, 0, B0 + 1, M0 + 4)
            with act.Fori(0, PAIRS) as j:
                for e in (1, 2):
                    expert_act(act, e, j * PER_PAIR, j * (BLOCKS_PAIR // 2), j * 2)
            expert_act(act, EXPERTS - 1)
            for n in range(2):
                i = tiles_of(EXPERTS)[0] + n
                if i + 2 < T_STOP:
                    high(act, i + 2)

        def expert_hidden(dve, e, i, g, g_gate, r=0, rb=0, re=0):
            dve.wait_ge(tile_used, i + r)
            dve.wait_ge(block_free[g_gate % 2], g_gate // 2 + 1 + rb)
            dve.tensor_tensor(hid, pair(g), silu_g, ALU.mult).then_inc(block_free[g % 2], 1)
            dve.wait_ge(hid_hi, e + 1 + re)
            h = 4 * (e % 2)
            dve.tensor_tensor(mid_lo[:, h:h + 4, :], hid.rearrange("p (k t) -> p k t", k=4),
                              mid_hi[:, h:h + 4, :].bitcast(f32), ALU.subtract).then_inc(hid_lo, 1)

        def expert_add(dve, e, n, i, g, before, r=0, rb=0, re=0):
            dve.wait_ge(tile_used, i + 1 + r)
            dve.wait_ge(block_free[before % 2], before // 2 + 1 + rb)
            for t in range(NT):
                xs = x_tm[:, t, 512 * n:512 * n + 512]
                c = cs[:, t * EXPERTS + e:t * EXPERTS + e + 1] if isinstance(re, int) else \
                    cs[:, bass.ds(re + (t * EXPERTS + e), 1)]
                last = dve.scalar_tensor_tensor(xs, pair(g)[:, t * 512:(t + 1) * 512], c, xs, ALU.mult, ALU.add)
            last.then_inc(block_free[g % 2], 1)

        def expert_dve(dve, e, r=0, rb=0, re=0):
            i, g = tiles_of(e)
            for n in range(6):
                if i + n + 2 < T_STOP:
                    low(dve, i + n + 2, r)
                if n in (2, 3):
                    expert_add(dve, e - 1, n - 2, i + n, g + n - 1, g + n - 5, r, rb, re)
                if n == 5:
                    expert_hidden(dve, e, i + 6, g + 3, g, r, rb, re)

        def first_match(dve, own, values, best, out4):
            tie, top = scratch(2, 4), scratch(2)
            own.done(dve.tensor_tensor(tie, values, bc(best, [P, NT, 4]), ALU.is_equal))
            own.wait()
            own.done(dve.tensor_tensor(tie, tie, prm("first").unsqueeze(1).broadcast_to([P, NT, 4]), ALU.mult))
            own.wait()
            own.done(dve.tensor_reduce(top, tie, AX.X, ALU.max))
            own.wait()
            own.done(dve.tensor_tensor(out4, tie, bc(top, [P, NT, 4]), ALU.is_equal))
            own.wait()

        def route(dve, own, between):
            g_max, g_one, g_sum = scratch(2), scratch(2, 4), scratch(2)
            dve.wait_ge(router_mm, 1)
            own.done(dve.tensor_tensor(logits, bank(4)[:, 0:40].rearrange("p (t n) -> p t n", t=NT),
                                       prm("router_b").unsqueeze(1).broadcast_to([P, NT, 20]), ALU.add))
            own.wait()
            gl = logits[:, :, 0:4]
            own.done(dve.tensor_reduce(g_max, gl, AX.X, ALU.max))
            own.wait()
            dve.tensor_tensor(g_dif, gl, bc(g_max, [P, NT, 4]), ALU.subtract).then_inc(route_exp, 1)
            first_match(dve, own, gl, g_max, g_one)
            between(1)
            mix, es = scratch(2, 4, 4), scratch(2, 4)
            own.done(dve.tensor_tensor(mix, logits[:, :, 4:20].rearrange("p t (g e) -> p t e g", g=4),
                                       g_one.unsqueeze(2).broadcast_to([P, NT, 4, 4]), ALU.mult))
            own.wait()
            own.done(dve.tensor_reduce(es, mix, AX.X, ALU.add))
            own.wait()
            m1, m2, one1, one2, es2 = scratch(2), scratch(2), scratch(2, 4), scratch(2, 4), scratch(2, 4)
            own.done(dve.tensor_reduce(m1, es, AX.X, ALU.max))
            own.wait()
            first_match(dve, own, es, m1, one1)
            own.done(dve.scalar_tensor_tensor(es2, one1, NEG, es, ALU.mult, ALU.add))
            own.wait()
            own.done(dve.tensor_reduce(m2, es2, AX.X, ALU.max))
            own.wait()
            dve.wait_ge(route_exp, 2)
            dve.tensor_tensor(e_dif, m2, m1, ALU.subtract).then_inc(route_exp, 1)
            first_match(dve, own, es2, m2, one2)
            own.done(dve.tensor_reduce(g_sum, g_exp, AX.X, ALU.add))
            between(2)
            w1, w2, cw, cw2 = scratch(2), scratch(2), scratch(2, 4), scratch(2, 4)
            own.wait()
            dve.wait_ge(route_exp, 4)
            own.done(dve.scalar_tensor_tensor(w1, e_exp, 1.0, g_sum, ALU.add, ALU.mult))
            own.wait()
            own.done(dve.reciprocal(w1, w1))
            own.wait()
            own.done(dve.tensor_tensor(w2, w1, e_exp, ALU.mult))
            own.done(dve.tensor_tensor(cw, one1, bc(w1, [P, NT, 4]), ALU.mult))
            own.wait()
            own.done(dve.tensor_tensor(cw2, one2, bc(w2, [P, NT, 4]), ALU.mult))
            own.wait()
            own.done(dve.tensor_tensor(cw, cw, cw2, ALU.add))
            own.wait()
            own.done(dve.tensor_tensor(cs.rearrange("p (t g e) -> p t g e", t=NT, g=4), bc3(g_one),
                                       cw.unsqueeze(2).broadcast_to([P, NT, 4, 4]), ALU.mult))
            own.wait()

        def bc3(a):
            return a.unsqueeze(3).broadcast_to([P, NT, 4, 4])

        def moe_dve(dve, own):
            norm_dve(dve, 1)
            dve.wait_ge(router_split, 1)
            dve.tensor_tensor(router_wl, prm("router_w"), router_wh.bitcast(f32), ALU.subtract)\
                .then_inc(router_split, 1)
            turn_dve(dve, 2, act_hi, act_lo, G2, lambda: low(dve, M0 + 1))
            at = [M0 + 2]

            def between(n):
                for _ in range(n):
                    low(dve, at[0])
                    at[0] += 1

            between(1)
            route(dve, own, between)
            assert at[0] == M0 + 6
            expert_hidden(dve, 0, M0 + 4, B0 + 1, B0)
            with dve.Fori(0, PAIRS) as j:
                for e in (1, 2):
                    expert_dve(dve, e, j * PER_PAIR, j * (BLOCKS_PAIR // 2), j * 2)
            expert_dve(dve, EXPERTS - 1)
            i, g = tiles_of(EXPERTS)
            for n in range(2):
                if i + n + 2 < T_STOP:
                    low(dve, i + n + 2)
                expert_add(dve, EXPERTS - 1, n, i + n, g + n, g + n - 3)

        def moe_sp(sp):
            for i in range(M0, M0 + 4):
                load_tile(sp, i)
            with sp.Fori(0, PAIRS) as j:
                for e in (1, 2):
                    i = tiles_of(e)[0]
                    for n in range(6):
                        m = (w["w_expert_gate"], w["w_expert_down"], w["w_expert_up"])[n // 2][0]
                        one = m[bass.ds(j * 2 + (e - 1 if n in (2, 3) else e), 1)]
                        if n in (2, 3):
                            src = one[:, :, 512 * (n - 2):512 * (n - 2) + 512]
                        else:
                            src = one[:, 512 * (n % 2):512 * (n % 2) + 512, :]
                        load_tile(sp, i + n, j * PER_PAIR, (src.rearrange("o (k p) n -> p (o k) n", p=P), 512))
            for i in range(tiles_of(EXPERTS - 1)[0], T_LAYERS):
                load_tile(sp, i)

        L_TILES, L_BLOCKS = 40, 26
        W_GATE, W_CMP, W_BRANCH, W_OUT = 14, 23, 32, 36
        EARLY_A = 12
        GATES_FIRST = W_CMP - W_GATE
        B_GATE, B_BRANCH, B_LOUT = 8, 16, 24
        TB, BB = T_LAYERS, 84

        def gate_tile(n):
            return W_GATE + n if n < GATES_FIRST else W_CMP + 2 + n - GATES_FIRST

        KINDS = ["A", "D", "B", "cmp", "slc", "win"]
        GROUPS_L = [(kind, t) for kind in KINDS for t in range(NT)]
        NG = len(GROUPS_L)
        PREPARED = [t == 0 and kind not in ("slc", "win") for kind, t in GROUPS_L]
        ROUNDS = [t + 1 if kind != "cmp" else 1 for kind, t in GROUPS_L]
        FIRST_ROUND = [sum(ROUNDS[:g]) for g in range(NG + 1)]
        NR = FIRST_ROUND[NG]
        FILLER = [0, 1, 2, 3, 6, 7, 10, 11, 12, 13, 14, 15]

        proj = arena[:, 0:NT * PROJ2].rearrange("p (t n) -> p t n", t=NT)
        kTs = arena[:, 7168:8192].rearrange("p (h t) -> p h t", h=4)
        gates = slot(4, 4)
        y_tm = tm(8)
        mask_at = 9 * SLOT
        mask_all = arena[:, mask_at:mask_at + 5 * 512]
        mask = {m: arena[:, mask_at + 512 * n:mask_at + 512 * n + 512].rearrange("p (t k) -> p t k", t=NT)
                for n, m in enumerate(MASKS)}
        pTs = arena[:, mask_at + 2560:mask_at + 3072]
        qTs = arena[:, mask_at + 3072:mask_at + 4096].rearrange("p (h t) -> p h t", h=4)
        uq = slot(7)[:, 0:768].rearrange("p (k n) -> p k n", k=2)
        ukv = slot(7)[:, 768:1280]
        probs = [slot(11)[:, 1024 * b:1024 * b + 1024].rearrange("p (h k) -> p h k", h=4) for b in range(2)]
        c_mask = extra[:, 0:128].rearrange("p (t h n) -> p t h n", t=NT, h=4)
        blk_hi, blk_lo = (m[:, 0:4, :].rearrange("p c t -> p (c t)") for m in (mid_hi, mid_lo))
        hid_tm = slot(11)[:, 256:256 + CMP_HID]
        hidT = extra[:, 128:160].rearrange("p (v n) -> p v n", v=2)
        kcT = extra[0:HD, 160:176]
        vcmp = extra[0:NCP, 176:240]
        l_nb, l_sum, l_rs, l_co = small(4), small(4), small(4), small(4)
        m_ss, m_ms, m_rt, m_rs = small(4), small(4), small(4), small(4)
        NGAIN = lambda c: lpar("ng", c, c + 1)
        UNIT = lambda c: 1.0

        def rows_of(kind):
            return MQK if kind == "B" else HD

        def keys_of(kind, t, h):
            n = (t + 1) * P
            if kind == "cmp":
                return kcT
            if kind in ("slc", "win"):
                return kTs[0:HD, 0 if kind == "slc" else 1, 0:n]
            return kTs[0:rows_of(kind), h, 0:n]

        def values_of(kind, kt, h):
            if kind == "cmp":
                return vcmp
            if kind == "B":
                return y_tm[:, kt, 512 + HD * h:512 + HD * h + HD]
            at = {"A": AV + HD * h, "D": DV + HD * h, "slc": CVS, "win": CVW}[kind]
            return proj[:, kt, at:at + HD]

        def layer_pe(pe, l):
            r, rb = l * L_TILES, l * (L_BLOCKS // 2)
            k = l * 2 + 3
            turn_pe(pe, k, xn)

            def projection(i):
                token_tile(pe, TB + i, BB + i // 2, i % 2, act_hi, act_lo, r, rb)

            for i in range(EARLY_A):
                if i < 2:
                    pe.wait_ge(turned_lo, k * 4 + 2 * i + 2)
                projection(i)

            def filler(n, s0=0, s1=4):
                feature_tile(pe, TB + gate_tile(n), BB + B_GATE + n // 2, n % 2, act_hi, act_lo, r, rb, s0, s1)

            def turn_heads(b, srcs, width):
                for h, src in enumerate(srcs):
                    for t in range(NT):
                        last = pe.transpose(bank(b)[0:width, h * SEQ + t * P:h * SEQ + (t + 1) * P], src(t), ident)
                return last

            def heads(at, width=HD, n=4):
                return [lambda t, h=h: proj[:, t, at + width * h:at + width * (h + 1)] for h in range(n)]

            def prepare(kind):
                if kind in ("A", "D"):
                    q, kk, n = (AQ, AK, 0) if kind == "A" else (DQ, DK, 1)
                    if kind == "A":
                        pe.wait_ge(turned_lo, k * 4 + 4)
                        pe.wait_ge(block_free[BB % 2], BB // 2 + 1 + rb)
                    else:
                        pe.wait_ge(l_out, 2 + l * NG)
                    pe.transpose(bank(4)[:, 0:P], ident, ident)
                    for b, srcs in enumerate((heads(q)[0:2], heads(q)[2:4], heads(kk)[0:2], heads(kk)[2:4])):
                        last = turn_heads(4 + b, srcs, HD)
                    last.then_inc(prep_pe, 1)
                    if kind == "A":
                        for i in range(EARLY_A, W_GATE):
                            projection(i)
                        for g in (6, 7):
                            pe.wait_ge(block_free[(BB + g) % 2], (BB + g) // 2 + 1 + rb)
                    pe.wait_ge(prep_act, n + 1 + l * 13)
                    pe.wait_ge(prep_dve, n + 1 + l * 9)
                elif kind == "B":
                    pe.wait_ge(l_out, 4 + l * NG)
                    pe.wait_ge(prep_dve, 4 + l * 9)
                    stage = slot(11)[:, 0:640].rearrange("p (t n) -> p t n", t=NT)
                    for t in range(NT):
                        cols = slice(t * P, (t + 1) * P)
                        pe.transpose(bank(4)[:, cols], stage[:, t, 0:P], ident)
                        pe.transpose(bank(4)[0:MQ - P, SEQ + t * P:SEQ + (t + 1) * P], stage[:, t, P:MQ], ident)
                        last = pe.transpose(bank(5)[:, cols], stage[:, t, MQ:MQ + MKV], ident)
                    last.then_inc(prep_pe, 1)
                    filler(4)
                    pe.wait_ge(prep_act, 5 + l * 13)
                    pe.wait_ge(layer_in, 64 + l * 64)
                    cT = slot(11)[:, 1024:1792].rearrange("p (k t) -> p k t", k=3)
                    for t in range(NT):
                        cols = slice(t * P, (t + 1) * P)
                        pe.matmul(bank(6 + t)[:, 0:384], cT[:, 0, cols], uq[:, 0, :], start=True, stop=False)
                        pe.matmul(bank(6 + t)[:, 0:384], cT[0:MQ - P, 1, cols], uq[0:MQ - P, 1, :],
                                  start=False, stop=True)
                        last = pe.matmul(bank(4 + t), cT[:, 2, cols], ukv, start=True, stop=True)
                    last.then_inc(prep_pe, 1)
                    filler(5)
                    pe.wait_ge(prep_act, 7 + l * 13)
                    pe.wait_ge(prep_dve, 5 + l * 9)
                    q, kk = heads(0, MQK), heads(384, MQK)
                    for b, srcs in enumerate((q[0:2], q[2:4], kk[0:2], kk[2:4])):
                        last = turn_heads(4 + b, srcs, MQK)
                    last.then_inc(prep_pe, 1)
                    pe.wait_ge(prep_act, 8 + l * 13)
                    pe.wait_ge(prep_dve, 6 + l * 9)
                elif kind == "cmp":
                    pe.wait_ge(l_out, 6 + l * NG)
                    for t in range(NT):
                        pe.transpose(bank(4)[:, t * P:(t + 1) * P], proj[:, t, CKC:CKC + P], ident)
                    turn_heads(5, heads(CQ)[0:2], HD)
                    turn_heads(6, heads(CQ)[2:4], HD)
                    turn_heads(7, [lambda t: proj[:, t, CKS:CKS + HD], lambda t: proj[:, t, CKW:CKW + HD]], HD)\
                        .then_inc(prep_pe, 1)
                    filler(8)
                    pe.wait_ge(prep_act, 10 + l * 13)
                    pe.wait_ge(prep_dve, 8 + l * 9)
                    for half in range(2):
                        i = TB + W_CMP + half
                        pe.wait_ge(lo_ready, i + 1 + r)
                        for n in range(16):
                            pos = 16 * half + n
                            cols = slice(2 * NCP * pos, 2 * NCP * (pos + 1))
                            for q, (a, b) in enumerate(passes(blk_hi, blk_lo, i, 512)):
                                last = pe.matmul(bank(4)[0:2 * NCP, 0:CMP_HID], a[:, cols], b[:, n * P:(n + 1) * P],
                                                 start=(pos == 0 and q == 0), stop=(pos == 31 and q == 2))
                        last.then_inc(tile_used, 1)
                    filler(9)
                    pe.wait_ge(prep_act, 11 + l * 13)
                    pe.transpose(bank(5)[:, 0:P], hid_tm, ident).then_inc(prep_pe, 1)
                    pe.wait_ge(prep_act, 12 + l * 13)
                    pe.matmul(bank(6)[0:HD, 0:NCP], lpar("w2", 0, HD), hidT[:, 0, :], start=True, stop=True)
                    pe.matmul(bank(7)[0:NCP, 0:HD], hidT[:, 1, :], lpar("w2", HD, 2 * HD), start=True, stop=True)\
                        .then_inc(prep_pe, 1)
                    pe.wait_ge(prep_act, 13 + l * 13)
                    pe.wait_ge(prep_dve, 9 + l * 9)

            def scores(g):
                kind, t = GROUPS_L[g]
                n = NCP if kind == "cmp" else (t + 1) * P
                for h in range(H2):
                    last = pe.matmul(bank(4 + h // 2)[:, (h % 2) * SEQ:(h % 2) * SEQ + n],
                                     qTs[0:rows_of(kind), h, t * P:(t + 1) * P], keys_of(kind, t, h),
                                     start=True, stop=True)
                last.then_inc(l_scores, 1)

            prepare("A")
            for g, (kind, t) in enumerate(GROUPS_L):
                if PREPARED[g]:
                    if kind != "A":
                        prepare(kind)
                    scores(g)
                parts = [3 if PREPARED[g] and ROUNDS[g] == 1 else 2]
                parts += [4] if ROUNDS[g] == 1 else [3, 4]
                filler(FILLER[g], 0, parts[0])
                if g + 1 < NG and not PREPARED[g + 1]:
                    pe.wait_ge(l_shift, g + 1 + l * NG)
                    scores(g + 1)
                pe.wait_ge(l_exp, g + 1 + l * NG)
                per = H2 // ROUNDS[g]
                kts = 1 if kind == "cmp" else t + 1
                for rd in range(ROUNDS[g]):
                    m = FIRST_ROUND[g] + rd
                    keys = NCP if kind == "cmp" else P
                    if m:
                        pe.wait_ge(l_copied, m + l * NR)
                    for hh in range(per):
                        for kt in range(kts):
                            last = pe.transpose(bank(6)[0:keys, (hh * kts + kt) * P:(hh * kts + kt + 1) * P],
                                                probs[g % 2][:, rd * per + hh, kt * P:kt * P + keys], ident)
                    last.then_inc(l_turned, 1)
                    filler(FILLER[g], parts[rd], parts[rd + 1])
                    pe.wait_ge(l_copied, m + 1 + l * NR)
                    if rd == 0 and g:
                        pe.wait_ge(l_out, g + l * NG)
                    for hh in range(per):
                        h = rd * per + hh
                        for kt in range(kts):
                            last = pe.matmul(bank(7)[:, HD * h:HD * h + HD],
                                             pTs[0:keys, (hh * kts + kt) * P:(hh * kts + kt + 1) * P],
                                             values_of(kind, kt, h), start=(kt == 0), stop=(kt == kts - 1))
                    last.then_inc(l_pv, 1)
            turn_pe(pe, k + 1, y_tm)
            for br in range(4):
                pe.wait_ge(turned_lo, k * 4 + 4 + br + 1)
                i = TB + W_BRANCH + br
                for half in range(2):
                    g = BB + B_BRANCH + 2 * br + half
                    start_tile(pe, i, g, True, r, rb)
                    for s in range(4):
                        at = half * 512 + s * P
                        for kc in range(2):
                            for q, (a, b) in enumerate(passes(mid_hi, mid_lo, i, 512)):
                                last = pe.matmul(pair(g)[:, s * SEQ:(s + 1) * SEQ], b[:, kc * D + at:kc * D + at + P],
                                                 a[:, 2 * br + kc, :], start=(kc == 0 and q == 0 and s % 2 == 0),
                                                 stop=(kc == 1 and q == 2), skip_group_check=True)
                    last.then_inc(tile_used if half else branch_half, 1)
            for n, (j, h) in enumerate(OUT_ORDER):
                if j == 0:
                    pe.wait_ge(mid_lo_ready, 2 * l + 4 + h)
                token_tile(pe, TB + W_OUT + n, BB + B_LOUT + j, h, act_hi, act_lo, r, rb)

        def layer_act(act, l):
            own = Own(act, l_act_own, l * OWN_ACT)
            r, rb = l * L_TILES, l * (L_BLOCKS // 2)
            k = l * 2 + 3

            def feed(n):
                high(act, TB + n + 2, r)

            def feed_gate(n):
                feed(gate_tile(n))
                if n % 2:
                    g = BB + B_GATE + n // 2
                    act.wait_ge(tile_used, TB + gate_tile(n) + 1 + r)
                    for s in range(4):
                        c = 4 * (n // 2) + s
                        last = nc.scalar.activation(gates[:, c * SEQ:(c + 1) * SEQ], pair(g)[:, s * SEQ:(s + 1) * SEQ],
                                                    ACT.Sigmoid, bias=lpar("bm", c, c + 1))
                    last.then_inc(block_free[g % 2], 1)

            high(act, TB, r)
            def half_of_x(half):
                if half:
                    high(act, TB + 1, r)
                act.wait_ge(block_free[half], (BB - 2) // 2 + 1 + rb)

            norm_act(act, l + 2, half_of_x)
            act.wait_ge(layer_in, 64 + l * 64)
            turn_act(act, k, act_hi, NGAIN)
            def take_queries(kind, n, b=4):
                act.wait_ge(prep_pe, n + l * 8)
                w_ = rows_of(kind)
                return nc.scalar.activation(qTs[0:w_, :, :], bank(b, 2)[0:w_, :].rearrange("p (h t) -> p h t", h=4),
                                            ACT.Copy, scale=float(w_) ** -0.5)

            def silu(at):
                return nc.scalar.activation(proj[:, :, at:at + BW], proj[:, :, at:at + BW], ACT.Silu)

            for i in range(W_GATE):
                feed(i)
                if i == EARLY_A:
                    take_queries("A", 1).then_inc(prep_act, 1)
                if i == 10:
                    for g in (3, 4):
                        act.wait_ge(block_free[(BB + g) % 2], (BB + g) // 2 + 1 + rb)
                    for at in (AG, BG, CG):
                        silu(at)
                    nc.scalar.activation(proj[:, :, CGT:CGT + 12], proj[:, :, CGT:CGT + 12], ACT.Sigmoid)\
                        .then_inc(gates_ready, 1)
                if i % 2:
                    g = i // 2
                    n = min(512, PROJ2 - 512 * g)
                    act.wait_ge(tile_used, TB + i + 1 + r)
                    src = pair(BB + g).rearrange("p (t n) -> p t n", t=NT)[:, :, 0:n]
                    nc.scalar.activation(proj[:, :, 512 * g:512 * g + n], src, ACT.Copy)\
                        .then_inc(block_free[(BB + g) % 2], 1)
            act.nop().then_inc(block_free[(BB + 7) % 2], 1)
            def prepare(kind):
                if kind == "D":
                    take_queries(kind, 2).then_inc(prep_act, 1)
                    g = BB + 6
                    act.wait_ge(block_free[g % 2], g // 2 + 1 + rb)
                    silu(DG).then_inc(gates_ready, 1)
                elif kind == "B":
                    act.wait_ge(l_turned, FIRST_ROUND[3] + l * NR)
                    for n, (at, w_) in enumerate(((BCQ, MQ), (BCKV, MKV))):
                        for t in range(NT):
                            last = nc.scalar.activation(slot(11)[:, 0:w_], proj[:, t, at:at + w_], ACT.Square,
                                                        accum_out=m_ss[:, 2 * n + t:2 * n + t + 1])
                            if (n, t) != (1, 1):
                                own.done(last)
                                own.wait()
                    last.then_inc(prep_act, 1)
                    act.wait_ge(prep_dve, 3 + l * 9)
                    nc.scalar.activation(m_rt, m_ms, ACT.Sqrt).then_inc(prep_act, 1)
                    act.wait_ge(prep_pe, 3 + l * 8)
                    cT = slot(11)[:, 1024:1792].rearrange("p (k t) -> p k t", k=3)
                    nc.scalar.activation(cT[:, 0, :], bank(4)[:, 0:SEQ], ACT.Copy, scale=lpar("mqg", 0, 1))
                    nc.scalar.activation(cT[0:MQ - P, 1, :], bank(4)[0:MQ - P, SEQ:2 * SEQ], ACT.Copy,
                                         scale=lpar("mqg", 1, 2)[0:MQ - P])
                    nc.scalar.activation(cT[:, 2, :], bank(5)[:, 0:SEQ], ACT.Copy, scale=lpar("mkvg", 0, 1))\
                        .then_inc(prep_act, 1)
                    feed_gate(4)
                    act.wait_ge(prep_pe, 4 + l * 8)
                    nc.scalar.activation(proj[:, :, 0:384], bank(6, 2).rearrange("p (t n) -> p t n", t=NT)[:, :, 0:384],
                                         ACT.Copy).then_inc(prep_act, 1)
                    kv = bank(4, 2).rearrange("p (t h n) -> p t h n", t=NT, h=4)
                    nc.scalar.activation(proj[:, :, 384:768].rearrange("p t (h n) -> p t h n", h=4)[:, :, :, 0:MN],
                                         kv[:, :, :, 0:MN], ACT.Copy)
                    nc.scalar.activation(y_tm[:, :, 512:768].rearrange("p t (h n) -> p t h n", h=4),
                                         kv[:, :, :, MN:MN + HD], ACT.Copy).then_inc(prep_act, 1)
                    feed_gate(5)
                    take_queries(kind, 5).then_inc(prep_act, 1)
                elif kind == "cmp":
                    take_queries(kind, 6, 5)
                    nc.scalar.activation(kTs[0:HD, 0:2, :], bank(7)[0:HD, :].rearrange("p (h t) -> p h t", h=2),
                                         ACT.Copy).then_inc(prep_act, 1)
                    act.wait_ge(prep_dve, 7 + l * 9)
                    nc.scalar.activation(blk_hi, slot(11)[:, 1024:2048], ACT.Copy).then_inc(prep_act, 1)
                    feed_gate(8)
                    feed(W_CMP)
                    act.wait_ge(tile_used, TB + W_CMP + 2 + r)
                    nc.scalar.activation(hid_tm[0:2 * NCP], bank(4)[0:2 * NCP, 0:CMP_HID], ACT.Copy)\
                        .then_inc(prep_act, 1)
                    feed(W_CMP + 1)
                    act.wait_ge(prep_pe, 7 + l * 8)
                    for v in range(2):
                        last = nc.scalar.activation(hidT[:, v, :], bank(5)[:, NCP * v:NCP * v + NCP],
                                                    ACT.Gelu_apprx_tanh, bias=lpar("b1", v, v + 1))
                    last.then_inc(prep_act, 1)
                    act.wait_ge(prep_pe, 8 + l * 8)
                    nc.scalar.activation(kcT, bank(6)[0:HD, 0:NCP], ACT.Identity, bias=lpar("b2k", 0, 1)[0:HD])\
                        .then_inc(prep_act, 1)
                    feed_gate(9)

            for g, (kind, t) in enumerate(GROUPS_L):
                if PREPARED[g]:
                    prepare(kind)
                n = NCP if kind == "cmp" else (t + 1) * P
                p = probs[g % 2][:, :, 0:n]
                s = bank(4, 2).rearrange("p (h k) -> p h k", h=4)[:, :, 0:n]
                if kind == "D":
                    act.wait_ge(l_scores, g + 1 + l * NG)
                    own.done(nc.scalar.activation(p, s, ACT.Abs))
                    own.wait()
                    own.done(nc.scalar.activation(p, p, ACT.Exp, scale=-1.0))
                    own.wait()
                    nc.scalar.activation(p, p, ACT.Ln, bias=1.0).then_inc(l_logs, 1)
                    act.wait_ge(l_shift, g + 1 + l * NG)
                    nc.scalar.activation(p, p, ACT.Exp).then_inc(l_exp, 1)
                else:
                    act.wait_ge(l_shift, g + 1 + l * NG)
                    for h in range(H2):
                        last = nc.scalar.activation(p[:, h, :], p[:, h, :], ACT.Exp, bias=l_nb[:, h:h + 1],
                                                    accum_out=l_sum[:, h:h + 1])
                    last.then_inc(l_exp, 1)
                for rd in range(ROUNDS[g]):
                    m = FIRST_ROUND[g] + rd
                    act.wait_ge(l_turned, m + 1 + l * NR)
                    act.wait_ge(l_pv, m + l * NR) if m else None
                    keys = NCP if kind == "cmp" else P
                    nc.scalar.activation(pTs[0:keys, :], bank(6)[0:keys, :], ACT.Copy).then_inc(l_copied, 1)
                feed_gate(FILLER[g])
            turn_act(act, k + 1, mid_hi, UNIT)
            for br in range(3):
                feed(W_BRANCH + br)
            for half in range(2):
                act.wait_ge(merged_ready, 2 * l + 3 + half)
                cs4 = slice(4 * half, 4 * half + 4)
                nc.scalar.activation(act_hi[:, cs4, :], fm(0)[:, cs4, :], ACT.Copy).then_inc(mid_hi_ready, 1)
                if half == 0:
                    feed(W_BRANCH + 3)
            for n in range(4):
                if n < 2:
                    feed(W_OUT + n)
            return own

        def layer_dve(dve, l):
            own = Own(dve, l_dve_own, l * OWN_DVE)
            r, rb = l * L_TILES, l * (L_BLOCKS // 2)
            k = l * 2 + 3

            def feed(n):
                low(dve, TB + n + 2, r)

            low(dve, TB, r)
            norm_dve(dve, l + 2)
            turn_dve(dve, k, act_hi, act_lo, NGAIN, lambda: low(dve, TB + 1, r))
            def take_keys(kind, n):
                dve.wait_ge(prep_pe, n + l * 8)
                w_ = rows_of(kind)
                dve.tensor_copy(kTs[0:w_, :, :], bank(6, 2)[0:w_, :].rearrange("p (h t) -> p h t", h=4))\
                    .then_inc(prep_dve, 1)

            for i in range(W_GATE):
                if i == EARLY_A:
                    take_keys("A", 1)
                feed(i)

            def rotate(x1, x2, o1, o2, n, at):
                temps = [slot(11)[:, at + 128 * j:at + 128 * j + 32 * n].rearrange("p (t h n) -> p t h n", t=NT, h=n)
                         for j in range(4)]
                cos, sin = (prm(m).rearrange("p (t n) -> p t n", t=NT).unsqueeze(2).broadcast_to([P, NT, n, 16])
                            for m in ("mcos", "msin"))
                for o, a, b in zip(temps, (x1, x2, x1, x2), (cos, sin, sin, cos)):
                    own.done(dve.tensor_tensor(o, a, b, ALU.mult))
                own.wait()
                own.done(dve.tensor_tensor(o1, temps[0], temps[1], ALU.subtract))
                return own.done(dve.tensor_tensor(o2, temps[2], temps[3], ALU.add))

            def prepare(kind):
                if kind == "D":
                    take_keys(kind, 2)
                elif kind == "B":
                    dve.wait_ge(prep_act, 3 + l * 13)
                    own.done(dve.tensor_scalar(m_ms[:, 0:2], m_ss[:, 0:2], 1.0 / MQ, EPS, ALU.mult, ALU.add))
                    own.done(dve.tensor_scalar(m_ms[:, 2:4], m_ss[:, 2:4], 1.0 / MKV, EPS, ALU.mult, ALU.add))
                    own.wait()
                    dve.nop().then_inc(prep_dve, 1)
                    dve.wait_ge(prep_act, 4 + l * 13)
                    own.done(dve.reciprocal(m_rs, m_rt))
                    own.wait()
                    stage = slot(11)[:, 0:640].rearrange("p (t n) -> p t n", t=NT)
                    for n, (at, w_, o) in enumerate(((BCQ, MQ, 0), (BCKV, MKV, MQ))):
                        for t in range(NT):
                            own.done(dve.tensor_scalar(stage[:, t, o:o + w_], proj[:, t, at:at + w_],
                                                       m_rs[:, 2 * n + t:2 * n + t + 1], None, ALU.mult))
                    own.wait()
                    dve.nop().then_inc(prep_dve, 1)
                    feed(gate_tile(4))
                    dve.wait_ge(prep_act, 6 + l * 13)
                    q = proj[:, :, 0:384].rearrange("p t (h n) -> p t h n", h=4)
                    kk = proj[:, :, 384:768].rearrange("p t (h n) -> p t h n", h=4)
                    x1, x2 = q[:, :, :, MN:MN + 16], q[:, :, :, MN + 16:MN + 32]
                    rotate(x1, x2, x1, x2, 4, 0)
                    kp = proj[:, :, BKPE:BKPE + MR].unsqueeze(2)
                    kr = slot(11)[:, 512 + 512:512 + 576].rearrange("p (t h n) -> p t h n", t=NT, h=1)
                    rotate(kp[:, :, :, 0:16], kp[:, :, :, 16:32], kr[:, :, :, 0:16], kr[:, :, :, 16:32], 1, 512)
                    own.wait()
                    for t in range(NT):
                        own.done(dve.tensor_copy(kk[:, t, :, MN:MQK], kr[:, t, :, :].broadcast_to([P, 4, MR])))
                    own.wait()
                    dve.nop().then_inc(prep_dve, 1)
                    feed(gate_tile(5))
                    take_keys(kind, 5)
                elif kind == "cmp":
                    dve.wait_ge(prep_pe, 6 + l * 8)
                    kv = slot(11)[:, 0:SEQ]
                    own.done(dve.tensor_copy(kv, bank(4)[:, 0:SEQ]))
                    blocks_f = slot(11)[:, 1024:2048].rearrange("p (s n) -> p s n", s=CMP_BLOCK)
                    own.done(dve.memset(slot(11)[:, 1024:2048], 0.0))
                    own.done(dve.memset(hid_tm, 0.0))
                    own.wait()
                    kv = kv.rearrange("p (n s) -> p s n", s=16)
                    for v in range(2):
                        rows_v = slice(HD * v, HD * v + HD)
                        for a in range(2):
                            m = NCP - a
                            own.done(dve.tensor_tensor(blocks_f[rows_v, 16 * a:16 * a + 16, NCP * v:NCP * v + m],
                                                       kv[rows_v, :, a:a + m],
                                                       bc(lpar("pos", 16 * a, 16 * a + 16)[rows_v], [HD, 16, m]),
                                                       ALU.add))
                    own.wait()
                    dve.nop().then_inc(prep_dve, 1)
                    dve.wait_ge(prep_act, 10 + l * 13)
                    dve.tensor_tensor(blk_lo, slot(11)[:, 1024:2048], blk_hi.bitcast(f32), ALU.subtract)\
                        .then_inc(prep_dve, 1)
                    feed(gate_tile(8))
                    feed(W_CMP)
                    feed(W_CMP + 1)
                    dve.wait_ge(prep_pe, 8 + l * 8)
                    dve.tensor_tensor(vcmp, bank(7)[0:NCP, 0:HD], lpar("b2v", 0, HD)[0:NCP], ALU.add)\
                        .then_inc(prep_dve, 1)
                    feed(gate_tile(9))

            def arguments(g, kind, t):
                n = NCP if kind == "cmp" else (t + 1) * P
                p = probs[g % 2][:, :, 0:n]
                s = bank(4, 2).rearrange("p (h k) -> p h k", h=4)[:, :, 0:n]

                def rows_mask(m):
                    return mask[m][:, t, 0:n].unsqueeze(1).broadcast_to([P, 4, n])

                dve.wait_ge(l_scores, g + 1 + l * NG)
                if kind == "D":
                    dve.wait_ge(l_logs, t + 1 + l * 2)
                    own.done(dve.scalar_tensor_tensor(p, s, 0.0, p, ALU.max, ALU.add))
                    own.wait()
                    own.done(dve.tensor_tensor(p, p, rows_mask("strict"), ALU.mult))
                    own.wait()
                    for h in range(H2):
                        own.done(dve.tensor_tensor_scan(p[:, h, ::-1], mask["strict"][:, t, 0:n][:, ::-1], p[:, h, ::-1],
                                                        0.0, ALU.mult, ALU.add))
                    own.wait()
                    own.done(dve.tensor_tensor(p, s, p, ALU.subtract))
                    own.wait()
                    dve.tensor_tensor(p, p, rows_mask("strict_neg"), ALU.add).then_inc(l_shift, 1)
                    return
                if kind in ("A", "slc", "win"):
                    for h in range(H2):
                        own.done(dve.scalar_tensor_tensor(p[:, h, :], mask["dist"][:, t, 0:n],
                                                          (SLOPES_A if kind == "A" else SLOPES_C)[h], s[:, h, :],
                                                          ALU.mult, ALU.add))
                    if kind == "A":
                        own.wait()
                        own.done(dve.tensor_tensor(p, p, rows_mask("count"), ALU.add))
                elif kind == "B":
                    own.done(dve.tensor_tensor(p, s, rows_mask("causal"), ALU.add))
                else:
                    own.done(dve.tensor_tensor(p, s, c_mask[:, t, :, :], ALU.add))
                own.wait()
                if kind != "cmp":
                    dve.tensor_reduce(l_nb, p, AX.X, ALU.max, negate=True).then_inc(l_shift, 1)
                else:
                    own.done(dve.tensor_reduce(l_nb, p, AX.X, ALU.max, negate=True))
                    own.wait()
                    dve.tensor_scalar(l_nb, l_nb, 1e20, None, ALU.min).then_inc(l_shift, 1)

            def factors(g, kind, t):
                if kind == "D":
                    return None
                dve.wait_ge(l_exp, g + 1 + l * NG)
                if kind == "cmp":
                    own.done(dve.tensor_scalar(l_sum, l_sum, 1e-30, None, ALU.max))
                    own.wait()
                own.done(dve.reciprocal(l_rs, l_sum))
                own.wait()
                if kind in ("A", "B"):
                    return l_rs
                j = ("cmp", "slc", "win").index(kind)
                own.done(dve.tensor_tensor(l_co, l_rs, proj[:, t, CGT + j:CGT + 12:3], ALU.mult))
                own.wait()
                return l_co

            def output(g, kind, t, factor):
                br = {"A": 0, "B": 1, "cmp": 2, "slc": 2, "win": 2, "D": 3}[kind]
                y = y_tm[:, t, BW * br:BW * br + BW]
                y4 = y.rearrange("p (h n) -> p h n", h=4)
                gate = proj[:, t, (AG, BG, CG, DG)[br]:(AG, BG, CG, DG)[br] + BW]
                o = bank(7)[:, 0:BW]
                o4 = o.rearrange("p (h n) -> p h n", h=4)
                dve.wait_ge(l_pv, FIRST_ROUND[g + 1] + l * NR)
                if kind == "D":
                    dve.tensor_tensor(y, o, gate, ALU.mult).then_inc(l_out, 1)
                elif kind in ("A", "B"):
                    own.done(dve.tensor_tensor(y4, o4, bc(factor, [P, 4, HD]), ALU.mult))
                    own.wait()
                    dve.tensor_tensor(y, y, gate, ALU.mult).then_inc(l_out, 1)
                elif kind == "cmp":
                    dve.tensor_tensor(y4, o4, bc(factor, [P, 4, HD]), ALU.mult).then_inc(l_out, 1)
                else:
                    part = probs[g % 2][:, 0, :]
                    own.done(dve.tensor_tensor(part.rearrange("p (h n) -> p h n", h=4), o4,
                                               bc(factor, [P, 4, HD]), ALU.mult))
                    own.wait()
                    if kind == "slc":
                        dve.tensor_tensor(y, y, part, ALU.add).then_inc(l_out, 1)
                    else:
                        own.done(dve.tensor_tensor(y, y, part, ALU.add))
                        own.wait()
                        dve.tensor_tensor(y, y, gate, ALU.mult).then_inc(l_out, 1)

            def begin(g):
                if g >= 2:
                    dve.wait_ge(l_turned, FIRST_ROUND[g - 1] + l * NR)
                    dve.wait_ge(l_out, g - 1 + l * NG)
                arguments(g, *GROUPS_L[g])

            for g, (kind, t) in enumerate(GROUPS_L):
                if PREPARED[g]:
                    prepare(kind)
                    begin(g)
                factor = factors(g, kind, t)
                if g + 1 < NG and not PREPARED[g + 1]:
                    begin(g + 1)
                if g == 0 or kind == "D" and t == 0:
                    dve.wait_ge(gates_ready, (2 if g else 1) + 2 * l)
                if g >= 2:
                    dve.wait_ge(l_out, g - 1 + l * NG)
                output(g, kind, t, factor)
                feed(gate_tile(FILLER[g]))
            dve.wait_ge(l_out, NG + l * NG)
            dve.nop().then_inc(src_ready, 2)
            turn_dve(dve, k + 1, mid_hi, mid_lo, UNIT)
            for half in range(2):
                g = BB + B_BRANCH - 2 + half
                dve.wait_ge(block_free[g % 2], g // 2 + 1 + rb)
            for br in range(4):
                for half in range(2):
                    g = BB + B_BRANCH + 2 * br + half
                    gate = gates[:, 2048 * br + 1024 * half:2048 * br + 1024 * half + 1024]
                    m, part = merged_half(half)
                    if half:
                        dve.wait_ge(tile_used, TB + W_BRANCH + br + 1 + r)
                    else:
                        dve.wait_ge(branch_half, br + 1 + 4 * l)
                    if br >= 2:
                        dve.wait_ge(branch_added, 2 * (br - 2) + half + 1 + 4 * l)
                    dve.tensor_tensor(part if br else m, pair(g), gate, ALU.mult).then_inc(block_free[g % 2], 1)
                    if br == 3:
                        dve.wait_ge(block_free[g % 2], g // 2 + 1 + rb)
                        dve.tensor_tensor(m, m, part, ALU.add).then_inc(merged_ready, 1)
                if br < 3:
                    feed(W_BRANCH + br)
            for half in range(2):
                dve.wait_ge(mid_hi_ready, 2 * l + 4 + half)
                cs4 = slice(4 * half, 4 * half + 4)
                dve.tensor_tensor(act_lo[:, cs4, :], fm(0)[:, cs4, :], act_hi[:, cs4, :].bitcast(f32), ALU.subtract)\
                    .then_inc(mid_lo_ready, 1)
                if half == 0:
                    feed(W_BRANCH + 3)
            for n in range(2):
                feed(W_OUT + n)
            for half in range(2):
                g = BB + B_LOUT + half
                dve.wait_ge(tile_used, TB + W_OUT + 3 + half + r)
                xs = x_tm[:, :, 512 * half:512 * half + 512]
                dve.tensor_tensor(xs, xs, pair(g).rearrange("p (t n) -> p t n", t=NT), ALU.add)\
                    .then_inc(block_free[g % 2], 1)
            return own

        def merged_half(half):
            cols = slice(1024 * half, 1024 * half + 1024)
            return slot(0)[:, cols], slot(1)[:, cols]

        def layer_pool(pool, l):
            rb = l * (L_BLOCKS // 2)
            for br in (1, 2):
                for half in range(2):
                    g = BB + B_BRANCH + 2 * br + half
                    m, part = merged_half(half)
                    pool.wait_ge(block_free[g % 2], g // 2 + 1 + rb)
                    if br == 2:
                        pool.wait_ge(branch_added, half + 1 + 4 * l)
                    pool.tensor_tensor(m, m, part, ALU.add).then_inc(branch_added, 1)

        def layer_sp(sp, l):
            r = l * L_TILES

            def one(name):
                return w[name][bass.ds(l, 1)]

            def rows4(m, k0, c0, n=512):
                return m[:, k0:k0 + 512, c0:c0 + n].rearrange("o (k p) n -> p (o k) n", p=P), n

            for i in range(W_GATE):
                j = i // 2
                load_tile(sp, TB + i, r, rows4(one("w_in_2"), 512 * (i % 2), 512 * j, min(512, PROJ2 - 512 * j)))

            def merge(n):
                m = one("w_merge_2")[:, n // 4]
                load_tile(sp, TB + gate_tile(n), r, rows4(m, 512 * (n % 2), 512 * (n // 2 % 2)))

            for n in range(GATES_FIRST):
                merge(n)
            for half in range(2):
                src = one("nsa_w1")[:, :, SLOT * half:SLOT * half + SLOT].rearrange("o p (k n) -> p (o k) n", k=4)
                load_tile(sp, TB + W_CMP + half, r, (src, 512))
            for n in range(GATES_FIRST, 16):
                merge(n)
            for br in range(4):
                load_tile(sp, TB + W_BRANCH + br, r,
                          (one("w_branch_2")[:, br].rearrange("o (k p) n -> p (o k) n", p=P), 512))
            for n, (j, h) in enumerate(OUT_ORDER):
                load_tile(sp, TB + W_OUT + n, r, rows4(one("w_out_2"), 512 * h, 512 * j))

        gain_row = slot(4)[:, 0:D]

        def last_act(act):
            g0 = BB + (LAYERS - 1) * L_BLOCKS + B_LOUT
            squares_act(act, lambda half: block_read(act, g0 + half))
            root_act(act, LAYERS + 2)

        def last_dve(dve):
            k = LAYERS + 2
            scales_dve(dve, k)
            dve.wait_ge(gain_in, 16)
            for t in range(NT):
                dve.scalar_tensor_tensor(xn[:, t, :], x_tm[:, t, :], n_rs[:, t:t + 1], gain_row, ALU.mult, ALU.mult)\
                    .then_inc(out_ready, 1)

        def last_sp(sp):
            for t in range(NT):
                sp.wait_ge(out_ready, t + 1)
                sp.dma_start(out[0][t * P:(t + 1) * P, :], xn[:, t, :]).then_inc(stored, 16)
            sp.wait_ge(stored, 16 * NT)

        @block.sync
        def _(sp):
            sp.dma_start(x_tm[:, :, :], w["x"][0].rearrange("(t p) d -> p t d", p=P)).then_inc(x_in, 16)
            for i in range(T_MOE):
                load_tile(sp, i)
            moe_sp(sp)
            with sp.Fori(0, LAYERS) as l:
                layer_sp(sp, l)
            last_sp(sp)

        @block.gpsimd
        def _(pool):
            pool.dma_start(extra[:, 0:128], w["cmp_masks"].rearrange("p t h n -> p (t h n)")).then_inc(mask_in, 16)
            for d in range(2):
                pool.wait_ge(lru_sig, 16 * (d + 1))
                pool.wait_ge(conv_ready, 1)
                pool.tensor_tensor(i_fm, i_fm, fm(2), ALU.mult).then_inc(lru_ix, 1)
            pool.wait_ge(merged_ready, 2)
            pool.dma_start(mask_all, w["masks"].rearrange("p m t k -> p (m t k)")).then_inc(mask_in, 16)
            with pool.Fori(0, LAYERS) as l:
                for g in (BB - 2, BB - 1):
                    pool.wait_ge(block_free[g % 2], g // 2 + 1 + l * (L_BLOCKS // 2))
                flat = "o k n -> (o k) n"
                pool.dma_start(layer_par[:, :], w["layer_params"][bass.ds(l, 1)].rearrange(flat)).then_inc(layer_in, 16)
                up = w["mla_w_uq_2"][bass.ds(l, 1)]
                pool.dma_start(uq[:, 0, :], up[:, 0:P].rearrange(flat)).then_inc(layer_in, 16)
                pool.dma_start(uq[0:MQ - P, 1, :], up[:, P:MQ].rearrange(flat)).then_inc(layer_in, 16)
                pool.dma_start(ukv, w["mla_w_ukv_2"][bass.ds(l, 1)].rearrange(flat)).then_inc(layer_in, 16)
                layer_pool(pool, l)
            for g in (B_LOUT, B_LOUT + 1):
                block_read(pool, BB + (LAYERS - 1) * L_BLOCKS + g)
            pool.dma_start(gain_row, w["final_gain"]).then_inc(gain_in, 16)

        @block.tensor
        def _(pe):
            first_pe(pe)
            moe_pe(pe)
            with pe.Fori(0, LAYERS) as l:
                layer_pe(pe, l)

        @block.vector
        def _(dve):
            own = first_dve(dve)
            moe_dve(dve, own)
            dve.wait_ge(mask_in, 32)
            with dve.Fori(0, LAYERS) as l:
                own = layer_dve(dve, l)
                assert own.n == OWN_DVE, own.n
            last_dve(dve)

        @block.scalar
        def _(act):
            act.dma_start(par[:, :], w["params"]).then_inc(par_in, 16)
            for m, name in enumerate(("lru_wa", "lru_wi")):
                act.dma_start(lru_w[:, m, :, :], w[name][0].rearrange("d c i o -> i (d c) o")).then_inc(lru_w_in, 16)
            first_act(act)
            moe_act(act)
            with act.Fori(0, LAYERS) as l:
                own = layer_act(act, l)
                assert own.n == OWN_ACT, own.n
            last_act(act)


DEVICE = ["x", "w_in", "lru_wa", "lru_wi", "w_lru_o", "w_attn_o", "w_out", "w_expert_gate", "w_expert_up",
          "w_expert_down", "w_in_2", "mla_w_uq_2", "mla_w_ukv_2", "w_branch_2", "w_merge_2", "w_out_2"]


def rotary(dim):
    pos = np.arange(SEQ, dtype=np.float32)
    inv = np.float32(10000.0) ** (-np.arange(0, dim, 2, dtype=np.float32) / np.float32(dim))
    ang = (pos[:, None] * inv[None, :]).astype(np.float32)
    lay = lambda a: a.reshape(NT, P, dim // 2).transpose(1, 0, 2).reshape(P, -1).astype(np.float32)
    return lay(np.cos(ang)), lay(np.sin(ang))


def masks():
    t, k = np.arange(SEQ)[:, None], np.arange(SEQ)[None, :]
    d = t - k
    count = (d <= 128).astype(int) + ((d % 4 == 0) & (d <= 512)) + ((d % 16 == 0) & (d <= 2048))
    seen = (d >= 0) & (count > 0)
    all_masks = [
        np.where(d >= 0, -d, NEG), np.where(d >= 0, 0.0, NEG),
        np.where(seen, np.log(np.maximum(count, 1)), NEG),
        (d > 0).astype(float), np.where(d > 0, 0.0, NEG),
    ]
    m = np.stack(all_masks).astype(np.float32)
    return np.ascontiguousarray(m.reshape(5, NT, P, SEQ).transpose(2, 0, 1, 3))


def cmp_masks():
    t = np.arange(SEQ)[:, None]
    end = (np.arange(NCP) * CMP_STRIDE + CMP_BLOCK - 1)[None, :]
    d = t - end
    ok = (d >= 0) & (np.arange(NCP)[None, :] < N_CMP)
    m = np.stack([np.where(ok, -s * d, NEG) for s in SLOPES_C]).astype(np.float32)
    return np.ascontiguousarray(m.reshape(H2, NT, P, NCP).transpose(2, 1, 0, 3))


def pack(inputs):
    cols = lambda a: np.ascontiguousarray(np.asarray(a).reshape(-1, P).T)
    rows = lambda a: np.tile(np.asarray(a).reshape(1, -1), (P, 1))
    cos, sin = rotary(SUB)
    mcos, msin = rotary(MR)
    i = inputs
    parts = {
        "ident": np.eye(P, dtype=np.float32), "g1": cols(i["norm1_gain"]), "g2": cols(i["norm2_gain"]),
        "qg": rows(i["q_norm_gain"]), "kg": rows(i["k_norm_gain"]),
        "lam": rows(np.concatenate([np.asarray(i[n]).ravel() for n in ("lambda_q1", "lambda_k1", "lambda_q2",
                                                                       "lambda_k2")])),
        "subln": cols(i["attn_subln_gain"]), "conv_w": cols(i["conv_w"]), "conv_b": cols(i["conv_b"]),
        "ba": cols(i["lru_ba"]), "bi": cols(i["lru_bi"]), "lru_lam": cols(i["lru_lambda"]),
        "bg": cols(i["b_gates"]),
        "router_b": rows(np.concatenate([np.asarray(i["b_group_router"]).ravel(),
                                         np.asarray(i["b_expert_router"]).ravel()])),
        "router_w": np.concatenate([np.asarray(i["w_group_router"])[0], np.asarray(i["w_expert_router"])[0]], axis=1)
                      .reshape(NC, P, 20).transpose(1, 0, 2).reshape(P, -1),
        "cos": cos, "sin": sin, "mcos": mcos, "msin": msin,
        "first": rows(np.arange(GROUPS, 0, -1).astype(np.float32)),
    }
    return beside([parts[n] for n in PARAMS])


def beside(parts):
    return np.ascontiguousarray(np.concatenate(parts, axis=1), dtype=np.float32)


def pack_layer(i, l):
    cols = lambda a: np.ascontiguousarray(np.asarray(a).reshape(-1, P).T)
    rows = lambda a: np.tile(np.asarray(a).reshape(1, -1), (P, 1))
    mq = np.zeros((P, 2), np.float32)
    g = np.asarray(i["mla_q_norm_2"])[l]
    mq[:, 0], mq[:MQ - P, 1] = g[:P], g[P:]
    b2k = np.zeros((P, 1), np.float32)
    b2k[:HD, 0] = np.asarray(i["nsa_b2_2"])[l, 0]
    parts = {
        "ng": cols(np.asarray(i["norm_g_2"])[l]), "mqg": mq, "mkvg": cols(np.asarray(i["mla_kv_norm_2"])[l]),
        "pos": np.asarray(i["nsa_pos_2"])[l].transpose(0, 2, 1).reshape(P, CMP_BLOCK),
        "b1": cols(np.asarray(i["nsa_b1_2"])[l]),
        "w2": np.asarray(i["nsa_w2_2"])[l].transpose(1, 0, 2).reshape(P, -1), "b2k": b2k,
        "b2v": rows(np.asarray(i["nsa_b2_2"])[l, 1]), "bm": cols(np.asarray(i["b_merge_2"])[l]),
    }
    return beside([parts[n] for n in LAYER_PARAMS])


def kernel(**inputs):
    import concourse.bacc as bacc
    from concourse.bass_utils import run_bass_kernel_spmd

    nc = bacc.Bacc("TRN2", target_bir_lowering=False, num_devices=1)
    arrays = {n: np.ascontiguousarray(inputs[n]) for n in DEVICE}
    w1 = np.asarray(inputs["nsa_w1_2"]).reshape(LAYERS, 2, CMP_BLOCK, HD, CMP_HID).transpose(0, 1, 3, 2, 4)
    arrays["nsa_w1"] = np.ascontiguousarray(w1.reshape(LAYERS, P, CMP_BLOCK * CMP_HID))
    arrays["layer_params"] = np.stack([pack_layer(inputs, l) for l in range(LAYERS)])
    arrays.update(params=pack(inputs), masks=masks(), cmp_masks=cmp_masks(),
                  final_gain=np.tile(np.asarray(inputs["final_norm_g_2"]).reshape(1, -1), (P, 1)))
    w = {n: nc.dram_tensor(f"in_{n}", a.shape, mybir.dt.from_np(a.dtype), kind="ExternalInput").ap()
         for n, a in arrays.items()}
    out = nc.dram_tensor("out", (1, SEQ, D), mybir.dt.float32, kind="ExternalOutput").ap()
    two_blocks(nc, w, out)
    r = run_bass_kernel_spmd(nc, [{f"in_{n}": a for n, a in arrays.items()}], core_ids=[0])
    return r.results[0]["out"]
```
